# Optimizing a Trainium2 kernel written in Bass

```python
import jax, jax.numpy as jnp
from jax import lax
import numpy as np
import math

D_MODEL = 1024
BATCH = 1
SEQ = 512
DEPTH = 1

CHUNK = 64
BAND_CHUNKS = 9
ATTN_HEADS = 8
HEAD_DIM = 64
ATTN_WIDTH = ATTN_HEADS * HEAD_DIM
POOL_WINDOWS = (2, 4, 8, 16)
POOL_GROUPS = len(POOL_WINDOWS)
POOL_WIDTH = D_MODEL // 2
POOL_GROUP_DIM = POOL_WIDTH // POOL_GROUPS
MAX_REL_DIST = 256
N_REL = 2 * MAX_REL_DIST + 1
D_FF = 2816
CONV_WIDTH = 3
N_BRANCH = 2
IN_WIDTH = 3 * ATTN_WIDTH + POOL_WIDTH + N_BRANCH * D_MODEL
EPS = 1e-6


def rms_norm(x, g):
    xf = x.astype(jnp.float32)
    y = xf * lax.rsqrt(jnp.mean(xf * xf, axis=-1, keepdims=True) + EPS)
    return (y * g.astype(jnp.float32)).astype(x.dtype)

def chunk_band_attention(q, k, v, rel_bias):
    b, s, h, dh = q.shape
    n_chunks = s // CHUNK
    band = BAND_CHUNKS * CHUNK
    lead = (BAND_CHUNKS - 1) * CHUNK
    pad = ((0, 0), (lead, 0), (0, 0), (0, 0))
    k_pad = jnp.pad(k, pad)
    v_pad = jnp.pad(v, pad)
    dist = jnp.arange(CHUNK)[:, None] + lead - jnp.arange(band)[None, :]
    idx = jnp.clip(dist, -MAX_REL_DIST, MAX_REL_DIST) + MAX_REL_DIST
    bias = rel_bias.astype(jnp.float32)[:, idx]
    scale = HEAD_DIM ** -0.5
    key_offsets = jnp.arange(band)

    def one_chunk(c):
        start = c * CHUNK
        q_c = lax.dynamic_slice_in_dim(q, start, CHUNK, axis=1)
        k_c = lax.dynamic_slice_in_dim(k_pad, start, band, axis=1)
        v_c = lax.dynamic_slice_in_dim(v_pad, start, band, axis=1)
        sc = jnp.einsum('bqhd,bkhd->bhqk', q_c, k_c,
                        preferred_element_type=jnp.float32) * scale + bias
        valid = (start - lead + key_offsets) >= 0
        sc = jnp.where(valid[None, None, None, :], sc, -1e30)
        p = jax.nn.softmax(sc, axis=-1).astype(v.dtype)
        return jnp.einsum('bhqk,bkhd->bqhd', p, v_c)

    out = lax.map(one_chunk, jnp.arange(n_chunks))
    return jnp.moveaxis(out, 0, 1).reshape(b, s, h * dh)

def multiscale_pool(u, w_group, scale):
    b, s, c = u.shape
    uf = u.astype(jnp.float32)
    max_w = max(POOL_WINDOWS)
    cs = jnp.pad(jnp.cumsum(uf, axis=1), ((0, 0), (max_w, 0), (0, 0)))
    t = jnp.arange(s)
    outs = []
    for g, w in enumerate(POOL_WINDOWS):
        sl = slice(g * POOL_GROUP_DIM, (g + 1) * POOL_GROUP_DIM)
        win = cs[:, max_w:, sl] - cs[:, max_w - w:max_w - w + s, sl]
        cnt = jnp.minimum(t + 1, w).astype(jnp.float32)[None, :, None]
        outs.append(win / cnt - uf[:, :, sl])
    pooled = jnp.stack(outs, axis=2).astype(u.dtype)
    mixed = jnp.einsum('bsgc,gcd->bsgd', pooled, w_group).reshape(b, s, c)
    return mixed * scale

def conv_gated_ffn(x, w_up, conv_w, conv_b, w_down):
    hu = x @ w_up
    s = hu.shape[1]
    hp = jnp.pad(hu, ((0, 0), (CONV_WIDTH - 1, 0), (0, 0)))
    hc = conv_b + conv_w[CONV_WIDTH - 1] * hu
    for i in range(CONV_WIDTH - 1):
        hc = hc + conv_w[i] * hp[:, i:i + s]
    val, gate = jnp.split(hc, 2, axis=-1)
    return (jax.nn.gelu(gate, approximate=True) * val) @ w_down

def first_inputs(seed: int = 0) -> dict:
    key = jax.random.key(seed)
    ks = jax.random.split(key, 20)
    f32 = jnp.float32

    def nrm(k, shape, s):
        return jax.random.normal(k, shape, f32) * s

    return {
        "x": jax.random.normal(ks[0], (BATCH, SEQ, D_MODEL), f32),
        "norm_mix_pre": 1.0 + nrm(ks[1], (DEPTH, D_MODEL), 0.05),
        "w_in": nrm(ks[2], (DEPTH, D_MODEL, IN_WIDTH), D_MODEL ** -0.5),
        "b_gate": nrm(ks[3], (DEPTH, N_BRANCH * D_MODEL), 0.01),
        "rel_bias": nrm(ks[4], (DEPTH, ATTN_HEADS, N_REL), 0.1),
        "w_attn_out": nrm(ks[5], (DEPTH, ATTN_WIDTH, D_MODEL), ATTN_WIDTH ** -0.5),
        "w_pool_group": nrm(ks[6], (DEPTH, POOL_GROUPS, POOL_GROUP_DIM, POOL_GROUP_DIM), POOL_GROUP_DIM ** -0.5),
        "pool_scale": 1.0 + nrm(ks[7], (DEPTH, POOL_WIDTH), 0.1),
        "w_pool_out": nrm(ks[8], (DEPTH, POOL_WIDTH, D_MODEL), POOL_WIDTH ** -0.5),
        "w_o": nrm(ks[9], (DEPTH, D_MODEL, D_MODEL), D_MODEL ** -0.5),
        "norm_mix_post": 1.0 + nrm(ks[10], (DEPTH, D_MODEL), 0.05),
        "norm_ffn_pre": 1.0 + nrm(ks[11], (DEPTH, D_MODEL), 0.05),
        "w_up": nrm(ks[12], (DEPTH, D_MODEL, 2 * D_FF), D_MODEL ** -0.5),
        "conv_w": nrm(ks[13], (DEPTH, CONV_WIDTH, 2 * D_FF), CONV_WIDTH ** -0.5),
        "conv_b": nrm(ks[14], (DEPTH, 2 * D_FF), 0.01),
        "w_down": nrm(ks[15], (DEPTH, D_FF, D_MODEL), D_FF ** -0.5),
        "norm_ffn_post": 1.0 + nrm(ks[16], (DEPTH, D_MODEL), 0.05),
    }

def first_block(x, norm_mix_pre, w_in, b_gate, rel_bias, w_attn_out, w_pool_group, pool_scale,
              w_pool_out, w_o, norm_mix_post, norm_ffn_pre, w_up, conv_w, conv_b, w_down,
              norm_ffn_post):
    b, s, _ = x.shape
    splits = [ATTN_WIDTH, 2 * ATTN_WIDTH, 3 * ATTN_WIDTH, 3 * ATTN_WIDTH + POOL_WIDTH]
    for l in range(DEPTH):
        h = rms_norm(x, norm_mix_pre[l])
        proj = h @ w_in[l]
        q, k, v, u, gates = jnp.split(proj, splits, axis=-1)
        q = q.reshape(b, s, ATTN_HEADS, HEAD_DIM)
        k = k.reshape(b, s, ATTN_HEADS, HEAD_DIM)
        v = v.reshape(b, s, ATTN_HEADS, HEAD_DIM)
        y_a = chunk_band_attention(q, k, v, rel_bias[l]) @ w_attn_out[l]
        y_b = multiscale_pool(u, w_pool_group[l], pool_scale[l]) @ w_pool_out[l]
        g_a, g_b = jnp.split(jax.nn.sigmoid(gates + b_gate[l]), N_BRANCH, axis=-1)
        mix = (g_a * y_a + g_b * y_b) @ w_o[l]
        x = x + rms_norm(mix, norm_mix_post[l])
        f = conv_gated_ffn(rms_norm(x, norm_ffn_pre[l]), w_up[l], conv_w[l], conv_b[l], w_down[l])
        x = x + rms_norm(f, norm_ffn_post[l])
    return x


D_MIX = D_MODEL
GDN_HEADS = 4
GDN_DK = 128
GDN_DV = 128
GDN_CHUNK = 64
CONV_K = 4
A_LOG_MIN = 1.0
A_LOG_MAX = 8.0
DIFF_HEADS = 4
DIFF_D = 64
ROPE_THETA = 10000.0
Q_BLOCK = 128
LAMBDA_STD = 0.1
SUBLN_EPS = 1e-5

GDN_QK = GDN_HEADS * GDN_DK
GDN_V = GDN_HEADS * GDN_DV
DIFF_QK = DIFF_HEADS * 2 * DIFF_D
DIFF_V = DIFF_HEADS * 2 * DIFF_D
SPLIT_SIZES = (GDN_QK, GDN_QK, GDN_V, GDN_V, GDN_HEADS, GDN_HEADS,
               DIFF_QK, DIFF_QK, DIFF_V, DIFF_V)
D_IN_PROJ = sum(SPLIT_SIZES)
CONV_CH = 2 * GDN_QK + GDN_V


def rms_norm_2(x, w, eps=EPS):
    x = x.astype(jnp.float32)
    return x * lax.rsqrt(jnp.mean(x * x, axis=-1, keepdims=True) + eps) * w.astype(jnp.float32)

def l2_norm(x, eps=EPS):
    return x * lax.rsqrt(jnp.sum(x * x, axis=-1, keepdims=True) + eps)

def rope_tables(seq, dim):
    inv_freq = ROPE_THETA ** (-jnp.arange(0, dim, 2, dtype=jnp.float32) / dim)
    ang = jnp.arange(seq, dtype=jnp.float32)[:, None] * inv_freq[None, :]
    return jnp.cos(ang), jnp.sin(ang)

def apply_rope(x, cos, sin):
    c = cos[None, :, None, None, :]
    s = sin[None, :, None, None, :]
    x1, x2 = jnp.split(x, 2, axis=-1)
    return jnp.concatenate([x1 * c - x2 * s, x2 * c + x1 * s], axis=-1)

def causal_depthwise_conv(x, w):
    c = x.shape[-1]
    return lax.conv_general_dilated(
        x, w[:, None, :], window_strides=(1,), padding=[(CONV_K - 1, 0)],
        dimension_numbers=("NWC", "WIO", "NWC"), feature_group_count=c)

def gated_delta_rule_chunked(q, k, v, g, beta):
    b, h, s, dk = q.shape
    dv = v.shape[-1]
    c = GDN_CHUNK
    n = s // c
    q = q.reshape(b, h, n, c, dk)
    k = k.reshape(b, h, n, c, dk)
    v = v.reshape(b, h, n, c, dv)
    beta = beta.reshape(b, h, n, c)
    g = jnp.cumsum(g.reshape(b, h, n, c), axis=-1)
    tril = jnp.tril(jnp.ones((c, c), dtype=bool))
    strict = jnp.tril(jnp.ones((c, c), dtype=bool), -1)
    decay = jnp.exp(jnp.where(tril, g[..., :, None] - g[..., None, :], -jnp.inf))
    k_beta = k * beta[..., None]
    v_beta = v * beta[..., None]
    lower = jnp.where(strict, jnp.einsum("bhncd,bhnmd->bhncm", k_beta, k) * decay, 0.0)
    a_mat = lower + jnp.eye(c, dtype=q.dtype)
    rhs = jnp.concatenate([v_beta, k_beta * jnp.exp(g)[..., None]], axis=-1)
    sol = lax.linalg.triangular_solve(a_mat, rhs, left_side=True, lower=True, unit_diagonal=True)
    u, w = sol[..., :dv], sol[..., dv:]
    qk_intra = jnp.where(tril, jnp.einsum("bhncd,bhnmd->bhncm", q, k) * decay, 0.0)

    def step(state, inp):
        q_c, k_c, u_c, w_c, g_c, a_c = inp
        v_new = u_c - jnp.einsum("bhcd,bhde->bhce", w_c, state)
        o = (jnp.einsum("bhcd,bhde->bhce", q_c * jnp.exp(g_c)[..., None], state)
             + jnp.einsum("bhcm,bhme->bhce", a_c, v_new))
        g_last = g_c[..., -1]
        k_dec = k_c * jnp.exp(g_last[..., None] - g_c)[..., None]
        state = state * jnp.exp(g_last)[..., None, None] + jnp.einsum("bhcd,bhce->bhde", k_dec, v_new)
        return state, o

    xs = tuple(jnp.moveaxis(t, 2, 0) for t in (q, k, u, w, g, qk_intra))
    state0 = jnp.zeros((b, h, dk, dv), dtype=q.dtype)
    _, o = lax.scan(step, state0, xs)
    return jnp.moveaxis(o, 0, 2).reshape(b, h, s, dv)

def diff_attention(q, k, v, lam):
    b, s, h, _, d = q.shape
    nblk = s // Q_BLOCK
    scale = 1.0 / math.sqrt(d)
    qb = jnp.moveaxis(q.reshape(b, nblk, Q_BLOCK, h, 2, d), 1, 0)
    key_pos = jnp.arange(s)

    def one_block(args):
        i, q_i = args
        sc = jnp.einsum("bqhcd,bkhcd->bhcqk", q_i, k) * scale
        q_pos = i * Q_BLOCK + jnp.arange(Q_BLOCK)
        mask = key_pos[None, :] <= q_pos[:, None]
        p = jax.nn.softmax(jnp.where(mask, sc, -jnp.inf), axis=-1)
        p = p[:, :, 0] - lam * p[:, :, 1]
        return jnp.einsum("bhqk,bkhe->bqhe", p, v)

    o = lax.map(one_block, (jnp.arange(nblk), qb))
    return jnp.moveaxis(o, 0, 1).reshape(b, s, h, 2 * d)

def hybrid_mixer(layer_idx, x, cos, sin, w_norm, w_in, conv_w, a_log, dt_bias, gdn_norm_w,
                 q_norm_w, k_norm_w, lambda_q1, lambda_k1, lambda_q2, lambda_k2, subln_w, w_out):
    b, s, _ = x.shape
    f32 = jnp.float32
    hn = rms_norm_2(x, w_norm)
    proj = jnp.einsum("bsd,de->bse", hn, w_in.astype(f32))
    idx = [int(t) for t in np.cumsum(SPLIT_SIZES)[:-1]]
    q_a, k_a, v_a, z_a, b_a, a_a, q_b, k_b, v_b, z_b = jnp.split(proj, idx, axis=-1)

    qkv = jax.nn.silu(causal_depthwise_conv(jnp.concatenate([q_a, k_a, v_a], -1), conv_w.astype(f32)))
    q_a, k_a, v_a = jnp.split(qkv, [GDN_QK, 2 * GDN_QK], axis=-1)
    to_heads = lambda t, dh: jnp.transpose(t.reshape(b, s, GDN_HEADS, dh), (0, 2, 1, 3))
    q_a = l2_norm(to_heads(q_a, GDN_DK)) * (GDN_DK ** -0.5)
    k_a = l2_norm(to_heads(k_a, GDN_DK))
    v_a = to_heads(v_a, GDN_DV)
    beta = jnp.transpose(jax.nn.sigmoid(b_a), (0, 2, 1))
    g = -jnp.exp(a_log.astype(f32)) * jax.nn.softplus(a_a + dt_bias.astype(f32))
    g = jnp.transpose(g, (0, 2, 1))
    o_a = gated_delta_rule_chunked(q_a, k_a, v_a, g, beta)
    o_a = jnp.transpose(o_a, (0, 2, 1, 3))
    o_a = rms_norm_2(o_a, gdn_norm_w) * jax.nn.silu(z_a.reshape(b, s, GDN_HEADS, GDN_DV))
    o_a = o_a.reshape(b, s, GDN_V)

    q_b = apply_rope(rms_norm_2(q_b.reshape(b, s, DIFF_HEADS, 2, DIFF_D), q_norm_w), cos, sin)
    k_b = apply_rope(rms_norm_2(k_b.reshape(b, s, DIFF_HEADS, 2, DIFF_D), k_norm_w), cos, sin)
    v_b = v_b.reshape(b, s, DIFF_HEADS, 2 * DIFF_D)
    lam_init = 0.8 - 0.6 * math.exp(-0.3 * layer_idx)
    lam = (jnp.exp(jnp.sum(lambda_q1.astype(f32) * lambda_k1.astype(f32)))
           - jnp.exp(jnp.sum(lambda_q2.astype(f32) * lambda_k2.astype(f32))) + lam_init)
    o_b = diff_attention(q_b, k_b, v_b, lam)
    o_b = rms_norm_2(o_b, subln_w, SUBLN_EPS) * (1.0 - lam_init)
    o_b = (o_b * jax.nn.silu(z_b.reshape(b, s, DIFF_HEADS, 2 * DIFF_D))).reshape(b, s, DIFF_V)

    o = jnp.concatenate([o_a, o_b], axis=-1).astype(x.dtype)
    return jnp.einsum("bse,ed->bsd", o, w_out)

def second_inputs(seed: int = 0) -> dict:
    key = jax.random.key(seed)
    ks = jax.random.split(key, 16)
    nrm = lambda k, shape, std: jax.random.normal(k, shape, jnp.float32) * std
    return {
        "x": jax.random.normal(ks[0], (BATCH, SEQ, D_MODEL), jnp.float32),
        "w_norm": 1.0 + nrm(ks[1], (DEPTH, D_MODEL), 0.02),
        "w_in": nrm(ks[2], (DEPTH, D_MODEL, D_IN_PROJ), D_MODEL ** -0.5),
        "conv_w": nrm(ks[3], (DEPTH, CONV_K, CONV_CH), CONV_K ** -0.5),
        "a_log": jnp.log(jax.random.uniform(ks[4], (DEPTH, GDN_HEADS), jnp.float32, A_LOG_MIN, A_LOG_MAX)),
        "dt_bias": nrm(ks[5], (DEPTH, GDN_HEADS), 0.1),
        "gdn_norm_w": 1.0 + nrm(ks[6], (DEPTH, GDN_DV), 0.02),
        "q_norm_w": 1.0 + nrm(ks[7], (DEPTH, DIFF_D), 0.02),
        "k_norm_w": 1.0 + nrm(ks[8], (DEPTH, DIFF_D), 0.02),
        "lambda_q1": nrm(ks[9], (DEPTH, DIFF_D), LAMBDA_STD),
        "lambda_k1": nrm(ks[10], (DEPTH, DIFF_D), LAMBDA_STD),
        "lambda_q2": nrm(ks[11], (DEPTH, DIFF_D), LAMBDA_STD),
        "lambda_k2": nrm(ks[12], (DEPTH, DIFF_D), LAMBDA_STD),
        "subln_w": 1.0 + nrm(ks[13], (DEPTH, 2 * DIFF_D), 0.02),
        "w_out": nrm(ks[14], (DEPTH, D_MIX, D_MODEL), D_MIX ** -0.5),
    }

def second_block(x, w_norm, w_in, conv_w, a_log, dt_bias, gdn_norm_w, q_norm_w, k_norm_w,
              lambda_q1, lambda_k1, lambda_q2, lambda_k2, subln_w, w_out):
    cos, sin = rope_tables(x.shape[1], DIFF_D)
    for l in range(DEPTH):
        x = x + hybrid_mixer(l, x, cos, sin, w_norm[l], w_in[l], conv_w[l], a_log[l], dt_bias[l],
                             gdn_norm_w[l], q_norm_w[l], k_norm_w[l], lambda_q1[l], lambda_k1[l],
                             lambda_q2[l], lambda_k2[l], subln_w[l], w_out[l])
    return x


def setup_inputs(seed=0):
    out = dict(first_inputs(seed))
    for name, value in second_inputs(seed + 1).items():
        if name != "x":
            out[name + "_2"] = value
    return out


def reference(
    x, norm_mix_pre, w_in, b_gate, rel_bias, w_attn_out, w_pool_group, pool_scale, w_pool_out,
    w_o, norm_mix_post, norm_ffn_pre, w_up, conv_w, conv_b, w_down, norm_ffn_post, w_norm_2,
    w_in_2, conv_w_2, a_log_2, dt_bias_2, gdn_norm_w_2, q_norm_w_2, k_norm_w_2, lambda_q1_2,
    lambda_k1_2, lambda_q2_2, lambda_k2_2, subln_w_2, w_out_2,
):
    x = first_block(
        x, norm_mix_pre, w_in, b_gate, rel_bias, w_attn_out, w_pool_group, pool_scale,
        w_pool_out, w_o, norm_mix_post, norm_ffn_pre, w_up, conv_w, conv_b, w_down,
        norm_ffn_post,
    )
    return second_block(
        x, w_norm_2, w_in_2, conv_w_2, a_log_2, dt_bias_2, gdn_norm_w_2, q_norm_w_2, k_norm_w_2,
        lambda_q1_2, lambda_k1_2, lambda_q2_2, lambda_k2_2, subln_w_2, w_out_2,
    )


_drawn_inputs = setup_inputs


def setup_inputs(seed=0):
    import zlib

    import numpy as np

    out = dict(_drawn_inputs(seed))
    spreads = {}
    factors = {'b_gate': 8.0,
     'rel_bias': 4.597,
     'conv_b': 5.731,
     'w_norm_2': 5.555,
     'dt_bias_2': 8.0,
     'gdn_norm_w_2': 8.0,
     'q_norm_w_2': 8.0,
     'k_norm_w_2': 8.0,
     'lambda_q1_2': 6.196,
     'lambda_k1_2': 8.0,
     'subln_w_2': 8.0}
    for name, (base, spread) in spreads.items():
        noise = np.random.default_rng([zlib.crc32(name.encode()), seed]).standard_normal(out[name].shape)
        drawn = base * np.exp(spread * noise) if base else spread * noise
        out[name] = __import__('jax').numpy.asarray(drawn.astype(out[name].dtype))
    for name, factor in factors.items():
        out[name] = (out[name] * factor).astype(out[name].dtype)
    return out
```

```python
from contextlib import ExitStack

import concourse.bass as bass
from concourse import mybir

F32 = mybir.dt.float32
F32R = mybir.dt.float32r
ACT = mybir.ActivationFunctionType
ALU = mybir.AluOpType
AXX = mybir.AxisListType.X

P = 128
S = 512
D = 1024
KT = D // P
NT = S // P
HEADS, HD = 8, 64
PAIRS = HEADS // 2
CH = 64
GH = 4
DFF = 2816
FT = DFF // P
EPS, SUB_EPS = 1e-6, 1e-5
WINDOWS = (2, 4, 8, 16)
LEAD = 16
LAM_INIT = 0.8 - 0.6
NEG = -1e30

N_P1, N_MIX, N_WO, N_UP, N_DOWN, N_P2, N_OUT = 32, 8, 8, 2 * FT, 3 * 8, 32, 8
N_UNITS = N_P1 + N_MIX + N_WO + N_UP + N_DOWN + N_P2 + N_OUT
RING = 4
BODY = 8

C_MIXPRE, C_MIXPOST, C_FFNPRE, C_FFNPOST, C_NORM2 = 0, 8, 16, 24, 32
C_BGATE = 40
C_PSCALE = 56
C_CONV = 60
C_CONV2 = C_CONV + 4 * 2 * FT
C_GNORM = C_CONV2 + 4 * 12
C_QNORM, C_KNORM, C_SUBLN = C_GNORM + 1, C_GNORM + 2, C_GNORM + 3
N_COLS = C_GNORM + 4

(K_ID, K_UPPER, K_SAME, K_SWAP, K_NEG_T, K_STRICT_T, K_LEVEL) = range(7)
N_LEVELS = 6
N_MATS = K_LEVEL + 1 + N_LEVELS
R_ALOG, R_DT, R_LAM = 0, GH, 2 * GH
N_ROWS = R_LAM + 4 * HD


class Tally:

    def __init__(self, name, sem, step=1, start=0):
        self.name, self.sem, self.step, self.n, self.per = name, sem, step, start, 0

    scope = 0

    def inc(self, ins):
        ins.then_inc(self.sem, self.step)
        self.n += self.step
        return self.now()

    def now(self):
        return self.at(self.n)

    def at(self, n):
        return (self, n, Tally.scope)


class Queue:

    def __init__(self, core, engine, sem):
        self.core, self.e, self.tally, self.seen = core, engine, sem, {}

    def on(self, *marks):
        for mark in marks:
            if mark is None:
                continue
            tally, n, scope = mark
            assert scope in (0, Tally.scope), "a mark of a loop that has ended"
            if self.seen.get((id(tally), scope), -1) >= n:
                continue
            self.seen[(id(tally), scope)] = n
            if scope:
                self.e.wait_ge(tally.sem, self.core.turn * tally.per + n)
            else:
                self.e.wait_ge(tally.sem, n)
        return self.e

    def on_apart(self, *marks):
        self.on(*marks)
        self.e.sem_inc(self.core.spare, 1)
        return self.e

    def mark(self, ins):
        return self.tally.inc(ins)

    def now(self):
        return self.tally.now()


class Core:
    def __init__(self, nc, ctx):
        self.nc, self.ctx, self.turn, self.loops, self.queues = nc, ctx, None, 0, []
        self.spare = ctx.enter_context(nc.semaphore("spare"))

    def queue(self, engine, name):
        q = Queue(self, engine, self.tally(name))
        self.queues.append(q)
        return q

    def tally(self, name, step=1, start=0):
        return Tally(name, self.ctx.enter_context(self.nc.semaphore(name)), step, start)

    def loop(self, turns, per, body, engines):
        begin = {t: t.n for t in per}
        for q in self.queues:
            q.seen = {}
        self.loops += 1
        with self.nc.Fori(0, turns, engines=engines) as i:
            self.turn, Tally.scope = i, self.loops
            for t, n in per.items():
                t.per = n
            body(i)
        self.turn, Tally.scope = None, 0
        bad = [(t.name, t.n - begin[t], n) for t, n in per.items() if t.n - begin[t] != n]
        assert not bad, bad
        for q in self.queues:
            q.seen = {}
        for t, n in per.items():
            t.n = begin[t] + turns * n


PER2 = (97, 38, 74, 17)


def build(nc, x_in, w_units, w_ba, cols_in, mats_in, rope_in, rows_in, relb_in, edge_in,
          wgrp_in, out, debug=None):
    ctx = ExitStack()
    with ctx:
        core = Core(nc, ctx)
        V = core.queue(nc.vector, "vector_done")
        A = core.queue(nc.scalar, "scalar_done")
        T = core.queue(nc.tensor, "tensor_done")
        G = core.queue(nc.gpsimd, "gpsimd_done")
        COMPUTE = [mybir.EngineType.PE, mybir.EngineType.Activation, mybir.EngineType.DVE,
                   mybir.EngineType.Pool]

        def sb(stack, name, shape, dt=F32):
            return stack.enter_context(nc.sbuf_tensor(name, shape, dt))

        X = sb(ctx, "X", [P, KT, S])
        h_place = nc.sbuf_base
        Hh = sb(ctx, "Hh", [P, KT, S], F32R)
        Hl = sb(ctx, "Hl", [P, KT, S], F32R)
        raw = sb(ctx, "raw", [P, RING, D])
        Wh = sb(ctx, "Wh", [P, RING, D], F32R)
        Wl = sb(ctx, "Wl", [P, RING, D], F32R)
        cols = sb(ctx, "cols", [P, N_COLS])
        ident = sb(ctx, "ident", [P, P])
        ones = sb(ctx, "ones", [P, 1])
        half = sb(ctx, "half", [P, 4 * NT])
        ssum = sb(ctx, "ssum", [P, S])
        sq = sb(ctx, "sq", [P, 2, S])
        rstd = sb(ctx, "rstd", [P, NT])
        tmp = sb(ctx, "tmp", [P, 2, S])
        PS = ctx.enter_context(nc.psum_tensor("PS", [P, 8, S], F32))

        landed = [core.tally(f"unit_landed{s}", 16) for s in range(RING)]
        rounded = core.tally("unit_rounded")
        split = core.tally("unit_split", start=RING)
        used = core.tally("unit_used", start=RING)
        bank_free = [core.tally(f"bank{b}_free", start=1) for b in range(2)]
        nc.vector.sem_inc(split.sem, RING)
        nc.tensor.sem_inc(used.sem, RING)
        for t in bank_free:
            nc.vector.sem_inc(t.sem, 1)
        loaded_small = core.tally("small_loaded", 16)

        for dst, src in ((cols, cols_in), (ident, mats_in[:, 0, :])):
            loaded_small.inc(nc.scalar.dma_start(dst[:], src))
        loaded_x = [core.tally(f"x_loaded{n}", 16) for n in range(2)]
        for n in range(2):
            loaded_x[n].inc(nc.scalar.dma_start(X[:, 4 * n:4 * n + 4, :], x_in[:, 4 * n:4 * n + 4, :]))

        n_units = N_UNITS - 36 if debug else N_UNITS
        with nc.sync.Fori(0, n_units // RING) as i:
            for s in range(RING):
                nc.sync.wait_ge(split.sem, i * RING + (s + 1))
                nc.sync.dma_start(raw[:, s, :], w_units[bass.ds(i * RING + s, 1)]
                                  .rearrange("a p n -> (a p) n")).then_inc(landed[s].sem, 16)

        class Dense:
            unit = 0
            ahead = 0
            group = 0

        def split_unit():
            n = Dense.ahead
            Dense.ahead += 1
            s = n % RING
            rounded.inc(A.on(landed[s].at(16 * (n // RING + 1)), used.at(n + 1))
                        .activation(Wh[:, s, :], raw[:, s, :], ACT.Copy))
            split.inc(V.on(rounded.at(n + 1)).tensor_tensor(
                Wl[:, s, :], raw[:, s, :], Wh[:, s, :].bitcast(F32), ALU.subtract))
            landed[s].n = 16 * (n // RING + 1)

        def products(bank, rhs_h, rhs_l, ks, ready, first=True, last=True, fresh=True):
            n = Dense.unit
            s = n % RING
            for j, (k, r) in enumerate(ks):
                T.on(split.at(n + 1 + RING), *(ready(r) if ready else ()))
                wsl = slice(k * P, (k + 1) * P)
                for m, (a, b) in enumerate(((Wh, rhs_h), (Wh, rhs_l), (Wl, rhs_h))):
                    ins = nc.tensor.matmul(bank, a[:, s, wsl], b(r), start=first and j == 0 and m == 0,
                                           stop=last and j == len(ks) - 1 and m == 2)
                yield ins

        def unit(evac, rhs=None, ready=None, nk=KT, group=(True, True), k0=0, second=None):
            b = Dense.group % 2
            if rhs is None:
                rhs = (lambda k: Hh[:, k, :], lambda k: Hl[:, k, :])
            if Dense.ahead < total_ahead[0]:
                split_unit()
            if group[0]:
                T.on(bank_free[b].at(Dense.group // 2 + 1))
            bank = PS[:, b, :]
            ins = None
            if second is None:
                for ins in products(bank, *rhs, [(k, k0 + k) for k in range(nk)], ready,
                                    first=group[0], last=group[1]):
                    yield
            else:
                for ins in products(bank, *rhs, [(k, k) for k in range(4)], ready):
                    yield
                for ins in products(second[0], *second[1], [(k, k - 4) for k in range(4, 8)], ready):
                    yield
            done = used.inc(ins)
            Dense.unit += 1
            if group[1]:
                Dense.group += 1
                evac(bank, done, bank_free[b])
            yield

        def run(gen):
            for _ in gen:
                pass

        total_ahead = [n_units]

        def inverse_rms(ready, bank=2, scale=1.0 / D, eps=EPS):
            for t in range(NT):
                ins = T.on(ready).matmul(PS[:, bank + 1, t:t + 1], ssum[:, t * P:(t + 1) * P],
                                         ones[:], start=True, stop=True)
            m = T.mark(ins)
            m = V.mark(V.on(m).tensor_scalar(rstd[:], PS[:, bank + 1, 0:NT], scale, eps,
                                             ALU.mult, ALU.add))
            m = G.mark(G.on(m).tensor_tensor(rstd[:], rstd[:], half[:, 0:NT], ALU.pow))
            for t in range(NT):
                ins = T.on(m).matmul(PS[:, bank, t * P:(t + 1) * P],
                                     rstd[:, t:t + 1].to_broadcast([P, P]), ident[:],
                                     start=True, stop=True)
            return T.mark(ins)

        def squares(k, src, ready):
            if k == 0:
                squares.m = A.mark(A.on(ready, squares.m).activation(ssum[:], src, ACT.Square))
                return squares.m
            a = A.mark(A.on_apart(ready, squares.free[k % 2]).activation(sq[:, k % 2, :], src, ACT.Square))
            squares.m = V.mark(V.on(a, squares.m).tensor_tensor(ssum[:], ssum[:], sq[:, k % 2, :],
                                                                ALU.add))
            squares.free[k % 2] = squares.m
            return squares.m
        squares.m = None
        squares.free = [None, None]

        def normed_input(col, ready_r, x_ready):
            marks, free = [], [None, None]
            for k in range(KT):
                c = col + k
                m = V.mark(V.on(ready_r, x_ready, free[k % 2]).scalar_tensor_tensor(
                    out=tmp[:, k % 2, :], in0=X[:, k, :], scalar=cols[:, c:c + 1],
                    in1=PS[:, 2, :], op0=ALU.mult, op1=ALU.mult))
                a = A.mark(A.on(m).activation(Hh[:, k, :], tmp[:, k % 2, :], ACT.Copy))
                free[k % 2] = V.mark(V.on(a).tensor_tensor(
                    Hl[:, k, :], tmp[:, k % 2, :], Hh[:, k, :].bitcast(F32), ALU.subtract))
                marks.append(free[k % 2])
            return marks

        def add_normed(M, col, ready_r):
            prev = [None, None]
            for k in range(KT):
                c = col + k
                m = V.mark(V.on(ready_r, prev[k % 2]).scalar_tensor_tensor(
                    out=M[:, k, :], in0=M[:, k, :], scalar=cols[:, c:c + 1], in1=PS[:, 2, :],
                    op0=ALU.mult, op1=ALU.mult))
                m = V.mark(V.on(m).tensor_tensor(X[:, k, :], X[:, k, :], M[:, k, :], ALU.add))
                m = squares(k, X[:, k, :], m)
            return m

        m_small = loaded_small.now()
        m0 = V.mark(nc.vector.memset(ones[:], 1.0))
        m0 = V.mark(nc.vector.memset(half[:], -0.5))
        run_marks = None
        for n in range(2):
            split_unit()
        for k in range(KT):
            m = squares(k, X[:, k, :], loaded_x[k // 4].now())
        T.on(m0, m_small)
        V.on(m_small)
        G.on(m0)
        m = inverse_rms(m)
        h_ready = normed_input(C_MIXPRE, m, None)

        def attend(a, qt, b, Q, K, scale, bias, ready, bufs, banks):
            nk = (qt + 1) * P
            r0 = HD * a
            SBs, Ps, nmax, rsum, rinv, free = bufs
            s_ps = PS[:, banks["S"][b % 2], 0:nk]
            m_s = T.mark(T.on(*ready, free["S"][b % 2]).matmul(
                s_ps, Q[r0:r0 + HD, qt * P:(qt + 1) * P], K[r0:r0 + HD, 0:nk],
                start=True, stop=True))
            m_b = V.mark(V.on(m_s, free["SB"][b % 2]).scalar_tensor_tensor(
                out=SBs[:, b % 2, 0:nk], in0=s_ps, scalar=scale, in1=bias, op0=ALU.mult, op1=ALU.add))
            free["S"][b % 2] = m_b
            m_x = V.mark(V.on(m_b).tensor_reduce(nmax[:, b:b + 1], SBs[:, b % 2, 0:nk], AXX, ALU.max,
                                                 negate=True))
            m_p = A.mark(A.on(m_x, free["P"][b % 2]).activation(
                Ps[:, b % 2, 0:nk], SBs[:, b % 2, 0:nk], ACT.Exp, bias=nmax[:, b:b + 1], scale=1.0,
                accum_out=rsum[:, b:b + 1]))
            free["SB"][b % 2] = m_p
            m_r = V.mark(V.on(m_p).reciprocal(rinv[:, b:b + 1], rsum[:, b:b + 1]))
            return m_p, m_r

        def turn_weights(qt, j, src, m_src, PTs, free, banks):
            nk = (qt + 1) * P
            bank = banks["PT"][j % 2]
            for kt in range(qt + 1):
                ins = T.on(m_src, free["PT"][j % 2]).transpose(
                    PS[:, bank, kt * P:(kt + 1) * P], src[:, kt * P:(kt + 1) * P], ident[:])
            m_read = T.mark(ins)
            m_t = A.mark(A.on(m_read, free["PTs"][j % 2]).activation(
                PTs[:, j % 2, 0:nk], PS[:, bank, 0:nk], ACT.Copy))
            free["PT"][j % 2] = m_t
            return m_read, m_t

        def apply_weights(qt, j, m_t, PTs, values, width, free, banks):
            for kt in range(qt + 1):
                ins = T.on(m_t, free["O"][j % 2]).matmul(
                    PS[:, banks["O"][j % 2], 0:width], PTs[:, j % 2, kt * P:(kt + 1) * P],
                    values(kt), start=(kt == 0), stop=(kt == qt))
            m = T.mark(ins)
            free["PTs"][j % 2] = m
            return m

        class Fill:
            gens = []

        def fill(steps):
            while steps > 0 and Fill.gens:
                try:
                    next(Fill.gens[0])
                    steps -= 1
                except StopIteration:
                    Fill.gens.pop(0)

        def fill_all():
            fill(1 << 30)

        b1 = ctx.enter_context(ExitStack())
        gates = sb(b1, "gates", [P, 16, S])
        U = sb(b1, "U", [P, 4, LEAD + S])
        AOh = sb(b1, "AOh", [P, 4, S], F32R)
        AOl = sb(b1, "AOl", [P, 4, S], F32R)
        att = ExitStack()
        relb = sb(att, "relb", [P, HEADS, S])
        Q2 = sb(att, "Q2", [P, S])
        K2 = sb(att, "K2", [P, S])
        V2 = sb(att, "V2", [P, S])
        Vt = sb(att, "Vt", [P, NT, P])
        SBs = sb(att, "SBs", [P, 2, S])
        Ps = sb(att, "Ps", [P, 2, S])
        PTs = sb(att, "PTs", [P, 2, S])
        Ot = sb(att, "Ot", [P, NT, P])
        nmax = sb(att, "nmax", [P, 8])
        rsum = sb(att, "rsum", [P, 8])
        rinv = sb(att, "rinv", [P, 8])

        rel_loaded = core.tally("rel_loaded", 16)
        rel_loaded.inc(nc.gpsimd.dma_start(relb[:], relb_in))
        m_relb = G.mark(G.on(rel_loaded.now()).memset(relb[0:CH, :, S - CH:S], NEG))
        m_u0 = G.mark(nc.gpsimd.memset(U[:, :, 0:LEAD], 0.0))

        def pair_body(i):
            start = [V.now(), A.now(), T.now(), G.now()]
            got = {}

            def to(name, dst):
                def evac(bank, done, freed):
                    freed.inc(A.on(done, *start).activation(dst, bank, ACT.Copy))
                    got[name] = freed.now()
                return evac

            def gate(col, dst):
                def evac(bank, done, freed):
                    freed.inc(A.on(done).activation(dst, bank, ACT.Identity,
                                                    bias=cols[:, bass.ds(col, 1)], scale=1.0))
                return evac

            def flat(tile, idx):
                return tile[:, bass.ds(idx, 1), :].rearrange("p a n -> p (a n)")

            hr = (lambda r: (h_ready[r],))
            run(unit(to("q", Q2[:]), ready=hr))
            run(unit(to("k", K2[:]), ready=hr))
            run(unit(to("v", V2[:]), ready=hr))
            Fill.gens = [unit(to("u", U[:, bass.ds(i, 1), LEAD:].rearrange("p a n -> p (a n)")))]
            Fill.gens += [unit(gate(C_BGATE + 2 * i + j, flat(gates, 2 * i + j))) for j in range(2)]
            Fill.gens += [unit(gate(C_BGATE + 8 + 2 * i + j, flat(gates, 8 + 2 * i + j)))
                          for j in range(2)]
            fill(4)
            for t in range(NT):
                ins = T.on(got["v"], *start).transpose(PS[:, 4, t * P:(t + 1) * P],
                                                       V2[:, t * P:(t + 1) * P], ident[:])
            m = T.mark(ins)
            m_v = V.mark(V.on(m).tensor_copy(Vt[:].rearrange("p t n -> p (t n)"), PS[:, 4, :]))
            free = {"S": [None] * 2, "SB": [None] * 2, "P": [None] * 2, "PT": [m_v, None],
                    "PTs": [None] * 2, "O": [None] * 2}
            banks = {"S": (2, 3), "PT": (4, 5), "O": (6, 7)}
            bufs = (SBs, Ps, nmax, rsum, rinv, free)
            blocks = [(a, qt) for a in range(2) for qt in (3, 2, 1, 0)]

            def turned(a, qt, b, m_p, m_r):
                free["P"][b % 2], m_t = turn_weights(qt, b, Ps[:, b % 2, :], m_p, PTs, free, banks)
                return (a, qt, b, m_t, m_r)

            def applied(a, qt, b, m_t, m_r):
                m = apply_weights(qt, b, m_t, PTs, lambda kt: Vt[:, kt, HD * a:HD * a + HD], HD,
                                  free, banks)
                free["O"][b % 2] = V.mark(V.on(m, m_r).tensor_scalar(
                    Ot[:, qt, HD * a:HD * a + HD], PS[:, 6 + b % 2, 0:HD], rinv[:, b:b + 1], None,
                    ALU.mult))
                return free["O"][b % 2]

            to_turn = to_apply = None
            for b in range(len(blocks) + 2):
                scored = got_turned = None
                if b < len(blocks):
                    a, qt = blocks[b]
                    off = i * (2 * S) + (a * S + (NT - 1 - qt) * P)
                    bias = relb[:].rearrange("p h n -> p (h n)")[:, bass.ds(off, (qt + 1) * P)]
                    scored = (a, qt, b, *attend(a, qt, b, Q2, K2, HD ** -0.5, bias,
                                                (got["q"], got["k"]), bufs, banks))
                fill(3)
                if to_turn:
                    got_turned = turned(*to_turn)
                fill(1)
                if to_apply:
                    m_o = applied(*to_apply)
                to_turn, to_apply = scored, got_turned
            m = None
            fill(3)
            for t in range(NT):
                ins = T.on(m_o, free["PT"][0]).transpose(PS[:, 4, t * P:(t + 1) * P], Ot[:, t, :],
                                                         ident[:])
            m = T.mark(ins)
            ah = flat(AOh, i)
            m = A.mark(A.on(m).activation(ah, PS[:, 4, :], ACT.Copy))
            V.mark(V.on(m).tensor_tensor(flat(AOl, i), PS[:, 4, :], ah.bitcast(F32), ALU.subtract))
            fill_all()

        def dense_loop(turns, units, groups, own, body):
            per = {q.tally: n for q, n in zip((V, A, T, G), own) if n}
            per.update({t: 16 * units // RING for t in landed})
            per.update({rounded: units, split: units, used: units})
            per.update({t: groups // 2 for t in bank_free})
            core.loop(turns, per, body, COMPUTE)
            Dense.unit += (turns - 1) * units
            Dense.ahead += (turns - 1) * units
            Dense.group += (turns - 1) * groups

        V.on(m_relb, m0)
        A.on(m_u0)
        T.on(m_small)
        dense_loop(PAIRS, BODY, BODY, (34, 17, 26, 0), pair_body)
        att.close()

        pool = ExitStack()
        W = LEAD + S
        sums = sb(pool, "sums", [P, 2, W])
        pooled = sb(pool, "pooled", [P, 4, S])
        wgrp = sb(pool, "wgrp", [P, 4, P])
        edge = sb(pool, "edge", [P, 4, LEAD])
        PLh = sb(pool, "PLh", [P, 4, S], F32R)
        PLl = sb(pool, "PLl", [P, 4, S], F32R)
        all_done = [V.now(), A.now(), T.now(), G.now()]
        pool_loaded = core.tally("pool_loaded", 16)
        pool_loaded.inc(G.on(*all_done).dma_start(wgrp[:], wgrp_in))
        pool_loaded.inc(nc.gpsimd.dma_start(edge[:], edge_in))
        m_gates = A.mark(A.on(*all_done, *[t.now() for t in bank_free]).activation(
            gates[:], gates[:], ACT.Sigmoid))
        m_z = G.mark(nc.gpsimd.memset(sums[:, :, 0:LEAD], 0.0))
        V.on(*all_done, *[t.now() for t in bank_free])
        m_pool = []
        m = m_z
        for g, w in enumerate(WINDOWS):
            src, step, j = U[:, g, :], 1, 0
            while step < w:
                dst = sums[:, j, :]
                m = V.mark(V.on(m).tensor_tensor(dst[:, LEAD:], src[:, LEAD:],
                                                 src[:, LEAD - step:W - step], ALU.add))
                src, step, j = dst, 2 * step, 1 - j
            m2 = V.mark(V.on(m).scalar_tensor_tensor(
                out=pooled[:, g, :], in0=src[:, LEAD:], scalar=1.0 / w, in1=U[:, g, LEAD:],
                op0=ALU.mult, op1=ALU.subtract))
            m3 = V.mark(V.on(pool_loaded.now(), m2).tensor_tensor(
                pooled[:, g, 0:LEAD], src[:, LEAD:2 * LEAD], edge[:, g, :], ALU.mult))
            m = V.mark(V.on(m3).tensor_tensor(pooled[:, g, 0:LEAD], pooled[:, g, 0:LEAD],
                                              U[:, g, LEAD:2 * LEAD], ALU.subtract))
            mm = T.mark(T.on(m, pool_loaded.now(), all_done[1]).matmul(
                PS[:, 4 + g, :], wgrp[:, g, :], pooled[:, g, :], start=True, stop=True))
            m = V.mark(V.on(mm).tensor_scalar(pooled[:, g, :], PS[:, 4 + g, :],
                                              cols[:, C_PSCALE + g:C_PSCALE + g + 1], None, ALU.mult))
            ma = A.mark(A.on(m).activation(PLh[:, g, :], pooled[:, g, :], ACT.Copy))
            m = V.mark(V.on(ma).tensor_tensor(PLl[:, g, :], pooled[:, g, :],
                                              PLh[:, g, :].bitcast(F32), ALU.subtract))
        T.on(m)
        V.on(m_gates)

        def flat2(tile, idx):
            return tile[:, bass.ds(idx, 1), :].rearrange("p a n -> p (a n)")

        def split_into(dst_h, dst_l, idx, src, ready):
            m = A.mark(A.on(ready).activation(flat2(dst_h, idx), src, ACT.Copy))
            return V.mark(V.on(m).tensor_tensor(flat2(dst_l, idx), src,
                                                flat2(dst_h, idx).bitcast(F32), ALU.subtract))

        def mix_body(i):
            start = V.now()
            last = [start, start]
            for j in range(4):
                b = j % 2

                def evac(bank, done, freed):
                    m1 = V.mark(V.on(done, last[b]).tensor_tensor(
                        tmp[:, b, :], bank, flat2(gates, i * 4 + j), ALU.mult))
                    m2 = freed.inc(V.e.tensor_tensor(
                        sq[:, b, :], PS[:, 2 + b, :], flat2(gates, i * 4 + (8 + j)), ALU.mult))
                    m3 = V.mark(V.on(m1, m2).tensor_tensor(tmp[:, b, :], tmp[:, b, :], sq[:, b, :],
                                                           ALU.add))
                    last[b] = split_into(Hh, Hl, i * 4 + j, tmp[:, b, :], m3)
                run(unit(evac, rhs=(lambda k: AOh[:, k, :], lambda k: AOl[:, k, :]),
                         second=(PS[:, 2 + b, :], (lambda k: PLh[:, k, :], lambda k: PLl[:, k, :]))))
        dense_loop(2, 4, 4, (12, 4, 0, 0), mix_body)
        pool.close()

        ffn = ExitStack()

        def normed_out(M, groups, rhs, post_col):
            def body(i):
                squares.m = V.now()
                squares.free = [squares.m, squares.m]
                for j, ks in enumerate(groups):
                    def evac(bank, done, freed):
                        dst = flat2(M, i * len(groups) + j)
                        m = freed.inc(A.on(done).activation(dst, bank, ACT.Copy))
                        squares(1 + j, dst, m)
                    for n, nk in enumerate(ks):
                        run(unit(evac, rhs=rhs, nk=nk, k0=KT * n,
                                 group=(n == 0, n == len(ks) - 1)))
            squares.m = V.mark(V.e.memset(ssum[:], 0.0))
            n = len(groups)
            dense_loop(KT // n, sum(len(g) for g in groups), n, (n, n, 0, 0), body)
            squares.m = V.now()
            squares.free = [squares.m, squares.m]
            return inverse_rms(squares.m)

        b1.close()
        M1 = sb(ffn, "M1", [P, KT, S])
        T.on(V.now())
        A.on(V.now())
        m = normed_out(M1, [[KT]] * 4, None, None)
        m = add_normed(M1, C_MIXPOST, m)
        m = inverse_rms(m)
        h_ready = normed_input(C_FFNPRE, m, None)
        ffn.close()

        ffn = ExitStack()
        Ah = sb(ffn, "Ah", [P, FT, S], F32R)
        Al = sb(ffn, "Al", [P, FT, S], F32R)
        A.on(V.now())

        ffn_up = ExitStack()
        conv = sb(ffn_up, "conv", [P, 2, 2, S])

        def up_body(i):
            start_v, start_a = V.now(), A.now()

            def c4(j, tap):
                return cols[:, bass.ds(C_CONV + i * 16 + (4 * j + tap), 1)]

            later = []
            for j in range(4):
                def evac(bank, done, freed, j=j):
                    c = conv[:, j // 2, j % 2, :]
                    m = A.mark(A.on(done, start_v, start_a).activation(
                        c, bank, ACT.Identity, bias=c4(j, 3), scale=c4(j, 2)))
                    m = V.mark(V.on(m).scalar_tensor_tensor(
                        out=c[:, 1:], in0=bank[:, 0:S - 1], scalar=c4(j, 1), in1=c[:, 1:],
                        op0=ALU.mult, op1=ALU.add))
                    m = freed.inc(V.on(m).scalar_tensor_tensor(
                        out=c[:, 2:], in0=bank[:, 0:S - 2], scalar=c4(j, 0), in1=c[:, 2:],
                        op0=ALU.mult, op1=ALU.add))
                    while later:
                        later.pop(0)()
                    if j % 2:
                        def finish(m=m, v=conv[:, j // 2, 0, :], c=c, j=j):
                            m = A.mark(A.on(m).activation(c, c, ACT.Gelu_apprx_tanh))
                            m = V.mark(V.on(m).tensor_tensor(v, v, c, ALU.mult))
                            split_into(Ah, Al, i * 2 + j // 2, v, m)
                        later.append(finish)
                run(unit(evac, ready=lambda r: (h_ready[r],)))
            while later:
                later.pop(0)()
        dense_loop(FT // 2, 4, 4, (8, 8, 0, 0), up_body)
        ffn_up.close()
        T.on(V.now())
        M2 = nc.alloc_sbuf_tensor_at("M2", [P, KT, S], F32, offset=h_place)
        A.on(V.now())
        m = normed_out(M2, [[KT, KT, FT - 2 * KT]] * 4,
                       (lambda k: Ah[:, k, :], lambda k: Al[:, k, :]), None)
        m = add_normed(M2, C_FFNPOST, m)
        m = inverse_rms(m)
        h_ready = normed_input(C_NORM2, m, None)
        ffn.close()

        if debug == "x1":
            stored = core.tally("stored", 16)
            A.on(landed[2].at(480), landed[3].at(480))
            stored.inc(A.on(V.now()).dma_start(out, X[:]))
            A.on(stored.now())
            return

        b2 = ctx.enter_context(ExitStack())
        mats = sb(b2, "mats", [P, N_MATS - 1, P])
        rope = sb(b2, "rope", [P, 3, S])
        rows = sb(b2, "rows", [P, N_ROWS])
        ba_w = sb(b2, "ba_w", [P, KT * 2 * GH])
        ba_h = sb(b2, "ba_h", [P, KT * 2 * GH], F32R)
        ba_l = sb(b2, "ba_l", [P, KT * 2 * GH], F32R)
        Z = sb(b2, "Z", [P, 2 * GH, S])
        O = sb(b2, "O", [P, 2 * GH, S])
        ffn_done = [V.now(), A.now(), T.now(), used.at(Dense.unit + RING)]
        b2_loaded = core.tally("b2_loaded", 16)
        G.on(*ffn_done)
        for dst, src in ((mats, mats_in[:, 1:, :]), (rope, rope_in), (rows, rows_in)):
            b2_loaded.inc(nc.gpsimd.dma_start(dst[:], src))
        b2_loaded.inc(nc.gpsimd.dma_start(ba_w[:], w_ba.rearrange("p k n -> p (k n)")))

        def mat(k):
            return mats[:, k - 1, :]

        def over_tiles(ap):
            return ap.unsqueeze(1).to_broadcast([P, NT, P])

        def tiles(ap):
            return ap.rearrange("p (t n) -> p t n", t=NT)

        def over_cols(ap, n=P):
            return ap.unsqueeze(2).to_broadcast([P, ap.shape[1], n])

        glog = sb(b2, "glog", [P, GH, NT])
        gcum = sb(b2, "gcum", [P, GH, NT])
        beta = sb(b2, "beta", [P, GH, NT])
        beta_eg = sb(b2, "beta_eg", [P, GH, NT])
        to_end = sb(b2, "to_end", [P, GH, NT])
        chunk_decay = sb(b2, "chunk_decay", [P, GH, 2 * NT])
        small = sb(b2, "small", [P, 4, GH * NT])
        neg_lam = sb(b2, "neg_lam", [P, 1])
        subln = sb(b2, "subln", [P, 1])
        lam = sb(b2, "lam", [P, 4])
        lam_prod = sb(b2, "lam_prod", [P, 2, HD])

        lv = rows[:, R_LAM:].rearrange("p (a b d) -> p a b d", a=2, b=2)
        V.on(b2_loaded.now(), *ffn_done)
        A.on(b2_loaded.now(), *ffn_done)
        T.on(b2_loaded.now(), *ffn_done)
        m = V.mark(V.e.tensor_tensor(lam_prod[:], lv[:, :, 0, :], lv[:, :, 1, :], ALU.mult))
        m = V.mark(V.on(m).tensor_reduce(lam[:, 0:2], lam_prod[:], AXX, ALU.add))
        m = A.mark(A.on(m).activation(lam[:, 2:4], lam[:, 0:2], ACT.Exp))
        m = V.mark(V.on(m).tensor_tensor(neg_lam[:], lam[:, 3:4], lam[:, 2:3], ALU.subtract))
        m = V.mark(V.on(m).tensor_scalar(neg_lam[:], neg_lam[:], -LAM_INIT, None, ALU.add))
        V.mark(V.e.tensor_scalar(subln[:], cols[:, C_SUBLN:C_SUBLN + 1], 1.0 - LAM_INIT, None,
                                 ALU.mult))

        m = A.mark(A.e.activation(ba_h[:], ba_w[:], ACT.Copy))
        m = V.mark(V.on(m).tensor_tensor(ba_l[:], ba_w[:], ba_h[:].bitcast(F32), ALU.subtract))
        for t in range(NT):
            for k in range(KT):
                tok, w = slice(t * P, (t + 1) * P), slice(2 * GH * k, 2 * GH * (k + 1))
                T.on(m, h_ready[k])
                for n, (a, b) in enumerate(((Hh, ba_h), (Hl, ba_h), (Hh, ba_l))):
                    ins = T.e.matmul(PS[:, 2, 2 * GH * t:2 * GH * (t + 1)], a[:, k, tok], b[:, w],
                                     start=(k == 0 and n == 0), stop=(k == KT - 1 and n == 2))
        m_ba = T.mark(ins)
        ba = PS[:, 2, 0:2 * GH * NT].rearrange("p (t n) -> p n t", t=NT)
        sm = [small[:, n, :].rearrange("p (h t) -> p h t", t=NT) for n in range(4)]
        m = A.mark(A.on(m_ba).activation(sm[0], ba[:, 0:GH, :], ACT.Exp, scale=-1.0))
        m = V.mark(V.on(m).tensor_scalar(sm[0], sm[0], 1.0, None, ALU.add))
        m_beta = V.mark(V.on(m).reciprocal(beta[:], sm[0]))
        m_y = V.mark(V.on(m_ba).tensor_tensor(
            sm[1], ba[:, GH:2 * GH, :], over_cols(rows[:, R_DT:R_DT + GH], NT), ALU.add))
        m = V.mark(V.on(m_y).tensor_scalar(sm[2], sm[1], -1.0, None, ALU.mult))
        m = V.mark(V.on(m).tensor_tensor(sm[2], sm[1], sm[2], ALU.max))
        m = A.mark(A.on(m).activation(sm[2], sm[2], ACT.Exp, scale=-1.0))
        m = V.mark(V.on(m).tensor_scalar(sm[2], sm[2], 1.0, None, ALU.add))
        m = A.mark(A.on(m).activation(sm[2], sm[2], ACT.Ln))
        m = V.mark(V.on(m).scalar_tensor_tensor(out=small[:, 2, :], in0=small[:, 1, :], scalar=0.0,
                                                in1=small[:, 2, :], op0=ALU.max, op1=ALU.add))
        m2 = A.mark(A.e.activation(lam[:, 0:GH], rows[:, R_ALOG:R_ALOG + GH], ACT.Exp))
        m = V.mark(V.on(m, m2).tensor_tensor(sm[2], sm[2], over_cols(lam[:, 0:GH], NT), ALU.mult))
        m_g = V.mark(V.on(m).tensor_scalar(glog[:], sm[2], -1.0, None, ALU.mult))
        gl2 = glog[:].rearrange("p h t -> p (h t)")
        n16 = GH * NT
        T.on(m_g).matmul(PS[:, 3, 0:n16], mat(K_UPPER), gl2, start=True, stop=True)
        T.e.matmul(PS[:, 3, n16:2 * n16], mat(K_SAME), gl2, start=True, stop=True)
        for n in range(n16):
            ins = T.e.matmul(PS[:, 3, 2 * n16 + 2 * n:2 * n16 + 2 * n + 2],
                             gl2[:, n:n + 1].to_broadcast([P, P]), mat(K_SAME)[:, 0:P:CH],
                             start=True, stop=True)
        m = T.mark(ins)
        m_gc = V.mark(V.on(m).tensor_copy(gcum[:].rearrange("p h t -> p (h t)"), PS[:, 3, 0:n16]))
        m_d = V.mark(V.on(m_gc).tensor_tensor(small[:, 0, :], PS[:, 3, n16:2 * n16],
                                              gcum[:].rearrange("p h t -> p (h t)"), ALU.subtract))
        A.mark(A.on(m_d).activation(to_end[:].rearrange("p h t -> p (h t)"), small[:, 0, :], ACT.Exp))
        A.mark(A.e.activation(chunk_decay[:].rearrange("p h t -> p (h t)"),
                              PS[:, 3, 2 * n16:4 * n16], ACT.Exp))
        m = A.mark(A.e.activation(small[:, 1, :], gcum[:].rearrange("p h t -> p (h t)"), ACT.Exp))
        m = V.mark(V.on(m, m_beta).tensor_tensor(
            beta_eg[:].rearrange("p h t -> p (h t)"), beta[:].rearrange("p h t -> p (h t)"),
            small[:, 1, :], ALU.mult))

        hb = ExitStack()
        names = ("CQ", "CK", "CV", "Vb", "Kb", "Kd", "DT", "Bm", "AT", "LT", "Lo", "LmT", "Ti",
                 "TiT", "Y", "Qb", "Kr", "Vd", "Vdt", "Od")
        B = {n: sb(hb, n, [P, S]) for n in names}
        B["Lm"], B["Wd"] = B["Y"], B["Vd"]
        EG = ssum
        SB2 = sb(hb, "SB2", [P, 2, S])
        P2 = sb(hb, "P2", [P, 2, S])
        St = sb(hb, "St", [P, P])
        gs = sb(hb, "gs", [P, 2, NT])
        rqk = sb(hb, "rqk", [P, 2 * NT])
        rqk_b = sb(hb, "rqk_b", [P, 2, NT, 2])
        r_o = sb(hb, "r_o", [P, 2, NT])
        nmax2 = sb(hb, "nmax2", [P, 8])
        rsum2 = sb(hb, "rsum2", [P, 8])
        rinv2 = sb(hb, "rinv2", [P, 8])
        neg_r = sb(hb, "neg_r", [P, 8])

        def row_of(scalars, bank, ready, rhs=None):
            for t in range(NT):
                ins = T.on(*ready).matmul(PS[:, bank, t * P:(t + 1) * P], scalars(t),
                                          ident[:] if rhs is None else rhs, start=True, stop=True)
            return T.mark(ins)

        def per_tile(bank, lhs, rhs, ready):
            for t in range(NT):
                tok = slice(t * P, (t + 1) * P)
                ins = T.on(*ready).matmul(PS[:, bank, tok], lhs[:, tok], rhs[:, tok],
                                          start=True, stop=True)
            return T.mark(ins)

        def turn_tiles(bank, src, ready):
            for t in range(NT):
                tok = slice(t * P, (t + 1) * P)
                ins = T.on(*ready).transpose(PS[:, bank, tok], src[:, tok], ident[:])
            return T.mark(ins)

        def head_body(i):
            start = [V.now(), A.now(), T.now(), G.now()]
            got = {}

            def flat(tile, idx):
                return tile[:, bass.ds(idx, 1), :].rearrange("p a n -> p (a n)")

            def head(tile):
                return flat(tile, i)

            def conv_silu(name, j):
                c = B[name]

                def tap(n):
                    return cols[:, bass.ds(C_CONV2 + i * 12 + (4 * j + n), 1)]

                def evac(bank, done, freed):
                    m = A.mark(A.on_apart(done, *start).activation(c[:], bank, ACT.Identity,
                                                                   bias=0.0, scale=tap(3)))
                    for n in (2, 1):
                        m = V.mark(V.on(m, *start).scalar_tensor_tensor(
                            out=c[:, 3 - n:], in0=bank[:, 0:S - 3 + n], scalar=tap(n),
                            in1=c[:, 3 - n:], op0=ALU.mult, op1=ALU.add))
                    m = freed.inc(V.on(m).scalar_tensor_tensor(
                        out=c[:, 3:], in0=bank[:, 0:S - 3], scalar=tap(0),
                        in1=c[:, 3:], op0=ALU.mult, op1=ALU.add))
                    got[name] = A.mark(A.on(m).activation(c[:], c[:], ACT.Silu))
                return evac

            def keep_z(branch):
                def evac(bank, done, freed):
                    freed.inc(A.on_apart(done).activation(flat(Z, i + GH * branch), bank, ACT.Copy))
                return evac

            def keep_qk(name, j, col):
                def evac(bank, done, freed):
                    got[name] = A.mark(A.on(done, *start).activation(
                        B[name][:], bank, ACT.Copy, scale=cols[:, col:col + 1]))
                    got[name + "2"] = freed.inc(A.on(sq_free[j]).activation(sq[:, j, :], bank,
                                                                            ACT.Square))
                return evac

            def keep_v(bank, done, freed):
                got["v"] = freed.inc(A.on(done, *start).activation(B["Vd"][:], bank, ACT.Copy))

            m_gs = V.mark(V.on(*start).tensor_copy(gs[:, 0, :], head(glog)))
            m_gs = V.mark(V.e.tensor_copy(gs[:, 1, :], head(beta)))
            m_st = V.mark(V.e.memset(St[:], 0.0))

            run(unit(conv_silu("CQ", 0)))
            run(unit(conv_silu("CK", 1)))
            run(unit(conv_silu("CV", 2)))
            sq_free = [None, None]
            Fill.gens = [unit(keep_z(0)), unit(keep_qk("Qb", 0, C_QNORM)),
                         unit(keep_qk("Kr", 1, C_KNORM)), unit(keep_v), unit(keep_z(1))]

            fill(3)
            for j, n in enumerate(("CQ", "CK")):
                m = A.mark(A.on(got[n], *start).activation(sq[:, j, :], B[n][:], ACT.Square))
                fill(1)
                for t in range(NT):
                    ins = T.on(m, *start).matmul(PS[:, 2, NT * j + t:NT * j + t + 1],
                                                 sq[:, j, t * P:(t + 1) * P], ones[:],
                                                 start=True, stop=True)
                sq_free[j] = m = T.mark(ins)
            m_grow = row_of(lambda t: gs[:, 0, t:t + 1].to_broadcast([P, P]), 4, (m_gs,),
                            rhs=mat(K_UPPER))
            m_brow = row_of(lambda t: gs[:, 1, t:t + 1].to_broadcast([P, P]), 5, (m_gs,))
            m_n = V.mark(V.on(m).tensor_scalar(rqk[:], PS[:, 2, 0:2 * NT], EPS, None, ALU.add))
            m_n = G.mark(G.on(m_n).tensor_tensor(rqk[:], rqk[:], half[:, 0:2 * NT], ALU.pow))
            m = V.mark(V.on(m_grow).tensor_tensor(tiles(B["DT"][:]), tiles(PS[:, 4, :]),
                                                  over_cols(head(gcum)), ALU.subtract))
            m = V.mark(V.on(m).tensor_tensor(tiles(B["DT"][:]), tiles(B["DT"][:]),
                                             over_tiles(mat(K_NEG_T)), ALU.add))
            m_bm = V.mark(V.on(m_brow).tensor_tensor(tiles(B["Bm"][:]), tiles(PS[:, 5, :]),
                                                     over_tiles(mat(K_STRICT_T)), ALU.mult))
            m_dt = A.mark(A.on(m).activation(B["DT"][:], B["DT"][:], ACT.Exp))
            m_eg = A.mark(A.on(m_grow).activation(EG[:], PS[:, 4, :], ACT.Exp))
            fill(1)
            m_vt = turn_tiles(6, B["CV"][:], (got["CV"],))
            m_rk = row_of(lambda t: rqk[:, NT + t:NT + t + 1].to_broadcast([P, P]), 3, (m_n,))
            m_kn = V.mark(V.on(m_rk).tensor_tensor(B["CK"][:], B["CK"][:], PS[:, 3, :], ALU.mult))
            m_vb = V.mark(V.on(m_vt).tensor_tensor(tiles(B["Vb"][:]), tiles(PS[:, 6, :]),
                                                   over_cols(head(beta)), ALU.mult))
            fill(1)
            m_kk = per_tile(2, B["CK"], B["CK"], (m_kn,))
            m_qk = per_tile(7, B["CK"], B["CQ"], (m_kn,))
            m_kt = turn_tiles(3, B["CK"][:], (m_kn,))
            m = V.mark(V.on(m_kk, m_dt).tensor_tensor(B["LT"][:], PS[:, 2, :], B["DT"][:], ALU.mult))
            m_lt = V.mark(V.on(m).tensor_tensor(B["LT"][:], B["LT"][:], B["Bm"][:], ALU.mult))
            m_at = V.mark(V.on(m_qk).tensor_tensor(B["AT"][:], PS[:, 7, :], B["DT"][:], ALU.mult))
            fill(2)
            m = turn_tiles(4, B["LT"][:], (m_lt, m_eg))
            m_lo = A.mark(A.on(m).activation(B["Lo"][:], PS[:, 4, :], ACT.Copy))

            def level_masks(lv, read):
                a = G.mark(G.on(m_lo, *read).tensor_tensor(
                    tiles(B["LmT"][:]), tiles(B["LT"][:]),
                    over_tiles(mat(K_LEVEL + 1 + lv)), ALU.mult))
                if lv:
                    return a
                return G.mark(G.e.tensor_tensor(tiles(B["Lm"][:]), tiles(B["Lo"][:]),
                                                over_tiles(mat(K_LEVEL)), ALU.mult))
            m_lm = level_masks(0, ())
            idn = over_tiles(ident[:])
            V.on(m_lm).tensor_tensor(tiles(B["Ti"][:]), idn, tiles(B["Lm"][:]), ALU.subtract)
            m_ti = V.mark(V.e.tensor_tensor(tiles(B["TiT"][:]), idn, tiles(B["LmT"][:]),
                                            ALU.subtract))
            m_kb = V.mark(V.on(m_kt).tensor_tensor(tiles(B["Kb"][:]), tiles(PS[:, 3, :]),
                                                   over_cols(head(beta_eg)), ALU.mult))
            m_kd = V.mark(V.e.tensor_tensor(tiles(B["Kd"][:]), tiles(PS[:, 3, :]),
                                            over_cols(head(to_end)), ALU.mult))
            m_qg = V.mark(V.on(m_qk, m_eg).tensor_tensor(B["CQ"][:], B["CQ"][:], EG[:], ALU.mult))
            for lv in range(1, N_LEVELS):
                m_lm = level_masks(lv, (m_ti, m_lm if lv == 1 else m_y))
                fill(2)
                m_y = per_tile(5, B["LmT"], B["Ti"], (m_lm, m_ti, m_bm))
                m_ya = A.mark(A.on(m_y).activation(B["Y"][:], PS[:, 5, :], ACT.Copy))
                fill(2)
                m_tt = per_tile(7, B["Y"], B["TiT"], (m_ya, m_at))
                if lv < N_LEVELS - 1:
                    m_t = per_tile(6, B["TiT"], B["Y"], (m_vb,))
                    V.mark(V.on(m_t).tensor_tensor(B["Ti"][:], B["Ti"][:], PS[:, 6, :],
                                                   ALU.subtract))
                m_ti = V.mark(V.on(m_tt).tensor_tensor(B["TiT"][:], B["TiT"][:], PS[:, 7, :],
                                                       ALU.subtract))
            fill(2)
            m = per_tile(5, B["TiT"], B["Vb"], (m_ti, m_vb, m_ya))
            m_u = A.mark(A.on(m).activation(B["CV"][:], PS[:, 5, :], ACT.Copy))
            m = per_tile(6, B["Kb"], B["TiT"], (m_kb,))
            m_w = V.mark(V.on(m, m_qg).tensor_copy(EG[:], PS[:, 6, :]))
            fill_all()

            def scan():
                VN, U_, W_ = B["Y"], B["CV"], EG
                m_s = m_st
                for c in range(S // CH):
                    t, r0 = c // 2, CH * (c % 2)
                    rows_ = slice(r0, r0 + CH)
                    own, tile_ = slice(t * P + r0, t * P + r0 + CH), slice(t * P, (t + 1) * P)
                    m = T.mark(T.on(m_s, m_w, m_kt, m_kd).matmul(
                        PS[rows_, 2, 0:P], W_[:, own], St[:], start=True, stop=True))
                    m_v = V.mark(V.on(m, m_u).tensor_tensor(VN[rows_, tile_], U_[rows_, tile_],
                                                            PS[rows_, 2, 0:P], ALU.subtract))
                    yield
                    T.on(m_qg).matmul(PS[rows_, 3, tile_], B["CQ"][:, own], St[:],
                                      start=True, stop=False)
                    m = T.mark(T.on(m_v).matmul(PS[:, 2, P:2 * P], B["Kd"][rows_, tile_],
                                                VN[rows_, tile_], start=True, stop=True))
                    m_o = T.mark(T.e.matmul(PS[rows_, 3, tile_], B["AT"][rows_, own],
                                            VN[rows_, tile_], start=False, stop=True))
                    m_s = V.mark(V.on(m).scalar_tensor_tensor(
                        out=St[:], in0=St[:],
                        scalar=chunk_decay[:].rearrange("p h c -> p (h c)")[
                            :, bass.ds(i * (2 * NT) + c, 1)],
                        in1=PS[:, 2, P:2 * P], op0=ALU.mult, op1=ALU.add))
                    yield
                m = V.mark(V.on(m_o).tensor_scalar(rqk[:, 0:NT], rqk[:, 0:NT], P ** -0.5, None,
                                                   ALU.mult))
                m = V.mark(V.on(m).tensor_tensor(tiles(B["Ti"][:]), tiles(PS[:, 3, :]),
                                                 over_cols(rqk[:, 0:NT]), ALU.mult))
                yield
                for _ in out_norm(B["Ti"], B["Y"], 0, 3, m, EPS, cols[:, C_GNORM:C_GNORM + 1]):
                    yield

            def out_norm(o, spare, branch, bank, m, eps, weight):
                m_q = G.mark(G.on(m).tensor_tensor(spare[:], o[:], o[:], ALU.mult))
                r = r_o[:, branch, :]
                yield
                m_q = V.mark(V.on(m_q).tensor_reduce(r, tiles(spare[:]), AXX, ALU.add))
                m_q = V.mark(V.on(m_q).tensor_scalar(r, r, 1.0 / P, eps, ALU.mult, ALU.add))
                m_q = G.mark(G.on(m_q).tensor_tensor(r, r, half[:, 0:NT], ALU.pow))
                m_q = V.mark(V.on(m_q).tensor_tensor(tiles(o[:]), tiles(o[:]), over_cols(r),
                                                     ALU.mult))
                yield
                m_q = turn_tiles(bank, o[:], (m_q,))
                A.mark(A.on_apart(m_q).activation(flat(O, i + GH * branch), PS[:, bank, :], ACT.Copy,
                                                  scale=weight))
                yield

            def squares_of(name, j, m):
                for t in range(NT):
                    ins = T.on(m).matmul(PS[:, 4, 8 * j + 2 * t:8 * j + 2 * t + 2],
                                         sq[:, j, t * P:(t + 1) * P], mat(K_SAME)[:, 0:P:CH],
                                         start=True, stop=True)
                return T.mark(ins)
            T.on(m_lo)
            squares_of("Qb", 0, got["Qb2"])
            m = squares_of("Kr", 1, got["Kr2"])
            r2 = rqk_b[:].rearrange("p a t c -> p (a t c)")
            m = V.mark(V.on(m).tensor_scalar(r2, PS[:, 4, 0:16], 1.0 / HD, EPS, ALU.mult, ALU.add))
            m = G.mark(G.on(m).tensor_tensor(r2, r2, half[:, 0:16], ALU.pow))
            m_rq = V.mark(V.on(m).tensor_scalar(rqk_b[:, 0, :, :], rqk_b[:, 0, :, :], HD ** -0.5,
                                                None, ALU.mult))
            for t in range(NT):
                for c in range(2):
                    ins = T.on(m, m_u).matmul(
                        PS[c * HD:(c + 1) * HD, 5, t * P:(t + 1) * P],
                        rqk_b[:, 1, t, c:c + 1].to_broadcast([P, HD]), ident[:],
                        start=True, stop=True)
            m_k = T.mark(ins)
            m_k = V.mark(V.on(m_k).tensor_tensor(B["Kr"][:], B["Kr"][:], PS[:, 5, :], ALU.mult))

            gens = [scan()]

            def advance(n=1):
                for _ in range(n):
                    if gens:
                        try:
                            next(gens[0])
                        except StopIteration:
                            gens.pop(0)
            advance()
            ready = {}
            for j, (name, bank, m) in enumerate((("Qb", 6, got["Qb"]), ("Kr", 7, m_k))):
                x = B[name][:]
                mr = T.mark(T.on(m, m_w, m_ti).matmul(PS[:, bank, :], mat(K_SWAP), x, start=True,
                                                      stop=True))
                mt = V.mark(V.on(mr).tensor_tensor(tmp[:, j, :], PS[:, bank, :], rope[:, 1, :],
                                                   ALU.mult))
                mc = G.mark(G.on(mr, m).tensor_tensor(x, x, rope[:, 0, :], ALU.mult))
                ready[name] = G.mark(G.on(mc, mt).tensor_tensor(x, x, tmp[:, j, :], ALU.add))
                advance()
            m = turn_tiles(6, B["Vd"][:], (got["v"], mt))
            m_v2 = A.mark(A.on(m).activation(B["Vdt"][:], PS[:, 6, :], ACT.Copy))
            free = {"S": [m_k, m_k], "SB": [None] * 2, "P": [None] * 2, "PT": [m_v2] * 2,
                    "PTs": [ready["Kr"]] * 2, "O": [mt] * 2}
            banks = {"S": (4, 5), "PT": (6, 6), "O": (7, 7)}
            bufs = (SB2, P2, nmax2, rsum2, rinv2, free)
            A.on(m_v2)
            T.on(m_v2)
            to_turn = to_apply = None
            wd_free = None
            for n, qt in enumerate((3, 2, 1, 0, None, None)):
                got_turned = scored = None
                if qt is not None:
                    nk = (qt + 1) * P
                    for a in range(2):
                        b = 2 * n + a
                        m_p, m_r = attend(a, qt, b, B["Qb"], B["Kr"], rqk_b[:, 0, qt, a:a + 1],
                                          rope[:, 2, S - nk:], (ready["Qb"], ready["Kr"], m_rq),
                                          bufs, banks)
                        advance()
                        if a == 0:
                            m0_ = V.mark(V.on(m_p, m_r).tensor_scalar(
                                P2[:, 0, 0:nk], P2[:, 0, 0:nk], rinv2[:, b:b + 1], None, ALU.mult))
                        else:
                            m_r = V.mark(V.on(m_r).tensor_tensor(neg_r[:, b:b + 1], neg_lam[:],
                                                                 rinv2[:, b:b + 1], ALU.mult))
                            m_w2 = V.mark(V.on(m_p, m_r, m0_, wd_free).scalar_tensor_tensor(
                                out=B["Wd"][:, 0:nk], in0=P2[:, 1, 0:nk], scalar=neg_r[:, b:b + 1],
                                in1=P2[:, 0, 0:nk], op0=ALU.mult, op1=ALU.add))
                            free["P"] = [m_w2, m_w2]
                        advance()
                    wd_free, m_t = turn_weights(qt, 0, B["Wd"], m_w2, tmp, free, banks)
                    advance()
                    m = apply_weights(qt, 0, m_t, tmp,
                                      lambda kt: B["Vdt"][:, kt * P:(kt + 1) * P], P, free, banks)
                    m_od = A.mark(A.on(m).activation(B["Od"][:, qt * P:(qt + 1) * P],
                                                     PS[:, 7, 0:P], ACT.Copy))
                    free["O"] = [m_od, m_od]
            while gens:
                advance()
            for _ in out_norm(B["Od"], B["Wd"], 1, 6, m_od, SUB_EPS, subln[:, 0:1]):
                pass

        T.on(m_beta, V.now(), A.now())
        A.on(V.now())
        G.on(V.now(), A.now())
        dense_loop(GH, BODY, BODY, PER2, head_body)
        hb.close()

        m_z = A.mark(A.on(V.now(), T.now(), G.now(), A.now(), *[t.now() for t in bank_free])
                     .activation(Z[:], Z[:], ACT.Silu))
        V.on(A.now(), T.now(), G.now())
        free = [None, None]
        h_ready = []
        for k in range(2 * GH):
            m = V.mark(V.on(m_z, free[k % 2]).tensor_tensor(tmp[:, k % 2, :], O[:, k, :], Z[:, k, :],
                                                            ALU.mult))
            m = A.mark(A.on(m).activation(Hh[:, k, :], tmp[:, k % 2, :], ACT.Copy))
            free[k % 2] = V.mark(V.on(m).tensor_tensor(
                Hl[:, k, :], tmp[:, k % 2, :], Hh[:, k, :].bitcast(F32), ALU.subtract))
            h_ready.append(free[k % 2])
        stored = core.tally("stored", 16)
        for k in range(KT):
            def evac(bank, done, freed, k=k):
                m = freed.inc(V.on(done).tensor_tensor(X[:, k, :], X[:, k, :], bank, ALU.add))
                stored.inc(A.on(m).dma_start(out[:, k, :], X[:, k, :]))
            run(unit(evac, ready=lambda r: (h_ready[r],)))
        A.on(stored.now())


def _units(np, w):
    k, n = w.shape
    return w.reshape(k // P, P, n // P, P).transpose(2, 1, 0, 3)


def _layout(np, inp):
    w1 = _units(np, inp["w_in"][0])
    order = []
    for h in range(PAIRS):
        order += [h, 4 + h, 8 + h, 12 + h, 16 + 2 * h, 17 + 2 * h, 24 + 2 * h, 25 + 2 * h]
    p1 = w1[order]
    mix = np.concatenate([_units(np, inp["w_attn_out"][0]), _units(np, inp["w_pool_out"][0])], axis=2)
    wo = _units(np, inp["w_o"][0])
    up = _units(np, inp["w_up"][0])
    up = up.reshape(2, FT, P, KT, P).transpose(1, 0, 2, 3, 4).reshape(2 * FT, P, KT, P)
    down = _units(np, inp["w_down"][0])
    down = np.concatenate([down, np.zeros((KT, P, 24 - FT, P), np.float32)], axis=2)
    down = down.reshape(KT, P, 3, KT, P).transpose(0, 2, 1, 3, 4).reshape(24, P, KT, P)
    w2 = inp["w_in_2"][0]
    n = 4 * GH * P
    big = np.concatenate([w2[:, :n], w2[:, n + 2 * GH:]], axis=1)
    p2 = _units(np, big).reshape(8, GH, P, KT, P).transpose(1, 0, 2, 3, 4).reshape(32, P, KT, P)
    wout = _units(np, inp["w_out_2"][0])
    units = np.concatenate([p1, mix, wo, up, down, p2, wout], axis=0)
    units = np.ascontiguousarray(units).reshape(N_UNITS, P, D)
    w_ba = np.ascontiguousarray(w2[:, n:n + 2 * GH].reshape(KT, P, 2 * GH).transpose(1, 0, 2))

    def by_part(v):
        return v.reshape(-1, P).T

    conv = np.concatenate([inp["conv_w"][0], inp["conv_b"]], axis=0)
    conv = conv.reshape(4, 2, FT, P).transpose(3, 2, 1, 0).reshape(P, 4 * 2 * FT)
    conv2 = inp["conv_w_2"][0].reshape(4, 3, GH, P).transpose(3, 2, 1, 0).reshape(P, 48)
    cols = np.concatenate(
        [by_part(inp[k][0]) for k in ("norm_mix_pre", "norm_mix_post", "norm_ffn_pre",
                                      "norm_ffn_post", "w_norm_2", "b_gate", "pool_scale")]
        + [conv, conv2, by_part(inp["gdn_norm_w_2"][0])]
        + [np.concatenate([inp[k][0], inp[k][0]])[:, None] for k in ("q_norm_w_2", "k_norm_w_2")]
        + [by_part(inp["subln_w_2"][0])], axis=1)
    rows = np.concatenate([inp["a_log_2"][0], inp["dt_bias_2"][0], inp["lambda_q1_2"][0],
                           inp["lambda_k1_2"][0], inp["lambda_q2_2"][0], inp["lambda_k2_2"][0]])
    rows = np.broadcast_to(rows[None, :], (P, N_ROWS))
    rb = inp["rel_bias"][0]
    mid = (rb.shape[1] - 1) // 2
    dist = (S - P) + np.arange(P)[:, None] - np.arange(S)[None, :]
    rel = rb[:, np.clip(dist, -mid, mid) + mid].transpose(1, 0, 2)
    wgrp = inp["w_pool_group"][0].transpose(1, 0, 2)
    x = inp["x"][0].T.reshape(KT, P, S).transpose(1, 0, 2)

    t = np.arange(P)
    i, j = np.meshgrid(t, t, indexing="ij")
    same = (i // CH) == (j // CH)
    mats = [i == j, (i <= j) & same, same, (i // 64 == j // 64) & ((i % 64 + 32) % 64 == j % 64),
            np.where((i <= j) & same, 0.0, NEG), (i < j) & same]
    for lv in range(N_LEVELS):
        b = 1 << lv
        low = (i // (2 * b) == j // (2 * b)) & (i // b > j // b)
        mats += [low, low.T] if lv == 0 else [low.T]
    mats = np.stack([m.astype(np.float32) for m in mats], axis=1)
    inv = 10000.0 ** (-np.arange(0, HD, 2, dtype=np.float32) / np.float32(HD))
    ang = np.arange(S, dtype=np.float32)[:, None] * inv.astype(np.float32)[None, :]
    c, s = np.cos(ang).T, np.sin(ang).T
    causal = np.zeros((P, S), np.float32)
    causal[:, S - P:] = np.where(i >= j, 0.0, NEG)
    rope = np.stack([np.concatenate([c, c, c, c]), np.concatenate([-s, s, -s, s]), causal], axis=1)
    edge = np.stack([1.0 / np.minimum(np.arange(LEAD) + 1, w) for w in WINDOWS])
    edge = np.broadcast_to(edge[None].astype(np.float32), (P, 4, LEAD))
    return {"x": x, "w_units": units, "w_ba": w_ba, "cols": cols, "mats": mats, "rope": rope,
            "rows": rows, "rel": rel, "edge": edge, "wgrp": wgrp}


def kernel(**inputs):
    import numpy as _np
    import concourse.bacc as _bacc
    from concourse import mybir as _mybir
    from concourse.bass_utils import run_bass_kernel_spmd as _run

    nc = _bacc.Bacc("TRN2", target_bir_lowering=False, num_devices=1)
    arrays = _layout(_np, {k: _np.asarray(v) for k, v in inputs.items()})
    arrays = {"in_" + k: _np.ascontiguousarray(v, dtype=_np.float32) for k, v in arrays.items()}
    args = [nc.dram_tensor(k, v.shape, _mybir.dt.from_np(v.dtype), kind="ExternalInput").ap()
            for k, v in arrays.items()]
    out = nc.dram_tensor("out_0", (P, KT, S), _mybir.dt.float32, kind="ExternalOutput").ap()
    build(nc, *args, out, debug=DEBUG)
    r = _run(nc, [arrays], core_ids=[0])
    got = r.results[0]["out_0"]
    return _np.ascontiguousarray(got.transpose(2, 1, 0)).reshape(1, S, D)


DEBUG = None
```

```python
from contextlib import ExitStack

import concourse.bass as bass
from concourse import mybir

F32 = mybir.dt.float32
F32R = mybir.dt.float32r
ACT = mybir.ActivationFunctionType
ALU = mybir.AluOpType
AXX = mybir.AxisListType.X

P = 128
S = 512
D = 1024
KT = D // P
NT = S // P
HEADS, HD = 8, 64
PAIRS = HEADS // 2
CH = 64
GH = 4
DFF = 2816
FT = DFF // P
EPS, SUB_EPS = 1e-6, 1e-5
WINDOWS = (2, 4, 8, 16)
LEAD = 16
LAM_INIT = 0.8 - 0.6
NEG = -1e30

N_P1, N_MIX, N_WO, N_UP, N_DOWN, N_P2, N_OUT = 32, 8, 8, 2 * FT, 3 * 8, 32, 8
N_UNITS = N_P1 + N_MIX + N_WO + N_UP + N_DOWN + N_P2 + N_OUT
RING = 4
BODY = 8

C_MIXPRE, C_MIXPOST, C_FFNPRE, C_FFNPOST, C_NORM2 = 0, 8, 16, 24, 32
C_BGATE = 40
C_PSCALE = 56
C_CONV = 60
C_CONV2 = C_CONV + 4 * 2 * FT
C_GNORM = C_CONV2 + 4 * 12
C_QNORM, C_KNORM, C_SUBLN = C_GNORM + 1, C_GNORM + 2, C_GNORM + 3
N_COLS = C_GNORM + 4

(K_ID, K_UPPER, K_SAME, K_SWAP, K_NEG_T, K_STRICT_T, K_LEVEL) = range(7)
N_LEVELS = 6
N_MATS = K_LEVEL + 1 + N_LEVELS
R_ALOG, R_DT, R_LAM = 0, GH, 2 * GH
N_ROWS = R_LAM + 4 * HD


class Tally:

    def __init__(self, name, sem, step=1, start=0):
        self.name, self.sem, self.step, self.n, self.per = name, sem, step, start, 0

    scope = 0

    def inc(self, ins):
        ins.then_inc(self.sem, self.step)
        self.n += self.step
        return self.now()

    def now(self):
        return self.at(self.n)

    def at(self, n):
        return (self, n, Tally.scope)


class Queue:

    def __init__(self, core, engine, sem):
        self.core, self.e, self.tally, self.seen = core, engine, sem, {}

    def on(self, *marks):
        for mark in marks:
            if mark is None:
                continue
            tally, n, scope = mark
            assert scope in (0, Tally.scope), "a mark of a loop that has ended"
            if self.seen.get((id(tally), scope), -1) >= n:
                continue
            self.seen[(id(tally), scope)] = n
            if scope:
                self.e.wait_ge(tally.sem, self.core.turn * tally.per + n)
            else:
                self.e.wait_ge(tally.sem, n)
        return self.e

    def on_apart(self, *marks):
        self.on(*marks)
        self.e.sem_inc(self.core.spare, 1)
        return self.e

    def mark(self, ins):
        return self.tally.inc(ins)

    def now(self):
        return self.tally.now()


class Core:
    def __init__(self, nc, ctx):
        self.nc, self.ctx, self.turn, self.loops, self.queues = nc, ctx, None, 0, []
        self.spare = ctx.enter_context(nc.semaphore("spare"))

    def queue(self, engine, name):
        q = Queue(self, engine, self.tally(name))
        self.queues.append(q)
        return q

    def tally(self, name, step=1, start=0):
        return Tally(name, self.ctx.enter_context(self.nc.semaphore(name)), step, start)

    def loop(self, turns, per, body, engines):
        begin = {t: t.n for t in per}
        for q in self.queues:
            q.seen = {}
        self.loops += 1
        with self.nc.Fori(0, turns, engines=engines) as i:
            self.turn, Tally.scope = i, self.loops
            for t, n in per.items():
                t.per = n
            body(i)
        self.turn, Tally.scope = None, 0
        bad = [(t.name, t.n - begin[t], n) for t, n in per.items() if t.n - begin[t] != n]
        assert not bad, bad
        for q in self.queues:
            q.seen = {}
        for t, n in per.items():
            t.n = begin[t] + turns * n


PER2 = (101, 33, 72, 19)


def build(nc, x_in, w_units, w_ba, cols_in, mats_in, rope_in, rows_in, relb_in, edge_in,
          wgrp_in, out, debug=None):
    ctx = ExitStack()
    with ctx:
        core = Core(nc, ctx)
        V = core.queue(nc.vector, "vector_done")
        A = core.queue(nc.scalar, "scalar_done")
        T = core.queue(nc.tensor, "tensor_done")
        G = core.queue(nc.gpsimd, "gpsimd_done")
        COMPUTE = [mybir.EngineType.PE, mybir.EngineType.Activation, mybir.EngineType.DVE,
                   mybir.EngineType.Pool]

        def sb(stack, name, shape, dt=F32):
            return stack.enter_context(nc.sbuf_tensor(name, shape, dt))

        X = sb(ctx, "X", [P, KT, S])
        h_place = nc.sbuf_base
        Hh = sb(ctx, "Hh", [P, KT, S], F32R)
        Hl = sb(ctx, "Hl", [P, KT, S], F32R)
        raw = sb(ctx, "raw", [P, RING, D])
        Wh = sb(ctx, "Wh", [P, RING, D], F32R)
        Wl = sb(ctx, "Wl", [P, RING, D], F32R)
        cols = sb(ctx, "cols", [P, N_COLS])
        ident = sb(ctx, "ident", [P, P])
        ones = sb(ctx, "ones", [P, 1])
        half = sb(ctx, "half", [P, 4 * NT])
        ssum = sb(ctx, "ssum", [P, S])
        sq = sb(ctx, "sq", [P, 2, S])
        rstd = sb(ctx, "rstd", [P, NT])
        tmp = sb(ctx, "tmp", [P, 2, S])
        PS = ctx.enter_context(nc.psum_tensor("PS", [P, 8, S], F32))

        landed = [core.tally(f"unit_landed{s}", 16) for s in range(RING)]
        rounded = core.tally("unit_rounded")
        split = core.tally("unit_split", start=RING)
        used = core.tally("unit_used", start=RING)
        bank_free = [core.tally(f"bank{b}_free", start=1) for b in range(2)]
        nc.vector.sem_inc(split.sem, RING)
        nc.tensor.sem_inc(used.sem, RING)
        for t in bank_free:
            nc.vector.sem_inc(t.sem, 1)
        loaded_small = core.tally("small_loaded", 16)

        for dst, src in ((cols, cols_in), (ident, mats_in[:, 0, :])):
            loaded_small.inc(nc.scalar.dma_start(dst[:], src))
        loaded_x = [core.tally(f"x_loaded{n}", 16) for n in range(2)]
        for n in range(2):
            loaded_x[n].inc(nc.scalar.dma_start(X[:, 4 * n:4 * n + 4, :], x_in[:, 4 * n:4 * n + 4, :]))

        n_units = N_UNITS - 36 if debug else N_UNITS
        with nc.sync.Fori(0, n_units // RING) as i:
            for s in range(RING):
                nc.sync.wait_ge(split.sem, i * RING + (s + 1))
                nc.sync.dma_start(raw[:, s, :], w_units[bass.ds(i * RING + s, 1)]
                                  .rearrange("a p n -> (a p) n")).then_inc(landed[s].sem, 16)

        class Dense:
            unit = 0
            ahead = 0
            group = 0

        def split_unit():
            n = Dense.ahead
            Dense.ahead += 1
            s = n % RING
            rounded.inc(A.on(landed[s].at(16 * (n // RING + 1)), used.at(n + 1))
                        .activation(Wh[:, s, :], raw[:, s, :], ACT.Copy))
            split.inc(V.on(rounded.at(n + 1)).tensor_tensor(
                Wl[:, s, :], raw[:, s, :], Wh[:, s, :].bitcast(F32), ALU.subtract))
            landed[s].n = 16 * (n // RING + 1)

        def products(bank, rhs_h, rhs_l, ks, ready, first=True, last=True, fresh=True):
            n = Dense.unit
            s = n % RING
            for j, (k, r) in enumerate(ks):
                T.on(split.at(n + 1 + RING), *(ready(r) if ready else ()))
                wsl = slice(k * P, (k + 1) * P)
                for m, (a, b) in enumerate(((Wh, rhs_h), (Wh, rhs_l), (Wl, rhs_h))):
                    ins = nc.tensor.matmul(bank, a[:, s, wsl], b(r), start=first and j == 0 and m == 0,
                                           stop=last and j == len(ks) - 1 and m == 2)
                yield ins

        def unit(evac, rhs=None, ready=None, nk=KT, group=(True, True), k0=0, second=None):
            b = Dense.group % 2
            if rhs is None:
                rhs = (lambda k: Hh[:, k, :], lambda k: Hl[:, k, :])
            if Dense.ahead < total_ahead[0]:
                split_unit()
            if group[0]:
                T.on(bank_free[b].at(Dense.group // 2 + 1))
            bank = PS[:, b, :]
            ins = None
            if second is None:
                for ins in products(bank, *rhs, [(k, k0 + k) for k in range(nk)], ready,
                                    first=group[0], last=group[1]):
                    yield
            else:
                for ins in products(bank, *rhs, [(k, k) for k in range(4)], ready):
                    yield
                for ins in products(second[0], *second[1], [(k, k - 4) for k in range(4, 8)], ready):
                    yield
            done = used.inc(ins)
            Dense.unit += 1
            if group[1]:
                Dense.group += 1
                evac(bank, done, bank_free[b])
            yield

        def run(gen):
            for _ in gen:
                pass

        total_ahead = [n_units]

        def inverse_rms(ready, bank=2, scale=1.0 / D, eps=EPS):
            for t in range(NT):
                ins = T.on(ready).matmul(PS[:, bank + 1, t:t + 1], ssum[:, t * P:(t + 1) * P],
                                         ones[:], start=True, stop=True)
            m = T.mark(ins)
            m = V.mark(V.on(m).tensor_scalar(rstd[:], PS[:, bank + 1, 0:NT], scale, eps,
                                             ALU.mult, ALU.add))
            m = G.mark(G.on(m).tensor_tensor(rstd[:], rstd[:], half[:, 0:NT], ALU.pow))
            for t in range(NT):
                ins = T.on(m).matmul(PS[:, bank, t * P:(t + 1) * P],
                                     rstd[:, t:t + 1].to_broadcast([P, P]), ident[:],
                                     start=True, stop=True)
            return T.mark(ins)

        def squares(k, src, ready):
            if k == 0:
                squares.m = A.mark(A.on(ready, squares.m).activation(ssum[:], src, ACT.Square))
                return squares.m
            a = A.mark(A.on_apart(ready, squares.free[k % 2]).activation(sq[:, k % 2, :], src, ACT.Square))
            squares.m = V.mark(V.on(a, squares.m).tensor_tensor(ssum[:], ssum[:], sq[:, k % 2, :],
                                                                ALU.add))
            squares.free[k % 2] = squares.m
            return squares.m
        squares.m = None
        squares.free = [None, None]

        def normed_input(col, ready_r, x_ready):
            marks, free = [], [None, None]
            for k in range(KT):
                c = col + k
                m = V.mark(V.on(ready_r, x_ready, free[k % 2]).scalar_tensor_tensor(
                    out=tmp[:, k % 2, :], in0=X[:, k, :], scalar=cols[:, c:c + 1],
                    in1=PS[:, 2, :], op0=ALU.mult, op1=ALU.mult))
                a = A.mark(A.on(m).activation(Hh[:, k, :], tmp[:, k % 2, :], ACT.Copy))
                free[k % 2] = V.mark(V.on(a).tensor_tensor(
                    Hl[:, k, :], tmp[:, k % 2, :], Hh[:, k, :].bitcast(F32), ALU.subtract))
                marks.append(free[k % 2])
            return marks

        def add_normed(M, col, ready_r):
            prev = [None, None]
            for k in range(KT):
                c = col + k
                m = V.mark(V.on(ready_r, prev[k % 2]).scalar_tensor_tensor(
                    out=M[:, k, :], in0=M[:, k, :], scalar=cols[:, c:c + 1], in1=PS[:, 2, :],
                    op0=ALU.mult, op1=ALU.mult))
                m = V.mark(V.on(m).tensor_tensor(X[:, k, :], X[:, k, :], M[:, k, :], ALU.add))
                m = squares(k, X[:, k, :], m)
            return m

        m_small = loaded_small.now()
        m0 = V.mark(nc.vector.memset(ones[:], 1.0))
        m0 = V.mark(nc.vector.memset(half[:], -0.5))
        run_marks = None
        for n in range(2):
            split_unit()
        for k in range(KT):
            m = squares(k, X[:, k, :], loaded_x[k // 4].now())
        T.on(m0, m_small)
        V.on(m_small)
        G.on(m0)
        m = inverse_rms(m)
        h_ready = normed_input(C_MIXPRE, m, None)

        def attend(a, qt, b, Q, K, scale, bias, ready, bufs, banks):
            nk = (qt + 1) * P
            r0 = HD * a
            SBs, Ps, nmax, rsum, rinv, free = bufs
            s_ps = PS[:, banks["S"][b % 2], 0:nk]
            m_s = T.mark(T.on(*ready, free["S"][b % 2]).matmul(
                s_ps, Q[r0:r0 + HD, qt * P:(qt + 1) * P], K[r0:r0 + HD, 0:nk],
                start=True, stop=True))
            m_b = V.mark(V.on(m_s, free["SB"][b % 2]).scalar_tensor_tensor(
                out=SBs[:, b % 2, 0:nk], in0=s_ps, scalar=scale, in1=bias, op0=ALU.mult, op1=ALU.add))
            free["S"][b % 2] = m_b
            m_x = V.mark(V.on(m_b).tensor_reduce(nmax[:, b:b + 1], SBs[:, b % 2, 0:nk], AXX, ALU.max,
                                                 negate=True))
            m_p = A.mark(A.on(m_x, free["P"][b % 2]).activation(
                Ps[:, b % 2, 0:nk], SBs[:, b % 2, 0:nk], ACT.Exp, bias=nmax[:, b:b + 1], scale=1.0,
                accum_out=rsum[:, b:b + 1]))
            free["SB"][b % 2] = m_p
            m_r = V.mark(V.on(m_p).reciprocal(rinv[:, b:b + 1], rsum[:, b:b + 1]))
            return m_p, m_r

        def turn_weights(qt, j, src, m_src, PTs, free, banks):
            nk = (qt + 1) * P
            bank = banks["PT"][j % 2]
            for kt in range(qt + 1):
                ins = T.on(m_src, free["PT"][j % 2]).transpose(
                    PS[:, bank, kt * P:(kt + 1) * P], src[:, kt * P:(kt + 1) * P], ident[:])
            m_read = T.mark(ins)
            m_t = A.mark(A.on(m_read, free["PTs"][j % 2]).activation(
                PTs[:, j % 2, 0:nk], PS[:, bank, 0:nk], ACT.Copy))
            free["PT"][j % 2] = m_t
            return m_read, m_t

        def apply_weights(qt, j, m_t, PTs, values, width, free, banks):
            for kt in range(qt + 1):
                ins = T.on(m_t, free["O"][j % 2]).matmul(
                    PS[:, banks["O"][j % 2], 0:width], PTs[:, j % 2, kt * P:(kt + 1) * P],
                    values(kt), start=(kt == 0), stop=(kt == qt))
            m = T.mark(ins)
            free["PTs"][j % 2] = m
            return m

        class Fill:
            gens = []

        def fill(steps):
            while steps > 0 and Fill.gens:
                try:
                    next(Fill.gens[0])
                    steps -= 1
                except StopIteration:
                    Fill.gens.pop(0)

        def fill_all():
            fill(1 << 30)

        b1 = ctx.enter_context(ExitStack())
        gates = sb(b1, "gates", [P, 16, S])
        U = sb(b1, "U", [P, 4, LEAD + S])
        AOh = sb(b1, "AOh", [P, 4, S], F32R)
        AOl = sb(b1, "AOl", [P, 4, S], F32R)
        att = ExitStack()
        relb = sb(att, "relb", [P, HEADS, S])
        Q2 = sb(att, "Q2", [P, S])
        K2 = sb(att, "K2", [P, S])
        V2 = sb(att, "V2", [P, S])
        Vt = sb(att, "Vt", [P, NT, P])
        SBs = sb(att, "SBs", [P, 2, S])
        Ps = sb(att, "Ps", [P, 2, S])
        PTs = sb(att, "PTs", [P, 2, S])
        Ot = sb(att, "Ot", [P, NT, P])
        nmax = sb(att, "nmax", [P, 8])
        rsum = sb(att, "rsum", [P, 8])
        rinv = sb(att, "rinv", [P, 8])

        rel_loaded = core.tally("rel_loaded", 16)
        rel_loaded.inc(nc.gpsimd.dma_start(relb[:], relb_in))
        m_relb = G.mark(G.on(rel_loaded.now()).memset(relb[0:CH, :, S - CH:S], NEG))
        m_u0 = G.mark(nc.gpsimd.memset(U[:, :, 0:LEAD], 0.0))

        def pair_body(i):
            start = [V.now(), A.now(), T.now(), G.now()]
            got = {}

            def to(name, dst):
                def evac(bank, done, freed):
                    freed.inc(A.on(done, *start).activation(dst, bank, ACT.Copy))
                    got[name] = freed.now()
                return evac

            def gate(col, dst):
                def evac(bank, done, freed):
                    freed.inc(A.on(done).activation(dst, bank, ACT.Identity,
                                                    bias=cols[:, bass.ds(col, 1)], scale=1.0))
                return evac

            def flat(tile, idx):
                return tile[:, bass.ds(idx, 1), :].rearrange("p a n -> p (a n)")

            hr = (lambda r: (h_ready[r],))
            run(unit(to("q", Q2[:]), ready=hr))
            run(unit(to("k", K2[:]), ready=hr))
            run(unit(to("v", V2[:]), ready=hr))
            Fill.gens = [unit(to("u", U[:, bass.ds(i, 1), LEAD:].rearrange("p a n -> p (a n)")))]
            Fill.gens += [unit(gate(C_BGATE + 2 * i + j, flat(gates, 2 * i + j))) for j in range(2)]
            Fill.gens += [unit(gate(C_BGATE + 8 + 2 * i + j, flat(gates, 8 + 2 * i + j)))
                          for j in range(2)]
            fill(4)
            for t in range(NT):
                ins = T.on(got["v"], *start).transpose(PS[:, 4, t * P:(t + 1) * P],
                                                       V2[:, t * P:(t + 1) * P], ident[:])
            m = T.mark(ins)
            m_v = V.mark(V.on(m).tensor_copy(Vt[:].rearrange("p t n -> p (t n)"), PS[:, 4, :]))
            free = {"S": [None] * 2, "SB": [None] * 2, "P": [None] * 2, "PT": [m_v, None],
                    "PTs": [None] * 2, "O": [None] * 2}
            banks = {"S": (2, 3), "PT": (4, 5), "O": (6, 7)}
            bufs = (SBs, Ps, nmax, rsum, rinv, free)
            blocks = [(a, qt) for a in range(2) for qt in (3, 2, 1, 0)]

            def turned(a, qt, b, m_p, m_r):
                free["P"][b % 2], m_t = turn_weights(qt, b, Ps[:, b % 2, :], m_p, PTs, free, banks)
                return (a, qt, b, m_t, m_r)

            def applied(a, qt, b, m_t, m_r):
                m = apply_weights(qt, b, m_t, PTs, lambda kt: Vt[:, kt, HD * a:HD * a + HD], HD,
                                  free, banks)
                free["O"][b % 2] = V.mark(V.on(m, m_r).tensor_scalar(
                    Ot[:, qt, HD * a:HD * a + HD], PS[:, 6 + b % 2, 0:HD], rinv[:, b:b + 1], None,
                    ALU.mult))
                return free["O"][b % 2]

            to_turn = to_apply = None
            for b in range(len(blocks) + 2):
                scored = got_turned = None
                if b < len(blocks):
                    a, qt = blocks[b]
                    off = i * (2 * S) + (a * S + (NT - 1 - qt) * P)
                    bias = relb[:].rearrange("p h n -> p (h n)")[:, bass.ds(off, (qt + 1) * P)]
                    scored = (a, qt, b, *attend(a, qt, b, Q2, K2, HD ** -0.5, bias,
                                                (got["q"], got["k"]), bufs, banks))
                fill(3)
                if to_turn:
                    got_turned = turned(*to_turn)
                fill(1)
                if to_apply:
                    m_o = applied(*to_apply)
                to_turn, to_apply = scored, got_turned
            m = None
            fill(3)
            for t in range(NT):
                ins = T.on(m_o, free["PT"][0]).transpose(PS[:, 4, t * P:(t + 1) * P], Ot[:, t, :],
                                                         ident[:])
            m = T.mark(ins)
            ah = flat(AOh, i)
            m = A.mark(A.on(m).activation(ah, PS[:, 4, :], ACT.Copy))
            V.mark(V.on(m).tensor_tensor(flat(AOl, i), PS[:, 4, :], ah.bitcast(F32), ALU.subtract))
            fill_all()

        def dense_loop(turns, units, groups, own, body):
            per = {q.tally: n for q, n in zip((V, A, T, G), own) if n}
            per.update({t: 16 * units // RING for t in landed})
            per.update({rounded: units, split: units, used: units})
            per.update({t: groups // 2 for t in bank_free})
            core.loop(turns, per, body, COMPUTE)
            Dense.unit += (turns - 1) * units
            Dense.ahead += (turns - 1) * units
            Dense.group += (turns - 1) * groups

        V.on(m_relb, m0)
        A.on(m_u0)
        T.on(m_small)
        dense_loop(PAIRS, BODY, BODY, (34, 17, 26, 0), pair_body)
        att.close()

        pool = ExitStack()
        W = LEAD + S
        sums = sb(pool, "sums", [P, 2, W])
        pooled = sb(pool, "pooled", [P, 4, S])
        wgrp = sb(pool, "wgrp", [P, 4, P])
        edge = sb(pool, "edge", [P, 4, LEAD])
        PLh = sb(pool, "PLh", [P, 4, S], F32R)
        PLl = sb(pool, "PLl", [P, 4, S], F32R)
        all_done = [V.now(), A.now(), T.now(), G.now()]
        pool_loaded = core.tally("pool_loaded", 16)
        pool_loaded.inc(G.on(*all_done).dma_start(wgrp[:], wgrp_in))
        pool_loaded.inc(nc.gpsimd.dma_start(edge[:], edge_in))
        m_gates = A.mark(A.on(*all_done, *[t.now() for t in bank_free]).activation(
            gates[:], gates[:], ACT.Sigmoid))
        m_z = G.mark(nc.gpsimd.memset(sums[:, :, 0:LEAD], 0.0))
        V.on(*all_done, *[t.now() for t in bank_free])
        m_pool = []
        m = m_z
        for g, w in enumerate(WINDOWS):
            src, step, j = U[:, g, :], 1, 0
            while step < w:
                dst = sums[:, j, :]
                m = V.mark(V.on(m).tensor_tensor(dst[:, LEAD:], src[:, LEAD:],
                                                 src[:, LEAD - step:W - step], ALU.add))
                src, step, j = dst, 2 * step, 1 - j
            m2 = V.mark(V.on(m).scalar_tensor_tensor(
                out=pooled[:, g, :], in0=src[:, LEAD:], scalar=1.0 / w, in1=U[:, g, LEAD:],
                op0=ALU.mult, op1=ALU.subtract))
            m3 = V.mark(V.on(pool_loaded.now(), m2).tensor_tensor(
                pooled[:, g, 0:LEAD], src[:, LEAD:2 * LEAD], edge[:, g, :], ALU.mult))
            m = V.mark(V.on(m3).tensor_tensor(pooled[:, g, 0:LEAD], pooled[:, g, 0:LEAD],
                                              U[:, g, LEAD:2 * LEAD], ALU.subtract))
            mm = T.mark(T.on(m, pool_loaded.now(), all_done[1]).matmul(
                PS[:, 4 + g, :], wgrp[:, g, :], pooled[:, g, :], start=True, stop=True))
            m = V.mark(V.on(mm).tensor_scalar(pooled[:, g, :], PS[:, 4 + g, :],
                                              cols[:, C_PSCALE + g:C_PSCALE + g + 1], None, ALU.mult))
            ma = A.mark(A.on(m).activation(PLh[:, g, :], pooled[:, g, :], ACT.Copy))
            m = V.mark(V.on(ma).tensor_tensor(PLl[:, g, :], pooled[:, g, :],
                                              PLh[:, g, :].bitcast(F32), ALU.subtract))
        T.on(m)
        V.on(m_gates)

        def flat2(tile, idx):
            return tile[:, bass.ds(idx, 1), :].rearrange("p a n -> p (a n)")

        def split_into(dst_h, dst_l, idx, src, ready):
            m = A.mark(A.on(ready).activation(flat2(dst_h, idx), src, ACT.Copy))
            return V.mark(V.on(m).tensor_tensor(flat2(dst_l, idx), src,
                                                flat2(dst_h, idx).bitcast(F32), ALU.subtract))

        def mix_body(i):
            start = V.now()
            last = [start, start]
            for j in range(4):
                b = j % 2

                def evac(bank, done, freed):
                    m1 = V.mark(V.on(done, last[b]).tensor_tensor(
                        tmp[:, b, :], bank, flat2(gates, i * 4 + j), ALU.mult))
                    m2 = freed.inc(V.e.tensor_tensor(
                        sq[:, b, :], PS[:, 2 + b, :], flat2(gates, i * 4 + (8 + j)), ALU.mult))
                    m3 = V.mark(V.on(m1, m2).tensor_tensor(tmp[:, b, :], tmp[:, b, :], sq[:, b, :],
                                                           ALU.add))
                    last[b] = split_into(Hh, Hl, i * 4 + j, tmp[:, b, :], m3)
                run(unit(evac, rhs=(lambda k: AOh[:, k, :], lambda k: AOl[:, k, :]),
                         second=(PS[:, 2 + b, :], (lambda k: PLh[:, k, :], lambda k: PLl[:, k, :]))))
        dense_loop(2, 4, 4, (12, 4, 0, 0), mix_body)
        pool.close()

        ffn = ExitStack()

        def normed_out(M, groups, rhs, post_col):
            def body(i):
                squares.m = V.now()
                squares.free = [squares.m, squares.m]
                for j, ks in enumerate(groups):
                    def evac(bank, done, freed):
                        dst = flat2(M, i * len(groups) + j)
                        m = freed.inc(A.on(done).activation(dst, bank, ACT.Copy))
                        squares(1 + j, dst, m)
                    for n, nk in enumerate(ks):
                        run(unit(evac, rhs=rhs, nk=nk, k0=KT * n,
                                 group=(n == 0, n == len(ks) - 1)))
            squares.m = V.mark(V.e.memset(ssum[:], 0.0))
            n = len(groups)
            dense_loop(KT // n, sum(len(g) for g in groups), n, (n, n, 0, 0), body)
            squares.m = V.now()
            squares.free = [squares.m, squares.m]
            return inverse_rms(squares.m)

        b1.close()
        M1 = sb(ffn, "M1", [P, KT, S])
        T.on(V.now())
        A.on(V.now())
        m = normed_out(M1, [[KT]] * 4, None, None)
        m = add_normed(M1, C_MIXPOST, m)
        m = inverse_rms(m)
        h_ready = normed_input(C_FFNPRE, m, None)
        ffn.close()

        ffn = ExitStack()
        Ah = sb(ffn, "Ah", [P, FT, S], F32R)
        Al = sb(ffn, "Al", [P, FT, S], F32R)
        A.on(V.now())

        ffn_up = ExitStack()
        conv = sb(ffn_up, "conv", [P, 2, 2, S])

        def up_body(i):
            start_v, start_a = V.now(), A.now()

            def c4(j, tap):
                return cols[:, bass.ds(C_CONV + i * 16 + (4 * j + tap), 1)]

            later = []
            for j in range(4):
                def evac(bank, done, freed, j=j):
                    c = conv[:, j // 2, j % 2, :]
                    m = A.mark(A.on(done, start_v, start_a).activation(
                        c, bank, ACT.Identity, bias=c4(j, 3), scale=c4(j, 2)))
                    m = V.mark(V.on(m).scalar_tensor_tensor(
                        out=c[:, 1:], in0=bank[:, 0:S - 1], scalar=c4(j, 1), in1=c[:, 1:],
                        op0=ALU.mult, op1=ALU.add))
                    m = freed.inc(V.on(m).scalar_tensor_tensor(
                        out=c[:, 2:], in0=bank[:, 0:S - 2], scalar=c4(j, 0), in1=c[:, 2:],
                        op0=ALU.mult, op1=ALU.add))
                    while later:
                        later.pop(0)()
                    if j % 2:
                        def finish(m=m, v=conv[:, j // 2, 0, :], c=c, j=j):
                            m = A.mark(A.on(m).activation(c, c, ACT.Gelu_apprx_tanh))
                            m = V.mark(V.on(m).tensor_tensor(v, v, c, ALU.mult))
                            split_into(Ah, Al, i * 2 + j // 2, v, m)
                        later.append(finish)
                run(unit(evac, ready=lambda r: (h_ready[r],)))
            while later:
                later.pop(0)()
        dense_loop(FT // 2, 4, 4, (8, 8, 0, 0), up_body)
        ffn_up.close()
        T.on(V.now())
        M2 = nc.alloc_sbuf_tensor_at("M2", [P, KT, S], F32, offset=h_place)
        A.on(V.now())
        m = normed_out(M2, [[KT, KT, FT - 2 * KT]] * 4,
                       (lambda k: Ah[:, k, :], lambda k: Al[:, k, :]), None)
        m = add_normed(M2, C_FFNPOST, m)
        m = inverse_rms(m)
        h_ready = normed_input(C_NORM2, m, None)
        ffn.close()

        if debug == "x1":
            stored = core.tally("stored", 16)
            A.on(landed[2].at(480), landed[3].at(480))
            stored.inc(A.on(V.now()).dma_start(out, X[:]))
            A.on(stored.now())
            return

        b2 = ctx.enter_context(ExitStack())
        mats = sb(b2, "mats", [P, N_MATS - 1, P])
        rope = sb(b2, "rope", [P, 3, S])
        rows = sb(b2, "rows", [P, N_ROWS])
        ba_w = sb(b2, "ba_w", [P, KT * 2 * GH])
        ba_h = sb(b2, "ba_h", [P, KT * 2 * GH], F32R)
        ba_l = sb(b2, "ba_l", [P, KT * 2 * GH], F32R)
        O = sb(b2, "O", [P, 2 * GH, S])
        ffn_done = [V.now(), A.now(), T.now(), used.at(Dense.unit + RING)]
        b2_loaded = core.tally("b2_loaded", 16)
        G.on(*ffn_done)
        for dst, src in ((mats, mats_in[:, 1:, :]), (rope, rope_in), (rows, rows_in)):
            b2_loaded.inc(nc.gpsimd.dma_start(dst[:], src))
        b2_loaded.inc(nc.gpsimd.dma_start(ba_w[:], w_ba.rearrange("p k n -> p (k n)")))

        def mat(k):
            return mats[:, k - 1, :]

        def over_tiles(ap):
            return ap.unsqueeze(1).to_broadcast([P, NT, P])

        def tiles(ap):
            return ap.rearrange("p (t n) -> p t n", t=NT)

        def over_cols(ap, n=P):
            return ap.unsqueeze(2).to_broadcast([P, ap.shape[1], n])

        glog = sb(b2, "glog", [P, GH, NT])
        gcum = sb(b2, "gcum", [P, GH, NT])
        beta = sb(b2, "beta", [P, GH, NT])
        beta_eg = sb(b2, "beta_eg", [P, GH, NT])
        to_end = sb(b2, "to_end", [P, GH, NT])
        chunk_decay = sb(b2, "chunk_decay", [P, GH, 2 * NT])
        small = sb(b2, "small", [P, 4, GH * NT])
        neg_lam = sb(b2, "neg_lam", [P, 1])
        subln = sb(b2, "subln", [P, 1])
        lam = sb(b2, "lam", [P, 4])
        lam_prod = sb(b2, "lam_prod", [P, 2, HD])

        lv = rows[:, R_LAM:].rearrange("p (a b d) -> p a b d", a=2, b=2)
        V.on(b2_loaded.now(), *ffn_done)
        A.on(b2_loaded.now(), *ffn_done)
        T.on(b2_loaded.now(), *ffn_done)
        m = V.mark(V.e.tensor_tensor(lam_prod[:], lv[:, :, 0, :], lv[:, :, 1, :], ALU.mult))
        m = V.mark(V.on(m).tensor_reduce(lam[:, 0:2], lam_prod[:], AXX, ALU.add))
        m = A.mark(A.on(m).activation(lam[:, 2:4], lam[:, 0:2], ACT.Exp))
        m = V.mark(V.on(m).tensor_tensor(neg_lam[:], lam[:, 3:4], lam[:, 2:3], ALU.subtract))
        m = V.mark(V.on(m).tensor_scalar(neg_lam[:], neg_lam[:], -LAM_INIT, None, ALU.add))
        V.mark(V.e.tensor_scalar(subln[:], cols[:, C_SUBLN:C_SUBLN + 1], 1.0 - LAM_INIT, None,
                                 ALU.mult))

        m = A.mark(A.e.activation(ba_h[:], ba_w[:], ACT.Copy))
        m = V.mark(V.on(m).tensor_tensor(ba_l[:], ba_w[:], ba_h[:].bitcast(F32), ALU.subtract))
        for t in range(NT):
            for k in range(KT):
                tok, w = slice(t * P, (t + 1) * P), slice(2 * GH * k, 2 * GH * (k + 1))
                T.on(m, h_ready[k])
                for n, (a, b) in enumerate(((Hh, ba_h), (Hl, ba_h), (Hh, ba_l))):
                    ins = T.e.matmul(PS[:, 2, 2 * GH * t:2 * GH * (t + 1)], a[:, k, tok], b[:, w],
                                     start=(k == 0 and n == 0), stop=(k == KT - 1 and n == 2))
        m_ba = T.mark(ins)
        ba = PS[:, 2, 0:2 * GH * NT].rearrange("p (t n) -> p n t", t=NT)
        sm = [small[:, n, :].rearrange("p (h t) -> p h t", t=NT) for n in range(4)]
        m = A.mark(A.on(m_ba).activation(sm[0], ba[:, 0:GH, :], ACT.Exp, scale=-1.0))
        m = V.mark(V.on(m).tensor_scalar(sm[0], sm[0], 1.0, None, ALU.add))
        m_beta = V.mark(V.on(m).reciprocal(beta[:], sm[0]))
        m_y = V.mark(V.on(m_ba).tensor_tensor(
            sm[1], ba[:, GH:2 * GH, :], over_cols(rows[:, R_DT:R_DT + GH], NT), ALU.add))
        m = V.mark(V.on(m_y).tensor_scalar(sm[2], sm[1], -1.0, None, ALU.mult))
        m = V.mark(V.on(m).tensor_tensor(sm[2], sm[1], sm[2], ALU.max))
        m = A.mark(A.on(m).activation(sm[2], sm[2], ACT.Exp, scale=-1.0))
        m = V.mark(V.on(m).tensor_scalar(sm[2], sm[2], 1.0, None, ALU.add))
        m = A.mark(A.on(m).activation(sm[2], sm[2], ACT.Ln))
        m = V.mark(V.on(m).scalar_tensor_tensor(out=small[:, 2, :], in0=small[:, 1, :], scalar=0.0,
                                                in1=small[:, 2, :], op0=ALU.max, op1=ALU.add))
        m2 = A.mark(A.e.activation(lam[:, 0:GH], rows[:, R_ALOG:R_ALOG + GH], ACT.Exp))
        m = V.mark(V.on(m, m2).tensor_tensor(sm[2], sm[2], over_cols(lam[:, 0:GH], NT), ALU.mult))
        m_g = V.mark(V.on(m).tensor_scalar(glog[:], sm[2], -1.0, None, ALU.mult))
        gl2 = glog[:].rearrange("p h t -> p (h t)")
        n16 = GH * NT
        T.on(m_g).matmul(PS[:, 3, 0:n16], mat(K_UPPER), gl2, start=True, stop=True)
        T.e.matmul(PS[:, 3, n16:2 * n16], mat(K_SAME), gl2, start=True, stop=True)
        for n in range(n16):
            ins = T.e.matmul(PS[:, 3, 2 * n16 + 2 * n:2 * n16 + 2 * n + 2],
                             gl2[:, n:n + 1].to_broadcast([P, P]), mat(K_SAME)[:, 0:P:CH],
                             start=True, stop=True)
        m = T.mark(ins)
        m_gc = V.mark(V.on(m).tensor_copy(gcum[:].rearrange("p h t -> p (h t)"), PS[:, 3, 0:n16]))
        m_d = V.mark(V.on(m_gc).tensor_tensor(small[:, 0, :], PS[:, 3, n16:2 * n16],
                                              gcum[:].rearrange("p h t -> p (h t)"), ALU.subtract))
        A.mark(A.on(m_d).activation(to_end[:].rearrange("p h t -> p (h t)"), small[:, 0, :], ACT.Exp))
        A.mark(A.e.activation(chunk_decay[:].rearrange("p h t -> p (h t)"),
                              PS[:, 3, 2 * n16:4 * n16], ACT.Exp))
        m = A.mark(A.e.activation(small[:, 1, :], gcum[:].rearrange("p h t -> p (h t)"), ACT.Exp))
        m = V.mark(V.on(m, m_beta).tensor_tensor(
            beta_eg[:].rearrange("p h t -> p (h t)"), beta[:].rearrange("p h t -> p (h t)"),
            small[:, 1, :], ALU.mult))

        hb = ExitStack()
        names = ("Vb", "DT", "LT", "Lo", "LmT", "Ti", "TiT", "Y",
                 "QG", "U", "Wt", "Kd", "AT", "VN", "Oa",
                 "Qb", "Kr", "Vd", "Vdt", "Od", "Wd")
        B = {n: sb(hb, "head_" + n, [P, S]) for n in names}
        B["Bm"] = B["Lm"] = B["Y"]
        B["Kb"] = B["Lo"]
        C3 = sb(hb, "C3", [P, 3, S])
        CQ, CK, CV = (C3[:, n, :] for n in range(3))
        EG = ssum
        Zr = sb(hb, "Zr", [P, 2, S])
        Zs = sb(hb, "Zs", [P, 2, S])
        SB2 = sb(hb, "SB2", [P, 2, S])
        P2 = sb(hb, "P2", [P, 2, S])
        St = sb(hb, "St", [P, P])
        gs = sb(hb, "gs", [P, 2, NT])
        rqk = sb(hb, "rqk", [P, 2 * NT])
        rq_scan = sb(hb, "rq_scan", [P, NT])
        rqk_b = sb(hb, "rqk_b", [P, 2, NT, 2])
        r_o = sb(hb, "r_o", [P, 2, NT])
        nmax2 = sb(hb, "nmax2", [P, 8])
        rsum2 = sb(hb, "rsum2", [P, 8])
        rinv2 = sb(hb, "rinv2", [P, 8])
        neg_r = sb(hb, "neg_r", [P, 8])
        B_SCAN, B_S, B_PT, B_A = 2, (3, 4), 5, (6, 7)

        def head(tile, i):
            return tile[:, bass.ds(i, 1), :].rearrange("p a n -> p (a n)")

        def row_of(scalars, bank, ready, rhs=None):
            for t in range(NT):
                ins = T.on(*ready).matmul(PS[:, bank, t * P:(t + 1) * P],
                                          scalars[:, t:t + 1].to_broadcast([P, P]),
                                          ident[:] if rhs is None else rhs, start=True, stop=True)
            return T.mark(ins)

        def per_tile(out, lhs, rhs, ready):
            for t in range(NT):
                ins = T.on(*ready).matmul(out(t), lhs(t), rhs(t), start=True, stop=True)
            return T.mark(ins)

        def tile_of(ap):
            return lambda t: ap[:, t * P:(t + 1) * P]

        def bank_tile(bank):
            return lambda t: PS[:, bank, t * P:(t + 1) * P]

        def turn_tiles(bank, src, ready):
            for t in range(NT):
                tok = slice(t * P, (t + 1) * P)
                ins = T.on(*ready).transpose(PS[:, bank, tok], src[:, tok], ident[:])
            return T.mark(ins)

        def blocks(ap, size, odd):
            return ap.rearrange("p (g two b) -> p g two b", two=2, b=size)[:, :, odd, :]

        class Head:

            def __init__(self):
                self.start = [q.now() for q in (V, A, T, G, *bank_free)]
                self.scan_done = self.diff_done = self.v_turned = None

        def conv_unit(st, i, j):
            c = C3[:, j, :]

            def tap(n):
                return cols[:, bass.ds(C_CONV2 + i * 12 + (4 * j + n), 1)]

            def evac(bank, done, freed):
                m = A.mark(A.on_apart(done, *st.start).activation(c, bank, ACT.Identity,
                                                                  bias=0.0, scale=tap(3)))
                for n in (2, 1):
                    m = V.mark(V.on(m, *st.start).scalar_tensor_tensor(
                        out=c[:, 3 - n:], in0=bank[:, 0:S - 3 + n], scalar=tap(n),
                        in1=c[:, 3 - n:], op0=ALU.mult, op1=ALU.add))
                st.conv = freed.inc(V.on(m).scalar_tensor_tensor(
                    out=c[:, 3:], in0=bank[:, 0:S - 3], scalar=tap(0),
                    in1=c[:, 3:], op0=ALU.mult, op1=ALU.add))
                st.convs.append(st.conv)
            return unit(evac, ready=st.h_ready)

        def z_unit(st, branch):
            def evac(bank, done, freed):
                freed.inc(A.on(done, st.zs).activation(Zr[:, branch, :], bank, ACT.Copy))
            return unit(evac, ready=st.h_ready)

        def qk_unit(st, name, j, col):
            def evac(bank, done, freed):
                A.on(done, *st.start, st.diff_done, st.sq_read).activation(
                    B[name][:], bank, ACT.Copy, scale=cols[:, col:col + 1])
                st.sq2[j] = freed.inc(A.e.activation(sq[:, j, :], bank, ACT.Square))
            return unit(evac, ready=st.h_ready)

        def v_unit(st):
            def evac(bank, done, freed):
                freed.inc(A.on(done, *st.start, st.v_turned).activation(B["Vd"][:], bank, ACT.Copy))
            return unit(evac, ready=st.h_ready)

        def prep(st, i, gates_too):
            b6, b7 = PS[:, B_A[0], :], PS[:, B_A[1], :]
            V.on(*st.start).tensor_copy(gs[:, 0, :], head(glog, i))
            m_gs = V.mark(V.e.tensor_copy(gs[:, 1, :], head(beta, i)))
            m_c = A.mark(A.on(*st.convs, *st.start).activation(C3[:], C3[:], ACT.Silu))
            if gates_too:
                st.zs = A.mark(A.e.activation(Zs[:], Zr[:], ACT.Silu))
            m_grow = row_of(gs[:, 0, :], B_A[0], (m_gs, *st.start), rhs=mat(K_UPPER))
            m_brow = row_of(gs[:, 1, :], B_A[1], (m_gs,))
            yield
            m_sq = [A.mark(A.on(m_c).activation(sq[:, j, :], c, ACT.Square))
                    for j, c in enumerate((CQ, CK))]
            m_d = V.mark(V.on(m_grow).tensor_tensor(tiles(B["DT"][:]), tiles(b6),
                                                    over_cols(head(gcum, i)), ALU.subtract))
            m_bm = V.mark(V.on(m_brow).tensor_tensor(tiles(B["Bm"][:]), tiles(b7),
                                                     over_tiles(mat(K_STRICT_T)), ALU.mult))
            m_dt = V.mark(V.on(m_d).tensor_tensor(tiles(B["DT"][:]), tiles(B["DT"][:]),
                                                over_tiles(mat(K_NEG_T)), ALU.add))
            m_eg = A.mark(A.on(m_d).activation(EG[:], b6, ACT.Exp))
            yield
            for j in range(2):
                for t in range(NT):
                    ins = T.on(m_sq[1 - j], m_bm).matmul(
                        b7[:, NT * j + t:NT * j + t + 1], sq[:, 1 - j, t * P:(t + 1) * P], ones[:],
                        start=True, stop=True)
            st.sq_read = T.mark(ins)
            m_dt = A.mark(A.on(m_dt).activation(B["DT"][:], B["DT"][:], ACT.Exp))
            yield
            m_n = V.mark(V.on(st.sq_read).tensor_scalar(rqk[:], b7[:, 0:2 * NT], EPS, None, ALU.add))
            yield
            m_rk = G.mark(G.on(m_n).tensor_tensor(rqk[:, 0:NT], rqk[:, 0:NT], half[:, 0:NT],
                                                  ALU.pow))
            m_rq = G.mark(G.e.tensor_tensor(rqk[:, NT:], rqk[:, NT:], half[:, 0:NT], ALU.pow))
            m_vt = turn_tiles(B_A[1], CV, (m_c, m_n))
            yield
            m_kr = row_of(rqk[:, 0:NT], B_A[0], (m_rk, m_eg, m_dt))
            m_vb = V.mark(V.on(m_vt).tensor_tensor(tiles(B["Vb"][:]), tiles(b7),
                                                   over_cols(head(beta, i)), ALU.mult))
            yield
            m_kn = V.mark(V.on(m_kr).tensor_tensor(CK, CK, b6, ALU.mult))
            yield
            m_kk = per_tile(bank_tile(B_A[1]), tile_of(CK), tile_of(CK), (m_kn, m_vb))
            yield
            m = V.mark(V.on(m_kk, m_dt).tensor_tensor(B["LT"][:], b7, B["DT"][:], ALU.mult))
            m_lt = V.mark(V.on(m).tensor_tensor(B["LT"][:], B["LT"][:], B["Bm"][:], ALU.mult))
            yield
            m = turn_tiles(B_A[0], B["LT"][:], (m_lt,))

            def level_mask(lv, read):
                return G.mark(G.on(m_lt, *read).tensor_tensor(
                    tiles(B["LmT"][:]), tiles(B["LT"][:]), over_tiles(mat(K_LEVEL + 1 + lv)),
                    ALU.mult))
            m_lm = level_mask(0, ())
            yield
            m_lo = A.mark(A.on(m).activation(B["Lo"][:], b6, ACT.Copy))
            m_tt = V.mark(V.on(m_lm).tensor_tensor(tiles(B["TiT"][:]), over_tiles(ident[:]),
                                                   tiles(B["LmT"][:]), ALU.subtract))
            yield
            m_l0 = G.mark(G.on(m_lo).tensor_tensor(tiles(B["Lm"][:]), tiles(B["Lo"][:]),
                                                   over_tiles(mat(K_LEVEL)), ALU.mult))
            m_lm = level_mask(1, (m_tt,))
            yield
            m_ti = V.mark(V.on(m_l0).tensor_tensor(tiles(B["Ti"][:]), over_tiles(ident[:]),
                                                   tiles(B["Lm"][:]), ALU.subtract))
            yield
            for lv in range(1, N_LEVELS):
                size = 1 << lv
                m_y = per_tile(bank_tile(B_A[0]), tile_of(B["LmT"]), tile_of(B["Ti"]),
                               (m_lm, m_ti, m_tt, m_lo))
                yield
                m_ya = A.mark(A.on(m_y).activation(B["Y"][:], b6, ACT.Copy))
                if lv + 1 < N_LEVELS:
                    m_lm = level_mask(lv + 1, (m_y,))
                yield
                H = P // 2
                if lv + 1 < N_LEVELS:
                    m_t = per_tile(lambda t: b7[:, t * H:(t + 1) * H], tile_of(B["TiT"]),
                                   lambda t: blocks(tile_of(B["Y"])(t), size, 0), (m_ya, m_lt))
                m_t2 = per_tile(lambda t: b7[:, 2 * P + t * H:2 * P + (t + 1) * H],
                                tile_of(B["Y"]), lambda t: blocks(tile_of(B["TiT"])(t), size, 1),
                                (m_ya, m_lt))
                yield
                for name, odd, off in (("Ti", 0, 0), ("TiT", 1, 2 * P)):
                    if name == "Ti" and lv + 1 == N_LEVELS:
                        continue
                    v = blocks(B[name][:], size, odd)
                    m_tt = V.mark(V.on(m_t2).tensor_tensor(
                        v, v, b7[:, off:off + 2 * P].rearrange("p (g b) -> p g b", b=size),
                        ALU.subtract))
                m_ti = m_tt
                yield
            while st.scanning:
                yield
            free = (*st.start, *st.scan_done) if st.scan_done else st.start
            m_kt = turn_tiles(B_A[0], CK, (m_ya, m_kn))
            m_qk = per_tile(bank_tile(B_A[1]), tile_of(CK), tile_of(CQ), (m_tt,))
            yield
            m_kb = V.mark(V.on(m_kt, m_l0, *free).tensor_tensor(
                tiles(B["Kb"][:]), tiles(b6), over_cols(head(beta_eg, i)), ALU.mult))
            m_kd = V.mark(V.e.tensor_tensor(tiles(B["Kd"][:]), tiles(b6),
                                            over_cols(head(to_end, i)), ALU.mult))
            m_at = V.mark(V.on(m_qk).tensor_tensor(B["AT"][:], b7, B["DT"][:], ALU.mult))
            G.mark(G.on(m_c, m_eg, m_qk, *free).tensor_tensor(B["QG"][:], CQ, EG[:], ALU.mult))
            V.mark(V.on(m_rq).tensor_scalar(rq_scan[:], rqk[:, NT:], P ** -0.5, None, ALU.mult))
            yield
            m_u = per_tile(bank_tile(B_A[0]), tile_of(B["TiT"]), tile_of(B["Vb"]), (m_kd,))
            m_w = per_tile(bank_tile(B_A[1]), tile_of(B["Kb"]), tile_of(B["TiT"]), (m_at,))
            yield
            m_u = A.mark(A.on(m_u, *free).activation(B["U"][:], b6, ACT.Copy))
            m_w = V.mark(V.on(m_w).tensor_copy(B["Wt"][:], b7))
            yield
            while None in st.sq2:
                yield
            for j in range(2):
                for t in range(NT):
                    ins = T.on(st.sq2[j], m_u).matmul(
                        b6[:, 8 * j + 2 * t:8 * j + 2 * t + 2],
                        sq[:, j, t * P:(t + 1) * P], mat(K_SAME)[:, 0:P:CH], start=True, stop=True)
            m = T.mark(ins)
            yield
            r2 = rqk_b[:].rearrange("p a t c -> p (a t c)")
            m = V.mark(V.on(m, *st.start).tensor_scalar(r2, b6[:, 0:16], 1.0 / HD, EPS, ALU.mult,
                                                        ALU.add))
            yield
            m = G.mark(G.on(m).tensor_tensor(r2, r2, half[:, 0:16], ALU.pow))
            yield
            V.mark(V.on(m).tensor_scalar(rqk_b[:, 0, :, :], rqk_b[:, 0, :, :], HD ** -0.5, None,
                                         ALU.mult))

        def out_norm(st, i, o, spare, branch, bank, m, eps, weight, ready):
            m_q = G.mark(G.on(m, *ready).tensor_tensor(spare[:], o[:], o[:], ALU.mult))
            r = r_o[:, branch, :]
            yield
            m_q = V.mark(V.on(m_q).tensor_reduce(r, tiles(spare[:]), AXX, ALU.add))
            m_q = V.mark(V.on(m_q).tensor_scalar(r, r, 1.0 / P, eps, ALU.mult, ALU.add))
            yield
            m_q = G.mark(G.on(m_q).tensor_tensor(r, r, half[:, 0:NT], ALU.pow))
            yield
            m_q = V.mark(V.on(m_q).tensor_tensor(tiles(o[:]), tiles(o[:]), over_cols(r), ALU.mult))
            yield
            m_q = turn_tiles(bank, o[:], (m_q,))
            yield
            while st.zs is None:
                yield
            V.mark(V.on(m_q, st.zs).scalar_tensor_tensor(
                out=head(O, i + GH * branch), in0=PS[:, bank, :], scalar=weight,
                in1=Zs[:, branch, :], op0=ALU.mult, op1=ALU.mult))

        def scan(st, i):
            bank = PS[:, B_SCAN, :]
            m_s = m_out = V.mark(V.on(*st.start).memset(St[:], 0.0))
            T.on(*st.start)
            for c in range(S // CH):
                t, r0 = c // 2, CH * (c % 2)
                rows_ = slice(r0, r0 + CH)
                own, tile_ = slice(t * P + r0, t * P + r0 + CH), slice(t * P, (t + 1) * P)
                m = T.mark(T.on(m_s, m_out).matmul(bank[rows_, 0:P], B["Wt"][:, own], St[:],
                                                   start=True, stop=True))
                yield
                m_v = V.mark(V.on(m).tensor_tensor(B["VN"][rows_, tile_], B["U"][rows_, tile_],
                                                   bank[rows_, 0:P], ALU.subtract))
                yield
                m = T.mark(T.on(m_v).matmul(bank[:, P:2 * P], B["Kd"][rows_, tile_],
                                            B["VN"][rows_, tile_], start=True, stop=True))
                T.e.matmul(bank[rows_, 2 * P:3 * P], B["QG"][:, own], St[:], start=True, stop=False)
                m = T.mark(T.e.matmul(bank[rows_, 2 * P:3 * P], B["AT"][rows_, own],
                                      B["VN"][rows_, tile_], start=False, stop=True))
                yield
                m_s = V.mark(V.on(m).scalar_tensor_tensor(
                    out=St[:], in0=St[:],
                    scalar=chunk_decay[:].rearrange("p h c -> p (h c)")[
                        :, bass.ds(i * (2 * NT) + c, 1)],
                    in1=bank[:, P:2 * P], op0=ALU.mult, op1=ALU.add))
                m_out = V.mark(V.e.tensor_scalar(B["Oa"][rows_, tile_], bank[rows_, 2 * P:3 * P],
                                                 rq_scan[rows_, t:t + 1], None, ALU.mult))
                yield
            st.scan_done = (m, m_out)
            st.scanning = False
            yield from out_norm(st, i, B["Oa"], B["VN"], 0, B_SCAN, m_out, EPS,
                                cols[:, C_GNORM:C_GNORM + 1], ())

        def diff(st, i):
            for t in range(NT):
                for c in range(2):
                    ins = T.on(*st.start).matmul(
                        PS[c * HD:(c + 1) * HD, B_S[0], t * P:(t + 1) * P],
                        rqk_b[:, 1, t, c:c + 1].to_broadcast([P, HD]), ident[:],
                        start=True, stop=True)
            m_k = T.mark(ins)
            m_r = {"Qb": T.mark(T.e.matmul(PS[:, B_S[1], :], mat(K_SWAP), B["Qb"][:],
                                           start=True, stop=True))}
            st.v_turned = turn_tiles(B_PT, B["Vd"][:], ())
            yield
            m_k = V.mark(V.on(m_k, *st.start).tensor_tensor(B["Kr"][:], B["Kr"][:],
                                                            PS[:, B_S[0], :], ALU.mult))
            m_v2 = A.mark(A.on(st.v_turned, *st.start).activation(B["Vdt"][:], PS[:, B_PT, :],
                                                                  ACT.Copy))
            yield
            m_r["Kr"] = T.mark(T.on(m_k).matmul(PS[:, B_S[0], :], mat(K_SWAP), B["Kr"][:],
                                                start=True, stop=True))
            ready, mts = [], []
            for j, name in ((0, "Qb"), (1, "Kr")):
                x = B[name][:]
                mt = V.mark(V.on(m_r[name], *st.start).tensor_tensor(
                    tmp[:, j, :], PS[:, B_S[1 - j], :], rope[:, 1, :], ALU.mult))
                mc = G.mark(G.on(m_r[name], *st.start).tensor_tensor(x, x, rope[:, 0, :], ALU.mult))
                yield
                ready.append(G.mark(G.on(mc, mt).tensor_tensor(x, x, tmp[:, j, :], ALU.add)))
                mts.append(mt)
                yield
            s_free = [mts[1], mts[0]]
            wd_free, pt_free, pts_free = None, m_v2, ready[1]
            before = None
            for n in range(NT + 1):
                qt = NT - 1 - n
                nk = (qt + 1) * P
                if n < NT:
                    m_s = []
                    for a in range(2):
                        r = slice(HD * a, HD * a + HD)
                        m_s.append(T.mark(T.on(*ready, s_free[a]).matmul(
                            PS[:, B_S[a], 0:nk], B["Qb"][r, qt * P:(qt + 1) * P], B["Kr"][r, 0:nk],
                            start=True, stop=True)))
                if before:
                    q_, m_wd = before
                    for kt in range(q_ + 1):
                        ins = T.on(m_wd, pt_free).transpose(
                            PS[:, B_PT, kt * P:(kt + 1) * P], B["Wd"][:, kt * P:(kt + 1) * P],
                            ident[:])
                    wd_free = T.mark(ins)
                yield
                if n < NT:
                    m_b, m_x = [], []
                    for a in range(2):
                        b = 2 * n + a
                        m_b.append(V.mark(V.on(m_s[a]).scalar_tensor_tensor(
                            out=SB2[:, a, 0:nk], in0=PS[:, B_S[a], 0:nk],
                            scalar=rqk_b[:, 0, qt, a:a + 1], in1=rope[:, 2, S - nk:],
                            op0=ALU.mult, op1=ALU.add)))
                        m_x.append(V.mark(V.on(m_b[a]).tensor_reduce(
                            nmax2[:, b:b + 1], SB2[:, a, 0:nk], AXX, ALU.max, negate=True)))
                    s_free = m_b
                if before:
                    m_pt = A.mark(A.on(wd_free, pts_free).activation(
                        tmp[:, 0, 0:(q_ + 1) * P], PS[:, B_PT, 0:(q_ + 1) * P], ACT.Copy))
                yield
                if n < NT:
                    m_p = []
                    for a in range(2):
                        b = 2 * n + a
                        m_p.append(A.mark(A.on(m_x[a]).activation(
                            P2[:, a, 0:nk], SB2[:, a, 0:nk], ACT.Exp, bias=nmax2[:, b:b + 1],
                            scale=1.0, accum_out=rsum2[:, b:b + 1])))
                if before:
                    for kt in range(q_ + 1):
                        ins = T.on(m_pt).matmul(
                            PS[:, B_PT, 0:P], tmp[:, 0, kt * P:(kt + 1) * P],
                            B["Vdt"][:, kt * P:(kt + 1) * P], start=(kt == 0), stop=(kt == q_))
                    pts_free = T.mark(ins)
                yield
                if n < NT:
                    b = 2 * n
                    m = V.mark(V.on(*m_p).reciprocal(rinv2[:, b:b + 2], rsum2[:, b:b + 2]))
                    m0 = V.mark(V.on(m).tensor_scalar(P2[:, 0, 0:nk], P2[:, 0, 0:nk],
                                                      rinv2[:, b:b + 1], None, ALU.mult))
                    m1 = V.mark(V.e.tensor_tensor(neg_r[:, b:b + 1], neg_lam[:],
                                                  rinv2[:, b + 1:b + 2], ALU.mult))
                    m_w = V.mark(V.on(m0, m1, wd_free).scalar_tensor_tensor(
                        out=B["Wd"][:, 0:nk], in0=P2[:, 1, 0:nk], scalar=neg_r[:, b:b + 1],
                        in1=P2[:, 0, 0:nk], op0=ALU.mult, op1=ALU.add))
                if before:
                    pt_free = m_od = A.mark(A.on(pts_free).activation(
                        B["Od"][:, q_ * P:(q_ + 1) * P], PS[:, B_PT, 0:P], ACT.Copy))
                before = (qt, m_w)
                yield
            st.diff_done = m_s[1]
            yield from out_norm(st, i, B["Od"], B["Wd"], 1, B_PT, m_od, SUB_EPS, subln[:, 0:1], ())

        class Rounds:

            def __init__(self, gens):
                self.gens = gens

            def __call__(self, steps):
                for g in list(self.gens):
                    try:
                        next(g)
                    except StopIteration:
                        self.gens.remove(g)
                fill(steps)

        def stages(i_a, i_b, h_mark):
            st = Head()
            st.convs, st.sq2, st.zs, st.sq_read = [], [None, None], None, None
            st.h_ready = h_mark
            st.scanning = i_b is not None
            rounds = Rounds([])
            if i_b is not None:
                rounds.gens = [scan(st, i_b), diff(st, i_b)]
                d = rounds.gens[1]
            if i_a is None:
                st.zs = A.mark(A.on(*st.start).activation(Zs[:], Zr[:], ACT.Silu))
            else:
                Fill.gens = [conv_unit(st, i_a, j) for j in range(3)]
                if i_b is None:
                    fill_all()
                while Fill.gens:
                    rounds(2)
                rounds.gens.insert(0, prep(st, i_a, i_b is not None))
                rounds(0)
                Fill.gens = [z_unit(st, 0), z_unit(st, 1)]
                while i_b is not None and d in rounds.gens and st.diff_done is None:
                    rounds(1)
                Fill.gens += [qk_unit(st, "Kr", 1, C_KNORM), qk_unit(st, "Qb", 0, C_QNORM),
                              v_unit(st)]
                while Fill.gens:
                    rounds(1)
            while rounds.gens:
                rounds(0)

        T.on(m_beta, V.now(), A.now())
        A.on(V.now())
        G.on(V.now(), A.now())
        stages(0, None, lambda r: (h_ready[r],))

        def next_head(i):
            stages(i + 1, i, None)
        dense_loop(GH - 1, BODY, BODY, PER2, next_head)
        stages(None, GH - 1, None)
        hb.close()

        free = [None, None]
        h_ready = []
        last = (V.now(), T.now(), A.now())
        for k in range(2 * GH):
            m = A.mark(A.on(*last).activation(Hh[:, k, :], O[:, k, :], ACT.Copy))
            h_ready.append(V.mark(V.on(m).tensor_tensor(
                Hl[:, k, :], O[:, k, :], Hh[:, k, :].bitcast(F32), ALU.subtract)))
        stored = core.tally("stored", 16)
        for k in range(KT):
            def evac(bank, done, freed, k=k):
                m = freed.inc(V.on(done).tensor_tensor(X[:, k, :], X[:, k, :], bank, ALU.add))
                stored.inc(A.on(m).dma_start(out[:, k, :], X[:, k, :]))
            run(unit(evac, ready=lambda r: (h_ready[r],)))
        A.on(stored.now())


def _units(np, w):
    k, n = w.shape
    return w.reshape(k // P, P, n // P, P).transpose(2, 1, 0, 3)


def _layout(np, inp):
    w1 = _units(np, inp["w_in"][0])
    order = []
    for h in range(PAIRS):
        order += [h, 4 + h, 8 + h, 12 + h, 16 + 2 * h, 17 + 2 * h, 24 + 2 * h, 25 + 2 * h]
    p1 = w1[order]
    mix = np.concatenate([_units(np, inp["w_attn_out"][0]), _units(np, inp["w_pool_out"][0])], axis=2)
    wo = _units(np, inp["w_o"][0])
    up = _units(np, inp["w_up"][0])
    up = up.reshape(2, FT, P, KT, P).transpose(1, 0, 2, 3, 4).reshape(2 * FT, P, KT, P)
    down = _units(np, inp["w_down"][0])
    down = np.concatenate([down, np.zeros((KT, P, 24 - FT, P), np.float32)], axis=2)
    down = down.reshape(KT, P, 3, KT, P).transpose(0, 2, 1, 3, 4).reshape(24, P, KT, P)
    w2 = inp["w_in_2"][0]
    n = 4 * GH * P
    big = np.concatenate([w2[:, :n], w2[:, n + 2 * GH:]], axis=1)
    p2 = _units(np, big).reshape(8, GH, P, KT, P)[[0, 1, 2, 3, 7, 5, 4, 6]]
    p2 = p2.transpose(1, 0, 2, 3, 4).reshape(32, P, KT, P)
    wout = _units(np, inp["w_out_2"][0])
    units = np.concatenate([p1, mix, wo, up, down, p2, wout], axis=0)
    units = np.ascontiguousarray(units).reshape(N_UNITS, P, D)
    w_ba = np.ascontiguousarray(w2[:, n:n + 2 * GH].reshape(KT, P, 2 * GH).transpose(1, 0, 2))

    def by_part(v):
        return v.reshape(-1, P).T

    conv = np.concatenate([inp["conv_w"][0], inp["conv_b"]], axis=0)
    conv = conv.reshape(4, 2, FT, P).transpose(3, 2, 1, 0).reshape(P, 4 * 2 * FT)
    conv2 = inp["conv_w_2"][0].reshape(4, 3, GH, P).transpose(3, 2, 1, 0).reshape(P, 48)
    cols = np.concatenate(
        [by_part(inp[k][0]) for k in ("norm_mix_pre", "norm_mix_post", "norm_ffn_pre",
                                      "norm_ffn_post", "w_norm_2", "b_gate", "pool_scale")]
        + [conv, conv2, by_part(inp["gdn_norm_w_2"][0])]
        + [np.concatenate([inp[k][0], inp[k][0]])[:, None] for k in ("q_norm_w_2", "k_norm_w_2")]
        + [by_part(inp["subln_w_2"][0])], axis=1)
    rows = np.concatenate([inp["a_log_2"][0], inp["dt_bias_2"][0], inp["lambda_q1_2"][0],
                           inp["lambda_k1_2"][0], inp["lambda_q2_2"][0], inp["lambda_k2_2"][0]])
    rows = np.broadcast_to(rows[None, :], (P, N_ROWS))
    rb = inp["rel_bias"][0]
    mid = (rb.shape[1] - 1) // 2
    dist = (S - P) + np.arange(P)[:, None] - np.arange(S)[None, :]
    rel = rb[:, np.clip(dist, -mid, mid) + mid].transpose(1, 0, 2)
    wgrp = inp["w_pool_group"][0].transpose(1, 0, 2)
    x = inp["x"][0].T.reshape(KT, P, S).transpose(1, 0, 2)

    t = np.arange(P)
    i, j = np.meshgrid(t, t, indexing="ij")
    same = (i // CH) == (j // CH)
    mats = [i == j, (i <= j) & same, same, (i // 64 == j // 64) & ((i % 64 + 32) % 64 == j % 64),
            np.where((i <= j) & same, 0.0, NEG), (i < j) & same]
    for lv in range(N_LEVELS):
        b = 1 << lv
        low = (i // (2 * b) == j // (2 * b)) & (i // b > j // b)
        mats += [low, low.T] if lv == 0 else [low.T]
    mats = np.stack([m.astype(np.float32) for m in mats], axis=1)
    inv = 10000.0 ** (-np.arange(0, HD, 2, dtype=np.float32) / np.float32(HD))
    ang = np.arange(S, dtype=np.float32)[:, None] * inv.astype(np.float32)[None, :]
    c, s = np.cos(ang).T, np.sin(ang).T
    causal = np.zeros((P, S), np.float32)
    causal[:, S - P:] = np.where(i >= j, 0.0, NEG)
    rope = np.stack([np.concatenate([c, c, c, c]), np.concatenate([-s, s, -s, s]), causal], axis=1)
    edge = np.stack([1.0 / np.minimum(np.arange(LEAD) + 1, w) for w in WINDOWS])
    edge = np.broadcast_to(edge[None].astype(np.float32), (P, 4, LEAD))
    return {"x": x, "w_units": units, "w_ba": w_ba, "cols": cols, "mats": mats, "rope": rope,
            "rows": rows, "rel": rel, "edge": edge, "wgrp": wgrp}


def kernel(**inputs):
    import numpy as _np
    import concourse.bacc as _bacc
    from concourse import mybir as _mybir
    from concourse.bass_utils import run_bass_kernel_spmd as _run

    nc = _bacc.Bacc("TRN2", target_bir_lowering=False, num_devices=1)
    arrays = _layout(_np, {k: _np.asarray(v) for k, v in inputs.items()})
    arrays = {"in_" + k: _np.ascontiguousarray(v, dtype=_np.float32) for k, v in arrays.items()}
    args = [nc.dram_tensor(k, v.shape, _mybir.dt.from_np(v.dtype), kind="ExternalInput").ap()
            for k, v in arrays.items()]
    out = nc.dram_tensor("out_0", (P, KT, S), _mybir.dt.float32, kind="ExternalOutput").ap()
    build(nc, *args, out, debug=DEBUG)
    r = _run(nc, [arrays], core_ids=[0])
    got = r.results[0]["out_0"]
    return _np.ascontiguousarray(got.transpose(2, 1, 0)).reshape(1, S, D)


DEBUG = None
```

```python
from contextlib import ExitStack

import concourse.bass as bass
from concourse import mybir

F32 = mybir.dt.float32
F32R = mybir.dt.float32r
ACT = mybir.ActivationFunctionType
ALU = mybir.AluOpType
AXX = mybir.AxisListType.X

P = 128
S = 512
D = 1024
KT = D // P
NT = S // P
HEADS, HD = 8, 64
PAIRS = HEADS // 2
CH = 64
GH = 4
DFF = 2816
FT = DFF // P
EPS, SUB_EPS = 1e-6, 1e-5
WINDOWS = (2, 4, 8, 16)
LEAD = max(WINDOWS)
LAM_INIT = 0.8 - 0.6
NEG = -1e30

N_P1, N_MIX, N_WO, N_UP, N_DOWN, N_P2, N_OUT = 32, 8, 8, 2 * FT, 3 * 8, 32, 8
N_UNITS = N_P1 + N_MIX + N_WO + N_UP + N_DOWN + N_P2 + N_OUT
RING = 4
BODY = 8
UP_FIRST, UP_TURN = 8, 12

C_MIXPRE, C_MIXPOST, C_FFNPRE, C_FFNPOST, C_NORM2 = 0, 8, 16, 24, 32
C_BGATE = 40
C_PSCALE = 56
C_CONV = 60
C_CONV2 = C_CONV + 4 * 2 * FT
C_GNORM = C_CONV2 + 4 * 12
C_QNORM, C_KNORM, C_SUBLN = C_GNORM + 1, C_GNORM + 2, C_GNORM + 3
N_COLS = C_GNORM + 4

(K_ID, K_UPPER, K_SAME, K_SWAP, K_NEG_T, K_STRICT_T, K_LEVEL) = range(7)
N_LEVELS = 6
N_MATS = K_LEVEL + 1 + N_LEVELS
R_ALOG, R_DT, R_LAM = 0, GH, 2 * GH
N_ROWS = R_LAM + 4 * HD


OUT_EARLY = [(k, r) for k in range(KT) for r in range(2 * GH) if r % GH < GH - 1]
OUT_LATE = [(k, r) for k in range(KT) for r in (GH - 1, 2 * GH - 1)]


class Tally:

    def __init__(self, name, sem, step=1, start=0):
        self.name, self.sem, self.step, self.n, self.per = name, sem, step, start, 0

    scope = 0

    def inc(self, ins):
        ins.then_inc(self.sem, self.step)
        self.n += self.step
        return self.now()

    def now(self):
        return self.at(self.n)

    def at(self, n):
        return (self, n, Tally.scope)


class Queue:

    def __init__(self, core, engine, sem):
        self.core, self.e, self.tally, self.seen = core, engine, sem, {}

    def on(self, *marks):
        for mark in marks:
            if mark is None:
                continue
            tally, n, scope = mark
            assert scope in (0, Tally.scope), "a mark of a loop that has ended"
            if self.seen.get((id(tally), scope), -1) >= n:
                continue
            self.seen[(id(tally), scope)] = n
            if scope:
                self.e.wait_ge(tally.sem, self.core.turn * tally.per + n)
            else:
                self.e.wait_ge(tally.sem, n)
        return self.e

    def on_apart(self, *marks):
        self.on(*marks)
        self.e.sem_inc(self.core.spare, 1)
        return self.e

    def mark(self, ins):
        return self.tally.inc(ins)

    def now(self):
        return self.tally.now()


class Core:
    def __init__(self, nc, ctx):
        self.nc, self.ctx, self.turn, self.loops, self.queues = nc, ctx, None, 0, []
        self.spare = ctx.enter_context(nc.semaphore("spare"))

    def queue(self, engine, name):
        q = Queue(self, engine, self.tally(name))
        self.queues.append(q)
        return q

    def tally(self, name, step=1, start=0):
        return Tally(name, self.ctx.enter_context(self.nc.semaphore(name)), step, start)

    def loop(self, turns, per, body, engines):
        begin = {t: t.n for t in per}
        for q in self.queues:
            q.seen = {}
        self.loops += 1
        with self.nc.Fori(0, turns, engines=engines) as i:
            self.turn, Tally.scope = i, self.loops
            for t, n in per.items():
                t.per = n
            body(i)
        self.turn, Tally.scope = None, 0
        bad = [(t.name, t.n - begin[t], n) for t, n in per.items() if t.n - begin[t] != n]
        assert not bad, bad
        for q in self.queues:
            q.seen = {}
        for t, n in per.items():
            t.n = begin[t] + turns * n


PACE_SCALARS, PACE_SCORES, PACE_PREP, PACE_END, PACE_FIRST = 3, 1.7, 1.1, 1.5, 1.2


def build(nc, x_in, w_units, w_ba, cols_in, mats_in, rope_in, rows_in, relb_in, window_in,
          wgrp_in, out):
    ctx = ExitStack()
    with ctx:
        core = Core(nc, ctx)
        V = core.queue(nc.vector, "vector_done")
        A = core.queue(nc.scalar, "scalar_done")
        T = core.queue(nc.tensor, "tensor_done")
        G = core.queue(nc.gpsimd, "gpsimd_done")
        COMPUTE = [mybir.EngineType.PE, mybir.EngineType.Activation, mybir.EngineType.DVE,
                   mybir.EngineType.Pool]

        def sb(stack, name, shape, dt=F32):
            return stack.enter_context(nc.sbuf_tensor(name, shape, dt))

        X = sb(ctx, "X", [P, KT, S])
        h_place = nc.sbuf_base
        Hh = sb(ctx, "Hh", [P, KT, S], F32R)
        Hl = sb(ctx, "Hl", [P, KT, S], F32R)
        raw = sb(ctx, "raw", [P, RING, D])
        Wh = sb(ctx, "Wh", [P, RING, D], F32R)
        Wl = sb(ctx, "Wl", [P, RING, D], F32R)
        cols = sb(ctx, "cols", [P, N_COLS])
        ident = sb(ctx, "ident", [P, P])
        ones = sb(ctx, "ones", [P, 1])
        half = sb(ctx, "half", [P, 4 * NT])
        ssum = sb(ctx, "ssum", [P, S])
        RB = sb(ctx, "RB", [P, S])
        sq = sb(ctx, "sq", [P, 2, S])
        rstd = sb(ctx, "rstd", [P, NT])
        rows = sb(ctx, "rows", [P, N_ROWS])
        ba_w = sb(ctx, "ba_w", [P, KT * 2 * GH])
        ba_h = sb(ctx, "ba_h", [P, KT * 2 * GH], F32R)
        ba_l = sb(ctx, "ba_l", [P, KT * 2 * GH], F32R)
        neg_lam = sb(ctx, "neg_lam", [P, 1])
        subln = sb(ctx, "subln", [P, 1])
        lam = sb(ctx, "lam", [P, 4])
        rate = sb(ctx, "rate", [P, GH])
        tmp = sb(ctx, "tmp", [P, 2, S])
        PS = ctx.enter_context(nc.psum_tensor("PS", [P, 8, S], F32))

        landed = [core.tally(f"unit_landed{s}", 16) for s in range(RING)]
        rounded = core.tally("unit_rounded")
        split = core.tally("unit_split", start=RING)
        used = core.tally("unit_used", start=RING)
        bank_free = [core.tally(f"bank{b}_free", start=1) for b in range(2)]
        nc.vector.sem_inc(split.sem, RING)
        nc.tensor.sem_inc(used.sem, RING)
        for t in bank_free:
            nc.vector.sem_inc(t.sem, 1)
        loaded_small = core.tally("small_loaded", 16)

        for dst, src in ((cols, cols_in), (ident, mats_in[:, 0, :])):
            loaded_small.inc(nc.scalar.dma_start(dst[:], src))
        loaded_x = [core.tally(f"x_loaded{n}", 16) for n in range(KT // 2)]
        for n in range(KT // 2):
            q = nc.gpsimd if n else nc.sync
            loaded_x[n].inc(q.dma_start(X[:, 2 * n:2 * n + 2, :], x_in[:, 2 * n:2 * n + 2, :]))

        with nc.sync.Fori(0, N_UNITS // RING) as i:
            for s in range(RING):
                nc.sync.wait_ge(split.sem, i * RING + (s + 1))
                nc.sync.dma_start(raw[:, s, :], w_units[bass.ds(i * RING + s, 1)]
                                  .rearrange("a p n -> (a p) n")).then_inc(landed[s].sem, 16)

        class Dense:
            unit = 0
            ahead = 0
            group = 0
            lazy = False
            lo = None

        class Norm:
            m = sum = rows = tiles = None
            sq_free, rb_read, waiting = [None, None], [None], []

        def split_unit():
            finish_split()
            n = Dense.ahead
            Dense.ahead += 1
            s = n % RING
            rounded.inc(A.on(landed[s].at(16 * (n // RING + 1)), used.at(n + 1))
                        .activation(Wh[:, s, :], raw[:, s, :], ACT.Copy))
            landed[s].n = 16 * (n // RING + 1)
            Dense.lo = lambda: split_lo(n)
            if not Dense.lazy:
                finish_split()

        def finish_split():
            lo, Dense.lo = Dense.lo, None
            if lo:
                lo()

        def split_lo(n):
            s = n % RING
            split.inc(V.on(rounded.at(n + 1)).tensor_tensor(
                Wl[:, s, :], raw[:, s, :], Wh[:, s, :].bitcast(F32), ALU.subtract))

        def products(bank, rhs_h, rhs_l, ks, ready, first=True, last=True):
            n = Dense.unit
            s = n % RING
            tiles, sums = Norm.tiles, None
            Norm.tiles = None
            for j, (k, r) in enumerate(ks):
                if Norm.rows and j == 2 and not tiles:
                    next(Norm.rows)
                if tiles:
                    if j == 4:
                        split_unit()
                    mark, sums = next(tiles)
                    h_ready.append(mark)
                T.on(split.at(n + 1 + RING), *(ready(r) if ready else ()))
                wsl = slice(k * P, (k + 1) * P)
                for m, (a, b) in enumerate(((Wh, rhs_h), (Wh, rhs_l), (Wl, rhs_h))):
                    ins = nc.tensor.matmul(bank, a[:, s, wsl], b(r), start=first and j == 0 and m == 0,
                                           stop=last and j == len(ks) - 1 and m == 2)
                if sums:
                    sums()
                yield ins

        def unit(evac, rhs=None, ready=None, nk=KT, group=(True, True), k0=0, second=None):
            b = Dense.group % 2
            if rhs is None:
                rhs = (lambda k: Hh[:, k, :], lambda k: Hl[:, k, :])
            if Dense.ahead < N_UNITS and not Norm.tiles:
                split_unit()
            if group[0]:
                T.on(bank_free[b].at(Dense.group // 2 + 1))
            bank = PS[:, b, :]
            ins = None
            if second is None:
                for ins in products(bank, *rhs, [(k, k0 + k) for k in range(nk)], ready,
                                    first=group[0], last=group[1]):
                    yield
            else:
                for ins in products(bank, *rhs, [(k, k) for k in range(4)], ready):
                    yield
                for ins in products(second[0], *second[1], [(k, k - 4) for k in range(4, 8)],
                                    second[2]):
                    yield
            done = used.inc(ins)
            Dense.unit += 1
            if group[1]:
                Dense.group += 1
                Norm.waiting.append(lambda: evac(bank, done, bank_free[b]))
                if Norm.rows and next(Norm.rows, Norm) is Norm:
                    Norm.rows = None
                while Norm.waiting and not Norm.rows:
                    Norm.waiting.pop(0)()
            yield

        def run(gen):
            for _ in gen:
                pass

        def finish_rms(m):
            m = V.mark(V.on(m).tensor_scalar(rstd[:], PS[:, 3, 0:NT], 1.0 / D, EPS, ALU.mult, ALU.add))
            m = G.mark(G.on(m).tensor_tensor(rstd[:], rstd[:], half[:, 0:NT], ALU.pow))
            yield
            for t in range(NT):
                ins = T.on(m).matmul(PS[:, 2, t * P:(t + 1) * P],
                                     rstd[:, t:t + 1].to_broadcast([P, P]), ident[:],
                                     start=True, stop=True)
            return T.mark(ins)

        def input_rows():
            row = ssum[0:1, :]
            m = V.mark(V.on(Norm.sum).tensor_copy(row, PS[0:1, 3, :]))
            yield
            for t in range(NT):
                ins = T.on(m).matmul(PS[:, 3, t:t + 1], row[:, t * P:(t + 1) * P], ones[0:1, :],
                                     start=True, stop=True)
            m = T.mark(ins)
            m = yield from finish_rms(m)
            Norm.m = V.mark(V.on(m, *Norm.rb_read).tensor_copy(RB[:], PS[:, 2, :]))

        def square(k, ready):
            dst = sq[:, k % 2, :]
            a = A.mark(A.on(ready, Norm.sq_free[k % 2]).activation(dst, X[:, k, :], ACT.Square))

            def sums():
                Norm.sum = Norm.sq_free[k % 2] = T.mark(T.on(a).matmul(
                    PS[0:1, 3, :], ones[:], dst, start=(k == 0), stop=(k == KT - 1)))
            return sums

        def dense_input(k, col, ready):
            g = cols[:, col + k:col + k + 1]
            m = A.mark(A.on(*ready).activation(Hh[:, k, :], X[:, k, :], ACT.Copy, scale=g))
            return V.mark(V.on(m).scalar_tensor_tensor(
                out=Hl[:, k, :], in0=X[:, k, :], scalar=g, in1=Hh[:, k, :].bitcast(F32),
                op0=ALU.mult, op1=ALU.subtract))

        def add_normed(M, ready, col):
            for t in range(NT):
                ins = T.on(ready).matmul(PS[:, 3, t:t + 1], ssum[:, t * P:(t + 1) * P], ones[:],
                                         start=True, stop=True)
            chain = finish_rms(T.mark(ins))
            next(chain)
            try:
                next(chain)
            except StopIteration as end:
                m_r = end.value
            Norm.rb_read = [V.now(), *(t.now() for t in bank_free)]
            m_rb = A.mark(A.on(m_r, *Norm.rb_read).activation(RB[:], PS[:, 2, :], ACT.Copy))
            Norm.rb_read.append(m_rb)
            Norm.sq_free = [m_r, m_r]
            Norm.rows = input_rows()
            share = (0, 1, 1, 0, 2, 0, 2, 0)
            scaled = {}
            for k in range(KT):
                if share[k]:
                    m = G.mark(G.on(m_rb).tensor_tensor(M[:, k, :], M[:, k, :], RB[:], ALU.mult))
                    if share[k] == 2:
                        m = G.mark(G.on(m).tensor_tensor(X[:, k, :], X[:, k, :], M[:, k, :],
                                                         ALU.add))
                    scaled[k] = m
            Norm.rb_read.append(G.now())

            def tiles():
                for k in range(KT):
                    m = scaled.get(k)
                    if not share[k]:
                        m = V.mark(V.on(m_rb).tensor_tensor(M[:, k, :], M[:, k, :], PS[:, 2, :],
                                                            ALU.mult))
                    if share[k] < 2:
                        m = V.mark(V.on(m).tensor_tensor(X[:, k, :], X[:, k, :], M[:, k, :],
                                                         ALU.add))
                    yield dense_input(k, col, (m,)), square(k, m)
            Norm.tiles = tiles()

        m_small = loaded_small.now()
        V.mark(nc.vector.memset(ones[:], 1.0))
        m0 = V.mark(nc.vector.memset(half[:], -0.5))
        A.on(m0).activation(rstd[:], half[:, 0:NT], ACT.Copy)
        V.on(m_small)
        A.on(m_small)
        G.on(m0)

        def first_tiles():
            for k in range(KT):
                m = loaded_x[k // 2].now()
                if k == 2:
                    split_unit()
                yield dense_input(k, C_MIXPRE, (m,)), square(k, m)
        split_unit()
        Norm.tiles = first_tiles()
        Norm.rows = input_rows()
        h_ready = []
        T.on(m0, m_small)

        def attend(a, qt, b, Q, K, scale, bias, ready, bufs, banks):
            nk = (qt + 1) * P
            r0 = HD * a
            SBs, nmax, rsum, rinv, free = bufs
            s_ps = PS[:, banks["S"][b % 2], 0:nk]
            m_s = T.mark(T.on(*ready, free["S"][b % 2]).matmul(
                s_ps, Q[r0:r0 + HD, qt * P:(qt + 1) * P], K[r0:r0 + HD, 0:nk],
                start=True, stop=True))
            m_b = V.mark(V.on(m_s, free["P"][b % 2]).scalar_tensor_tensor(
                out=SBs[:, b % 2, 0:nk], in0=s_ps, scalar=scale, in1=bias, op0=ALU.mult, op1=ALU.add))
            free["S"][b % 2] = m_b
            m_x = V.mark(V.on(m_b).tensor_reduce(nmax[:, b:b + 1], SBs[:, b % 2, 0:nk], AXX, ALU.max,
                                                 negate=True))
            m_p = A.mark(A.on(m_x).activation(
                SBs[:, b % 2, 0:nk], SBs[:, b % 2, 0:nk], ACT.Exp, bias=nmax[:, b:b + 1], scale=1.0,
                accum_out=rsum[:, b:b + 1]))
            m_r = V.mark(V.on(m_p).reciprocal(rinv[:, b:b + 1], rsum[:, b:b + 1]))
            return m_p, m_r

        def turn_weights(qt, j, src, m_src, PTs, free, banks):
            nk = (qt + 1) * P
            bank = banks["PT"][j % 2]
            for kt in range(qt + 1):
                ins = T.on(m_src, free["PT"][j % 2]).transpose(
                    PS[:, bank, kt * P:(kt + 1) * P], src[:, kt * P:(kt + 1) * P], ident[:])
            m_read = T.mark(ins)
            m_t = A.mark(A.on(m_read, free["PTs"][j % 2]).activation(
                PTs[:, j % 2, 0:nk], PS[:, bank, 0:nk], ACT.Copy))
            free["PT"][j % 2] = m_t
            return m_read, m_t

        def apply_weights(qt, j, m_t, PTs, values, width, free, banks):
            for kt in range(qt + 1):
                ins = T.on(m_t, free["O"][j % 2]).matmul(
                    PS[:, banks["O"][j % 2], 0:width], PTs[:, j % 2, kt * P:(kt + 1) * P],
                    values(kt), start=(kt == 0), stop=(kt == qt))
            m = T.mark(ins)
            free["PTs"][j % 2] = m
            return m

        class Fill:
            gens = []

        def fill(steps):
            while steps > 0 and Fill.gens:
                try:
                    next(Fill.gens[0])
                    steps -= 1
                except StopIteration:
                    Fill.gens.pop(0)

        def fill_all():
            fill(1 << 30)

        b1 = ctx.enter_context(ExitStack())
        gates = sb(b1, "gates", [P, 16, S])
        AOh = sb(b1, "AOh", [P, 4, S], F32R)
        AOl = sb(b1, "AOl", [P, 4, S], F32R)
        PLh = sb(b1, "PLh", [P, 4, S], F32R)
        PLl = sb(b1, "PLl", [P, 4, S], F32R)
        att = ExitStack()
        relb = sb(att, "relb", [P, HEADS, S])
        Q2 = sb(att, "Q2", [P, S])
        K2 = sb(att, "K2", [P, S])
        V2 = sb(att, "V2", [P, S])
        Vt = sb(att, "Vt", [P, NT, P])
        SBs, PTs = sq, tmp
        Ot = V2[:].rearrange("p (t n) -> p t n", t=NT)
        nmax = sb(att, "nmax", [P, 8])
        rsum = sb(att, "rsum", [P, 8])
        rinv = sb(att, "rinv", [P, 8])
        U = ssum
        UW = Q2
        wgrp = sb(att, "wgrp", [P, 4, P])
        window = sb(att, "window", [P, 4, 2 * P + LEAD])

        rel_loaded = core.tally("rel_loaded", 16)
        rel_loaded.inc(G.on(loaded_x[-1].now()).dma_start(relb[:], relb_in))
        rel_loaded.inc(nc.gpsimd.dma_start(wgrp[:], wgrp_in))
        rel_loaded.inc(nc.gpsimd.dma_start(window[:], window_in))
        rows_loaded = core.tally("rows_loaded", 16)
        rows_loaded.inc(nc.gpsimd.dma_start(rows[:], rows_in))
        rows_loaded.inc(nc.gpsimd.dma_start(ba_w[:], w_ba.rearrange("p k n -> p (k n)")))
        m_relb = G.mark(G.on(rel_loaded.now()).memset(relb[0:CH, :, S - CH:S], NEG))

        def pair_body(i):
            start = [q.now() for q in (V, A, T, G, *bank_free)]
            got = {}

            def to(name, dst):
                def evac(bank, done, freed):
                    freed.inc(V.on(done, Norm.m, *start).tensor_tensor(dst, bank, RB[:], ALU.mult))
                    got[name] = freed.now()
                return evac

            def flat(tile, idx):
                return tile[:, bass.ds(idx, 1), :].rearrange("p a n -> p (a n)")

            hr = (lambda r: (h_ready[r],))
            run(unit(to("q", Q2[:]), ready=hr))
            run(unit(to("k", K2[:]), ready=hr))
            run(unit(to("v", V2[:]), ready=hr))
            Fill.gens = [unit(to("u", U[:]))]
            Fill.gens += [unit(to("gate", flat(gates, 4 * i + j))) for j in range(4)]
            fill(4)
            V.on(m_relb)
            T.on(rel_loaded.now())
            for t in range(NT):
                ins = T.on(got["v"], *start).transpose(PS[:, 4, t * P:(t + 1) * P],
                                                       V2[:, t * P:(t + 1) * P], ident[:])
            m = T.mark(ins)
            m_v = V.mark(V.on(m).tensor_copy(Vt[:].rearrange("p t n -> p (t n)"), PS[:, 4, :]))
            free = {"S": [None] * 2, "P": [None] * 2, "PT": [m_v, None],
                    "PTs": [None] * 2, "O": [None] * 2}
            banks = {"S": (2, 3), "PT": (4, 5), "O": (6, 7)}
            bufs = (SBs, nmax, rsum, rinv, free)
            blocks = [(a, qt) for a in range(2) for qt in (3, 2, 1, 0)]

            def turned(a, qt, b, m_p, m_r):
                free["P"][b % 2], m_t = turn_weights(qt, b, SBs[:, b % 2, :], m_p, PTs, free, banks)
                return (a, qt, b, m_t, m_r)

            def applied(a, qt, b, m_t, m_r):
                m = apply_weights(qt, b, m_t, PTs, lambda kt: Vt[:, kt, HD * a:HD * a + HD], HD,
                                  free, banks)
                free["O"][b % 2] = V.mark(V.on(m, m_r).tensor_scalar(
                    Ot[:, qt, HD * a:HD * a + HD], PS[:, 6 + b % 2, 0:HD], rinv[:, b:b + 1], None,
                    ALU.mult))
                return free["O"][b % 2]

            to_turn = to_apply = None
            for b in range(len(blocks) + 2):
                scored = got_turned = None
                if b < len(blocks):
                    a, qt = blocks[b]
                    off = i * (2 * S) + (a * S + (NT - 1 - qt) * P)
                    bias = relb[:].rearrange("p h n -> p (h n)")[:, bass.ds(off, (qt + 1) * P)]
                    scored = (a, qt, b, *attend(a, qt, b, Q2, K2, HD ** -0.5, bias,
                                                (got["q"], got["k"]), bufs, banks))
                fill(3 if b < len(blocks) else 1)
                if to_turn:
                    got_turned = turned(*to_turn)
                fill(1)
                if to_apply:
                    m_o = applied(*to_apply)
                to_turn, to_apply = scored, got_turned
            fill(3)
            for t in range(NT):
                ins = T.on(m_o, free["PT"][0]).transpose(PS[:, 4, t * P:(t + 1) * P], Ot[:, t, :],
                                                         ident[:])
            m_t = T.mark(ins)
            for t in range(NT):
                ins = T.on_apart(got["u"], free["PT"][1]).matmul(
                    PS[:, 5, t * P:(t + 1) * P], U[:, t * P:(t + 1) * P], flat(wgrp, i),
                    start=True, stop=True)
            m = T.mark(ins)
            ah = flat(AOh, i)
            m_t = A.mark(A.on(m_t).activation(ah, PS[:, 4, :], ACT.Copy))
            m_uw = A.mark(A.on(m, *start).activation(UW[:], PS[:, 5, :], ACT.Copy))
            V.mark(V.on(m_t).tensor_tensor(flat(AOl, i), PS[:, 4, :], ah.bitcast(F32), ALU.subtract))
            fill(4)
            T.on_apart(m_uw, free["O"][1])
            win = flat(window, i)
            for t in range(NT):
                ins = T.e.matmul(PS[:, 7, t * P:(t + 1) * P], UW[:, t * P:(t + 1) * P],
                                 win[:, 0:P] if t else win[:, P:2 * P], start=True, stop=not t)
                if t:
                    ins = T.e.matmul(PS[:, 7, t * P:t * P + LEAD], UW[:, (t - 1) * P:t * P],
                                     win[:, 2 * P:], start=False, stop=True)
            m = T.mark(ins)
            fill(2)
            ph, scale = flat(PLh, i), cols[:, bass.ds(C_PSCALE + i, 1)]
            m = A.mark(A.on_apart(m).activation(ph, PS[:, 7, :], ACT.Copy, scale=scale))
            V.mark(V.on(m).scalar_tensor_tensor(out=flat(PLl, i), in0=PS[:, 7, :], scalar=scale,
                                                in1=ph.bitcast(F32), op0=ALU.mult,
                                                op1=ALU.subtract))
            fill_all()

        def dense_loop(turns, units, groups, own, body):
            per = {q.tally: n for q, n in zip((V, A, T, G), own) if n}
            per.update({t: 16 * units // RING for t in landed})
            per.update({rounded: units, split: units, used: units})
            per.update({t: groups // 2 for t in bank_free})
            core.loop(turns, per, body, COMPUTE)
            Dense.unit += (turns - 1) * units
            Dense.ahead += (turns - 1) * units
            Dense.group += (turns - 1) * groups

        pair_body(0)

        lv = rows[:, R_LAM:].rearrange("p (a b d) -> p a b d", a=2, b=2)
        V.on(rows_loaded.now())
        lam_prod = tmp[:, 0, 0:2 * HD].rearrange("p (a d) -> p a d", a=2)
        m = V.mark(V.on(V.now()).tensor_tensor(lam_prod, lv[:, :, 0, :], lv[:, :, 1, :], ALU.mult))
        m = V.mark(V.on(m).tensor_reduce(lam[:, 0:2], lam_prod, AXX, ALU.add))
        m = A.mark(A.on(m).activation(lam[:, 2:4], lam[:, 0:2], ACT.Exp))
        m = V.mark(V.on(m).tensor_tensor(neg_lam[:], lam[:, 3:4], lam[:, 2:3], ALU.subtract))
        m = V.mark(V.on(m).tensor_scalar(neg_lam[:], neg_lam[:], -LAM_INIT, None, ALU.add))
        V.mark(V.e.tensor_scalar(subln[:], cols[:, C_SUBLN:C_SUBLN + 1], 1.0 - LAM_INIT, None,
                                 ALU.mult))

        m = A.mark(A.on(rows_loaded.now()).activation(ba_h[:], ba_w[:], ACT.Copy))
        A.mark(A.on(rows_loaded.now()).activation(rate[:], rows[:, R_ALOG:R_ALOG + GH], ACT.Exp))
        m_ba_w = V.mark(V.on(m).tensor_tensor(ba_l[:], ba_w[:], ba_h[:].bitcast(F32), ALU.subtract))

        dense_loop(PAIRS - 1, BODY, BODY, (35, 19, 28, 0), lambda i: pair_body(i + 1))
        att.close()

        m_pooled = V.now()
        T.on(V.tally.at(V.tally.n - 1))
        V.on(T.now(), A.now())
        A.on(*[t.now() for t in bank_free])

        def flat2(tile, idx):
            return tile[:, bass.ds(idx, 1), :].rearrange("p a n -> p (a n)")

        def split_into(dst_h, dst_l, idx, src, ready):
            m = A.mark(A.on(ready).activation(flat2(dst_h, idx), src, ACT.Copy))
            return V.mark(V.on(m).tensor_tensor(flat2(dst_l, idx), src,
                                                flat2(dst_h, idx).bitcast(F32), ALU.subtract))

        def mix_body(i):
            last = [V.now(), V.now()]
            for j in range(4):
                b = j % 2
                for n in (j, 8 + j):
                    g = flat2(gates, i * 4 + n)
                    gated = A.mark(A.e.activation(
                        g, g, ACT.Sigmoid, bias=cols[:, bass.ds(C_BGATE + i * 4 + n, 1)],
                        scale=1.0))

                def evac(bank, done, freed):
                    m1 = V.mark(V.on(done, gated, last[b]).tensor_tensor(
                        tmp[:, b, :], bank, flat2(gates, i * 4 + j), ALU.mult))
                    m2 = freed.inc(V.e.tensor_tensor(
                        sq[:, b, :], PS[:, 2 + b, :], flat2(gates, i * 4 + (8 + j)), ALU.mult))
                    m3 = V.mark(V.on(m1, m2).tensor_tensor(tmp[:, b, :], tmp[:, b, :], sq[:, b, :],
                                                           ALU.add))
                    last[b] = split_into(Hh, Hl, i * 4 + j, tmp[:, b, :], m3)
                run(unit(evac, rhs=(lambda k: AOh[:, k, :], lambda k: AOl[:, k, :]),
                         second=(PS[:, 2 + b, :], (lambda k: PLh[:, k, :], lambda k: PLl[:, k, :]),
                                 lambda r: (m_pooled,) if r == 3 else ())))
        dense_loop(2, 4, 4, (12, 12, 0, 0), mix_body)

        ffn = ExitStack()

        def normed_out(M, groups, rhs, post_col, own, ready=None):
            def body(i):
                Norm.sum, Norm.sq_free = G.now(), [G.now(), G.now()]
                for j, ks in enumerate(groups):
                    def evac(bank, done, freed):
                        k = i * len(groups) + j
                        a = A.mark(A.on(done, Norm.sq_free[j % 2]).activation(
                            sq[:, j % 2, :], bank, ACT.Square))
                        freed.inc(A.on_apart(done).activation(
                            flat2(M, k), bank, ACT.Copy, scale=cols[:, bass.ds(post_col + k, 1)]))
                        Norm.sum = Norm.sq_free[j % 2] = G.mark(G.on(a, Norm.sum).tensor_tensor(
                            ssum[:], ssum[:], sq[:, j % 2, :], ALU.add))
                    for n, nk in enumerate(ks):
                        run(unit(evac, rhs=rhs, ready=ready, nk=nk, k0=KT * n,
                                 group=(n == 0, n == len(ks) - 1)))
            G.mark(G.on(Norm.m, V.now(), T.now()).memset(ssum[:], 0.0))
            n = len(groups)
            dense_loop(KT // n, sum(len(g) for g in groups), n, own, body)
            return G.now()

        b1.close()
        M1 = sb(ffn, "M1", [P, KT, S])
        m_mix = V.now()
        T.on(V.tally.at(V.tally.n - 3))
        A.on(m_mix)
        m = normed_out(M1, [[KT]] * 4, None, C_MIXPOST, (0, 4, 0, 4),
                       ready=lambda r: (m_mix,) if r == KT - 1 else ())
        add_normed(M1, m, C_FFNPRE)
        h_ready = []
        ffn.close()

        Ah = sb(ffn, "Ah", [P, FT, S], F32R)
        Al = sb(ffn, "Al", [P, FT, S], F32R)
        A.on(V.now())

        ffn_up = ExitStack()
        conv = sb(ffn_up, "conv", [P, 2, 2, S])

        def up_body(first, tile0, n_units):
            start_v, start_a = V.now(), A.now()
            y_free = [None, None]
            c_free = [None, None]
            later = []

            def c4(j, tap):
                return cols[:, bass.ds(C_CONV + first * 4 + (4 * j + tap), 1)]

            def behind():
                for step in list(later):
                    later.remove(step)
                    try:
                        next(step)
                        later.append(step)
                    except StopIteration:
                        pass

            def rest(j, m, y):
                pair = j // 2 % 2
                v, c = conv[:, pair, 0, :], conv[:, pair, j % 2, :]
                for tap in (1, 0):
                    d = 2 - tap
                    m = V.mark(V.on(m).scalar_tensor_tensor(
                        out=c[:, d:], in0=y[:, 0:S - d], scalar=c4(j, tap), in1=c[:, d:],
                        op0=ALU.mult, op1=ALU.add))
                y_free[j % 2] = m
                if j % 2:
                    m = A.mark(A.on(m).activation(c, c, ACT.Gelu_apprx_tanh))
                    yield
                    m = c_free[pair] = V.mark(V.on(m).tensor_tensor(v, v, c, ALU.mult))
                    dst = flat2(Ah, tile0 + j // 2)
                    m = A.mark(A.on(m).activation(dst, v, ACT.Copy))
                    yield
                    c_free[pair] = V.mark(V.on(m).tensor_tensor(
                        flat2(Al, tile0 + j // 2), v, dst.bitcast(F32), ALU.subtract))

            for j in range(n_units):
                def evac(bank, done, freed, j=j):
                    c, y = conv[:, j // 2 % 2, j % 2, :], tmp[:, j % 2, :]
                    m = freed.inc(V.on(done, Norm.m, start_a, y_free[j % 2]).tensor_tensor(
                        y, bank, RB[:], ALU.mult))
                    finish_split()
                    behind()
                    m = A.mark(A.on_apart(m, start_v, start_a, c_free[j // 2 % 2]).activation(
                        c, y, ACT.Identity, bias=c4(j, 3), scale=c4(j, 2)))
                    later.append(rest(j, m, y))
                run(unit(evac, ready=lambda r: (h_ready[r],)))
            while later:
                behind()
        Dense.lazy = True
        up_body(0, 0, UP_FIRST)
        own = (3 * UP_TURN, 2 * UP_TURN, 0, 0)
        dense_loop((N_UP - UP_FIRST) // UP_TURN, UP_TURN, UP_TURN, own, lambda i: up_body(
            i * UP_TURN + UP_FIRST, i * (UP_TURN // 2) + UP_FIRST // 2, UP_TURN))
        Dense.lazy = False
        ffn_up.close()
        M2 = nc.alloc_sbuf_tensor_at("M2", [P, KT, S], F32, offset=h_place)
        T.on(V.tally.at(V.tally.n - own[0]))
        m_ffn = V.now()
        A.on(m_ffn)
        m = normed_out(M2, [[KT, KT, FT - 2 * KT]] * 4,
                       (lambda k: Ah[:, k, :], lambda k: Al[:, k, :]), C_FFNPOST, (0, 4, 0, 4),
                       ready=lambda r: (m_ffn,) if r >= 2 * KT else ())
        ffn.close()

        b2 = ctx.enter_context(ExitStack())
        mats = sb(b2, "mats", [P, N_MATS - 1, P])
        rope = sb(b2, "rope", [P, 2, S])
        causal = sb(b2, "causal", [P, P])
        O = sb(b2, "O", [P, 2 * GH, S])
        ffn_done = [V.now(), A.now(), T.now(), used.at(Dense.unit + RING)]
        b2_loaded = core.tally("b2_loaded", 16)
        G.on(*ffn_done, *[t.now() for t in bank_free])
        for dst, src in ((mats, mats_in[:, 1:, :]), (rope, rope_in[:, 0:2, :]),
                         (causal, rope_in[:, 2, S - P:])):
            b2_loaded.inc(nc.gpsimd.dma_start(dst[:], src))

        def mat(k):
            return mats[:, k - 1, :]

        def over_tiles(ap):
            return ap.unsqueeze(1).to_broadcast([P, NT, P])

        def tiles(ap):
            return ap.rearrange("p (t n) -> p t n", t=NT)

        def over_cols(ap, n=P):
            return ap.unsqueeze(2).to_broadcast([P, ap.shape[1], n])

        glog = sb(b2, "glog", [P, GH, NT])
        gcum = sb(b2, "gcum", [P, GH, NT])
        beta = sb(b2, "beta", [P, GH, NT])
        beta_eg = sb(b2, "beta_eg", [P, GH, NT])
        to_end = sb(b2, "to_end", [P, GH, NT])
        chunk_decay = sb(b2, "chunk_decay", [P, GH, 2 * NT])
        small = sb(b2, "small", [P, 4, GH * NT])

        ba = sb(b2, "ba", [P, 2 * GH, NT])
        add_normed(M2, m, C_NORM2)
        h_ready = []

        def scalars():
            m = m_ba_w
            T.on(m)
            for k in range(KT):
                w = slice(2 * GH * k, 2 * GH * (k + 1))
                T.on(m, h_ready[k])
                for n, (a, b) in enumerate(((ba_h, Hh), (ba_h, Hl), (ba_l, Hh))):
                    ins = T.e.matmul(PS[0:2 * GH, 4, :], a[:, w], b[:, k, :],
                                     start=(k == 0 and n == 0), stop=(k == KT - 1 and n == 2))
            m = T.mark(ins)
            yield
            ba_rows = tmp[0:2 * GH, 0, :]
            m = V.mark(V.on(m).tensor_copy(ba_rows, PS[0:2 * GH, 4, :]))
            yield
            for t in range(NT):
                ins = T.on(m).transpose(PS[:, 5, 2 * GH * t:2 * GH * (t + 1)],
                                        ba_rows[:, t * P:(t + 1) * P], ident[0:2 * GH, 0:2 * GH])
            m_ba = T.mark(ins)
            yield
            m_ba = V.mark(V.on(m_ba, Norm.m).tensor_tensor(
                ba[:], PS[:, 5, 0:2 * GH * NT].rearrange("p (t n) -> p n t", t=NT),
                rstd[:].unsqueeze(1).to_broadcast([P, 2 * GH, NT]), ALU.mult))
            yield
            sm = [small[:, n, :].rearrange("p (h t) -> p h t", t=NT) for n in range(4)]
            m = A.mark(A.on(m_ba).activation(sm[0], ba[:, 0:GH, :], ACT.Exp, scale=-1.0))
            m = V.mark(V.on(m).tensor_scalar(sm[0], sm[0], 1.0, None, ALU.add))
            m_beta = V.mark(V.on(m).reciprocal(beta[:], sm[0]))
            m_y = V.mark(V.on(m_ba).tensor_tensor(
                sm[1], ba[:, GH:2 * GH, :], over_cols(rows[:, R_DT:R_DT + GH], NT), ALU.add))
            m = V.mark(V.on(m_y).tensor_scalar(sm[2], sm[1], -1.0, None, ALU.mult))
            m = V.mark(V.on(m).tensor_tensor(sm[2], sm[1], sm[2], ALU.max))
            m = A.mark(A.on(m).activation(sm[2], sm[2], ACT.Exp, scale=-1.0))
            m = V.mark(V.on(m).tensor_scalar(sm[2], sm[2], 1.0, None, ALU.add))
            yield
            m = A.mark(A.on(m).activation(sm[2], sm[2], ACT.Ln))
            m = V.mark(V.on(m).scalar_tensor_tensor(out=small[:, 2, :], in0=small[:, 1, :], scalar=0.0,
                                                    in1=small[:, 2, :], op0=ALU.max, op1=ALU.add))
            m = V.mark(V.on(m).tensor_tensor(sm[2], sm[2], over_cols(rate[:], NT), ALU.mult))
            m_g = V.mark(V.on(m).tensor_scalar(glog[:], sm[2], -1.0, None, ALU.mult))
            yield
            V.on(b2_loaded.now())
            A.on(b2_loaded.now())
            T.on(b2_loaded.now())
            gl2 = glog[:].rearrange("p h t -> p (h t)")
            by_chunk = small[:, 2:4, :].rearrange("p a n -> p (a n)")
            m_c = V.mark(V.on(m_g).tensor_tensor(
                by_chunk.rearrange("p (n c) -> p n c", c=2), over_cols(gl2, 2),
                mat(K_SAME)[:, 0:P:CH].unsqueeze(1).to_broadcast([P, GH * NT, 2]), ALU.mult))
            n16 = GH * NT
            T.on(m_g).matmul(PS[:, 4, 0:n16], mat(K_UPPER), gl2, start=True, stop=True)
            T.e.matmul(PS[:, 4, n16:2 * n16], mat(K_SAME), gl2, start=True, stop=True)
            ins = T.on(m_c).matmul(PS[:, 4, 2 * n16:4 * n16], ones[:].to_broadcast([P, P]),
                                   by_chunk, start=True, stop=True)
            m = T.mark(ins)
            yield
            m_gc = V.mark(V.on(m).tensor_copy(gcum[:].rearrange("p h t -> p (h t)"), PS[:, 4, 0:n16]))
            m_d = V.mark(V.on(m_gc).tensor_tensor(small[:, 0, :], PS[:, 4, n16:2 * n16],
                                                  gcum[:].rearrange("p h t -> p (h t)"), ALU.subtract))
            A.mark(A.on(m_d).activation(to_end[:].rearrange("p h t -> p (h t)"), small[:, 0, :], ACT.Exp))
            A.mark(A.e.activation(chunk_decay[:].rearrange("p h t -> p (h t)"),
                                  PS[:, 4, 2 * n16:4 * n16], ACT.Exp))
            m = A.mark(A.e.activation(small[:, 1, :], gcum[:].rearrange("p h t -> p (h t)"), ACT.Exp))
            m = V.mark(V.on(m, m_beta).tensor_tensor(
                beta_eg[:].rearrange("p h t -> p (h t)"), beta[:].rearrange("p h t -> p (h t)"),
                small[:, 1, :], ALU.mult))

        hb = ExitStack()
        names = ("Vb", "DT", "LT", "Lo", "LmT", "Ti", "TiT", "Y",
                 "QG", "U", "Wt", "Kd", "AT", "VN", "Oa",
                 "Qb", "Kr", "Vd", "Vdt", "Od", "Wd")
        B = {n: sb(hb, "head_" + n, [P, S]) for n in names}
        B["Bm"] = B["Lm"] = B["Y"]
        B["Kb"] = B["Lo"]
        C3 = sb(hb, "C3", [P, 3, S])
        CQ, CK, CV = (C3[:, n, :] for n in range(3))
        Yc = sb(hb, "Yc", [P, 2, S])
        EG = ssum
        Zr = sb(hb, "Zr", [P, 2, S])
        Zs = sb(hb, "Zs", [P, 2, S])
        P2 = sb(hb, "P2", [P, 2, S])
        St = sb(hb, "St", [P, P])
        gs = sb(hb, "gs", [P, 2, NT])
        rqk = sb(hb, "rqk", [P, 2 * NT])
        rq_scan = sb(hb, "rq_scan", [P, NT])
        rqk_b = sb(hb, "rqk_b", [P, 2, NT, 2])
        r_o = sb(hb, "r_o", [P, 2, NT])
        nmax2 = sb(hb, "nmax2", [P, 8])
        rsum2 = sb(hb, "rsum2", [P, 8])
        rinv2 = sb(hb, "rinv2", [P, 8])
        neg_r = sb(hb, "neg_r", [P, 8])
        B_SCAN, B_S, B_PT, B_A = 2, (3, 4), 5, (6, 7)

        def head(tile, i):
            return tile[:, bass.ds(i, 1), :].rearrange("p a n -> p (a n)")

        def row_of(scalars, bank, ready, rhs=None):
            for t in range(NT):
                ins = T.on(*ready).matmul(PS[:, bank, t * P:(t + 1) * P],
                                          scalars[:, t:t + 1].to_broadcast([P, P]),
                                          ident[:] if rhs is None else rhs, start=True, stop=True)
            return T.mark(ins)

        def per_tile(out, lhs, rhs, ready):
            for t in range(NT):
                ins = T.on(*ready).matmul(out(t), lhs(t), rhs(t), start=True, stop=True)
            return T.mark(ins)

        def tile_of(ap):
            return lambda t: ap[:, t * P:(t + 1) * P]

        def bank_tile(bank):
            return lambda t: PS[:, bank, t * P:(t + 1) * P]

        def turn_tiles(bank, src, ready):
            for t in range(NT):
                tok = slice(t * P, (t + 1) * P)
                ins = T.on(*ready).transpose(PS[:, bank, tok], src[:, tok], ident[:])
            return T.mark(ins)

        def blocks(ap, size, odd):
            return ap.rearrange("p (g two b) -> p g two b", two=2, b=size)[:, :, odd, :]

        class Head:

            def __init__(self):
                self.start = [q.now() for q in (V, A, T, G, *bank_free)]
                self.scores_read = [V.now(), A.now()]
                self.scan_done = self.diff_done = self.v_turned = None

        def conv_unit(st, i, j):
            c = C3[:, j, :]

            def tap(n):
                return cols[:, bass.ds(C_CONV2 + i * 12 + (4 * j + n), 1)]

            def evac(bank, done, freed):
                y = Yc[:, j % 2, :]
                run(st.taps[j % 2])
                m = freed.inc(V.on(done, Norm.m, *st.start, st.y_free[j % 2]).tensor_tensor(
                    y, bank, RB[:], ALU.mult))
                m = A.mark(A.on_apart(m, *st.start).activation(
                    c, y, ACT.Identity, bias=0.0, scale=tap(3)))

                def rest(m):
                    for n in (2, 1, 0):
                        yield
                        m = V.mark(V.on(m).scalar_tensor_tensor(
                            out=c[:, 3 - n:], in0=y[:, 0:S - 3 + n], scalar=tap(n),
                            in1=c[:, 3 - n:], op0=ALU.mult, op1=ALU.add))
                    st.y_free[j % 2] = m
                    st.convs.append(m)
                st.taps[j % 2] = rest(m)
                st.rounds.gens.insert(0, st.taps[j % 2])
            return unit(evac, ready=st.h_ready)

        def z_unit(st, branch):
            def evac(bank, done, freed):
                freed.inc(V.on(done, Norm.m, st.zs).tensor_tensor(Zr[:, branch, :], bank, RB[:],
                                                                  ALU.mult))
            return unit(evac, ready=st.h_ready)

        def qk_unit(st, name, j, col):
            def evac(bank, done, freed):
                y = Yc[:, j, :]
                run(st.taps[j])
                m = freed.inc(V.on(done, Norm.m, *st.start, st.y_free[j]).tensor_tensor(
                    y, bank, RB[:], ALU.mult))
                A.on(m, *st.start, st.diff_done, st.sq_read).activation(
                    B[name][:], y, ACT.Copy, scale=cols[:, col:col + 1])
                st.sq2[j] = A.mark(A.e.activation(sq[:, j, :], y, ACT.Square))
            return unit(evac, ready=st.h_ready)

        def v_unit(st):
            def evac(bank, done, freed):
                freed.inc(V.on(done, Norm.m, *st.start, st.v_turned).tensor_tensor(
                    B["Vd"][:], bank, RB[:], ALU.mult))
            return unit(evac, ready=st.h_ready)

        def prep(st, i, gates_too):
            b6, b7 = PS[:, B_A[0], :], PS[:, B_A[1], :]
            V.on(*st.start).tensor_copy(gs[:, 0, :], head(glog, i))
            m_gs = V.mark(V.e.tensor_copy(gs[:, 1, :], head(beta, i)))
            if gates_too:
                st.zs = A.mark(A.on(*st.start).activation(Zs[:], Zr[:], ACT.Silu))
            yield
            m_grow = row_of(gs[:, 0, :], B_A[0], (m_gs, *st.start), rhs=mat(K_UPPER))
            m_brow = row_of(gs[:, 1, :], B_A[1], (m_gs,))
            yield
            m_d = V.mark(V.on(m_grow).tensor_tensor(tiles(B["DT"][:]), tiles(b6),
                                                    over_cols(head(gcum, i)), ALU.subtract))
            m_bm = V.mark(V.on(m_brow).tensor_tensor(tiles(B["Bm"][:]), tiles(b7),
                                                     over_tiles(mat(K_STRICT_T)), ALU.mult))
            m_dt = V.mark(V.on(m_d).tensor_tensor(tiles(B["DT"][:]), tiles(B["DT"][:]),
                                                over_tiles(mat(K_NEG_T)), ALU.add))
            m_eg = A.mark(A.on(m_d, *st.start).activation(EG[:], b6, ACT.Exp))
            yield
            m_dt = A.mark(A.on(m_dt).activation(B["DT"][:], B["DT"][:], ACT.Exp))
            while len(st.convs) < 3:
                yield
            m_c = A.mark(A.on(*st.convs, *st.start).activation(C3[:], C3[:], ACT.Silu))
            yield
            m_sq = [A.mark(A.on(m_c).activation(sq[:, j, :], c, ACT.Square))
                    for j, c in enumerate((CQ, CK))]
            yield
            for j in range(2):
                for t in range(NT):
                    ins = T.on(m_sq[1 - j], m_bm).matmul(
                        b7[:, NT * j + t:NT * j + t + 1], sq[:, 1 - j, t * P:(t + 1) * P], ones[:],
                        start=True, stop=True)
            st.sq_read = T.mark(ins)
            yield
            m_n = V.mark(V.on(st.sq_read).tensor_scalar(rqk[:], b7[:, 0:2 * NT], EPS, None, ALU.add))
            yield
            m_rk = G.mark(G.on(m_n).tensor_tensor(rqk[:, 0:NT], rqk[:, 0:NT], half[:, 0:NT],
                                                  ALU.pow))
            m_rq = G.mark(G.e.tensor_tensor(rqk[:, NT:], rqk[:, NT:], half[:, 0:NT], ALU.pow))
            m_vt = turn_tiles(B_A[1], CV, (m_c, m_n))
            yield
            m_kr = row_of(rqk[:, 0:NT], B_A[0], (m_rk, m_eg, m_dt))
            m_vb = V.mark(V.on(m_vt).tensor_tensor(tiles(B["Vb"][:]), tiles(b7),
                                                   over_cols(head(beta, i)), ALU.mult))
            yield
            m_kn = V.mark(V.on(m_kr).tensor_tensor(CK, CK, b6, ALU.mult))
            yield
            m_kk = per_tile(bank_tile(B_A[1]), tile_of(CK), tile_of(CK), (m_kn, m_vb))
            yield
            m = V.mark(V.on(m_kk, m_dt).tensor_tensor(B["LT"][:], b7, B["DT"][:], ALU.mult))
            m_lt = V.mark(V.on(m).tensor_tensor(B["LT"][:], B["LT"][:], B["Bm"][:], ALU.mult))
            yield
            m = turn_tiles(B_A[0], B["LT"][:], (m_lt,))

            def level_mask(lv, read):
                return G.mark(G.on(m_lt, *read).tensor_tensor(
                    tiles(B["LmT"][:]), tiles(B["LT"][:]), over_tiles(mat(K_LEVEL + 1 + lv)),
                    ALU.mult))
            m_lm = level_mask(0, ())
            yield
            m_lo = A.mark(A.on(m).activation(B["Lo"][:], b6, ACT.Copy))
            m_tt = V.mark(V.on(m_lm).tensor_tensor(tiles(B["TiT"][:]), over_tiles(ident[:]),
                                                   tiles(B["LmT"][:]), ALU.subtract))
            yield
            m_l0 = G.mark(G.on(m_lo).tensor_tensor(tiles(B["Lm"][:]), tiles(B["Lo"][:]),
                                                   over_tiles(mat(K_LEVEL)), ALU.mult))
            m_lm = level_mask(1, (m_tt,))
            yield
            m_ti = V.mark(V.on(m_l0).tensor_tensor(tiles(B["Ti"][:]), over_tiles(ident[:]),
                                                   tiles(B["Lm"][:]), ALU.subtract))
            yield
            for lv in range(1, N_LEVELS):
                size = 1 << lv
                m_y = per_tile(bank_tile(B_A[0]), tile_of(B["LmT"]), tile_of(B["Ti"]),
                               (m_lm, m_ti, m_tt, m_lo))
                yield
                m_ya = A.mark(A.on(m_y).activation(B["Y"][:], b6, ACT.Copy))
                if lv + 1 < N_LEVELS:
                    m_lm = level_mask(lv + 1, (m_y,))
                yield
                H = P // 2
                if lv + 1 < N_LEVELS:
                    m_t = per_tile(lambda t: b7[:, t * H:(t + 1) * H], tile_of(B["TiT"]),
                                   lambda t: blocks(tile_of(B["Y"])(t), size, 0), (m_ya, m_lt))
                m_t2 = per_tile(lambda t: b7[:, 2 * P + t * H:2 * P + (t + 1) * H],
                                tile_of(B["Y"]), lambda t: blocks(tile_of(B["TiT"])(t), size, 1),
                                (m_ya, m_lt))
                yield
                for name, odd, off in (("Ti", 0, 0), ("TiT", 1, 2 * P)):
                    if name == "Ti" and lv + 1 == N_LEVELS:
                        continue
                    v = blocks(B[name][:], size, odd)
                    m_tt = V.mark(V.on(m_t2).tensor_tensor(
                        v, v, b7[:, off:off + 2 * P].rearrange("p (g b) -> p g b", b=size),
                        ALU.subtract))
                m_ti = m_tt
                yield
            while st.scanning:
                yield
            free = (*st.start, *st.scan_done) if st.scan_done else st.start
            m_kt = turn_tiles(B_A[0], CK, (m_ya, m_kn))
            m_qk = per_tile(bank_tile(B_A[1]), tile_of(CK), tile_of(CQ), (m_tt,))
            yield
            V.mark(V.on(m_kt, m_l0, *free).tensor_tensor(
                tiles(B["Kb"][:]), tiles(b6), over_cols(head(beta_eg, i)), ALU.mult))
            m_kd = V.mark(V.e.tensor_tensor(tiles(B["Kd"][:]), tiles(b6),
                                            over_cols(head(to_end, i)), ALU.mult))
            m_at = V.mark(V.on(m_qk).tensor_tensor(B["AT"][:], b7, B["DT"][:], ALU.mult))
            G.mark(G.on(m_c, m_eg, m_qk, *free).tensor_tensor(B["QG"][:], CQ, EG[:], ALU.mult))
            V.mark(V.on(m_rq).tensor_scalar(rq_scan[:], rqk[:, NT:], P ** -0.5, None, ALU.mult))
            yield
            m_u = per_tile(bank_tile(B_A[0]), tile_of(B["TiT"]), tile_of(B["Vb"]), (m_kd,))
            m_w = per_tile(bank_tile(B_A[1]), tile_of(B["Kb"]), tile_of(B["TiT"]), (m_at,))
            yield
            m_u = A.mark(A.on(m_u, *free).activation(B["U"][:], b6, ACT.Copy))
            m_w = V.mark(V.on(m_w).tensor_copy(B["Wt"][:], b7))

        def norms(st):
            bank = PS[:, B_S[0], :]
            while None in st.sq2:
                yield
            for j in range(2):
                for t in range(NT):
                    ins = T.on(st.sq2[j], *st.scores_read).matmul(
                        bank[:, 8 * j + 2 * t:8 * j + 2 * t + 2],
                        sq[:, j, t * P:(t + 1) * P], mat(K_SAME)[:, 0:P:CH], start=True, stop=True)
            m = T.mark(ins)
            yield
            r2 = rqk_b[:].rearrange("p a t c -> p (a t c)")
            m = V.mark(V.on(m, *st.start).tensor_scalar(r2, bank[:, 0:16], 1.0 / HD, EPS, ALU.mult,
                                                        ALU.add))
            yield
            m = G.mark(G.on(m).tensor_tensor(r2, r2, half[:, 0:16], ALU.pow))
            yield
            V.mark(V.on(m).tensor_scalar(rqk_b[:, 0, :, :], rqk_b[:, 0, :, :], HD ** -0.5, None,
                                         ALU.mult))

        def out_norm(st, i, o, spare, branch, bank, m, eps, weight, ready):
            r = r_o[:, branch, :]
            A.on(m, *ready, *st.start)
            for t in range(NT):
                tile_ = slice(t * P, (t + 1) * P)
                m_q = A.mark(A.e.activation(spare[:, tile_], o[:, tile_], ACT.Square,
                                            accum_out=r[:, t:t + 1]))
            yield
            m_q = V.mark(V.on(m_q).tensor_scalar(r, r, 1.0 / P, eps, ALU.mult, ALU.add))
            yield
            m_q = G.mark(G.on(m_q).tensor_tensor(r, r, half[:, 0:NT], ALU.pow))
            yield
            m_q = V.mark(V.on(m_q).tensor_tensor(tiles(o[:]), tiles(o[:]), over_cols(r), ALU.mult))
            yield
            m_q = turn_tiles(bank, o[:], (m_q,))
            yield
            while st.zs is None:
                yield
            V.mark(V.on(m_q, st.zs).scalar_tensor_tensor(
                out=head(O, i + GH * branch), in0=PS[:, bank, :], scalar=weight,
                in1=Zs[:, branch, :], op0=ALU.mult, op1=ALU.mult))

        def scan(st, i):
            bank = PS[:, B_SCAN, :]
            m_s = m_out = V.mark(V.on(*st.start).memset(St[:], 0.0))
            T.on(*st.start)
            for c in range(S // CH):
                t, r0 = c // 2, CH * (c % 2)
                rows_ = slice(r0, r0 + CH)
                own, tile_ = slice(t * P + r0, t * P + r0 + CH), slice(t * P, (t + 1) * P)
                m = T.mark(T.on(m_s, m_out).matmul(bank[rows_, 0:P], B["Wt"][:, own], St[:],
                                                   start=True, stop=True))
                yield
                m_v = V.mark(V.on(m).tensor_tensor(B["VN"][rows_, tile_], B["U"][rows_, tile_],
                                                   bank[rows_, 0:P], ALU.subtract))
                yield
                m = T.mark(T.on(m_v).matmul(bank[:, P:2 * P], B["Kd"][rows_, tile_],
                                            B["VN"][rows_, tile_], start=True, stop=True))
                T.e.matmul(bank[rows_, 2 * P:3 * P], B["QG"][:, own], St[:], start=True, stop=False)
                m = T.mark(T.e.matmul(bank[rows_, 2 * P:3 * P], B["AT"][rows_, own],
                                      B["VN"][rows_, tile_], start=False, stop=True))
                yield
                m_s = V.mark(V.on(m).scalar_tensor_tensor(
                    out=St[:], in0=St[:],
                    scalar=chunk_decay[:].rearrange("p h c -> p (h c)")[
                        :, bass.ds(i * (2 * NT) + c, 1)],
                    in1=bank[:, P:2 * P], op0=ALU.mult, op1=ALU.add))
                m_out = V.mark(V.e.tensor_scalar(B["Oa"][rows_, tile_], bank[rows_, 2 * P:3 * P],
                                                 rq_scan[rows_, t:t + 1], None, ALU.mult))
                yield
            st.scan_done = (m, m_out)
            st.scanning = False
            yield from out_norm(st, i, B["Oa"], B["VN"], 0, B_SCAN, m_out, EPS,
                                cols[:, C_GNORM:C_GNORM + 1], ())

        def diff(st, i):
            for t in range(NT):
                for c in range(2):
                    ins = T.on(*st.start).matmul(
                        PS[c * HD:(c + 1) * HD, B_S[0], t * P:(t + 1) * P],
                        rqk_b[:, 1, t, c:c + 1].to_broadcast([P, HD]), ident[:],
                        start=True, stop=True)
            m_k = T.mark(ins)
            m_r = {"Qb": T.mark(T.e.matmul(PS[:, B_S[1], :], mat(K_SWAP), B["Qb"][:],
                                           start=True, stop=True))}
            st.v_turned = turn_tiles(B_PT, B["Vd"][:], ())
            yield
            m_k = V.mark(V.on(m_k, *st.start).tensor_tensor(B["Kr"][:], B["Kr"][:],
                                                            PS[:, B_S[0], :], ALU.mult))
            m_v2 = A.mark(A.on(st.v_turned, *st.start).activation(B["Vdt"][:], PS[:, B_PT, :],
                                                                  ACT.Copy))
            yield
            m_r["Kr"] = T.mark(T.on(m_k).matmul(PS[:, B_S[0], :], mat(K_SWAP), B["Kr"][:],
                                                start=True, stop=True))
            ready, mts = [], []
            for j, name in ((0, "Qb"), (1, "Kr")):
                x = B[name][:]
                mt = V.mark(V.on(m_r[name], *st.start).tensor_tensor(
                    tmp[:, j, :], PS[:, B_S[1 - j], :], rope[:, 1, :], ALU.mult))
                mc = G.mark(G.on(m_r[name], *st.start).tensor_tensor(x, x, rope[:, 0, :], ALU.mult))
                yield
                ready.append(G.mark(G.on(mc, mt).tensor_tensor(x, x, tmp[:, j, :], ALU.add)))
                mts.append(mt)
                yield
            s_free = [mts[1], mts[0]]
            wd_free, pt_free, pts_free = None, m_v2, ready[1]
            before = None
            for n in range(NT + 1):
                qt = NT - 1 - n
                nk = (qt + 1) * P
                if n < NT:
                    m_s = []
                    for a in range(2):
                        r = slice(HD * a, HD * a + HD)
                        m_s.append(T.mark(T.on(*ready, s_free[a]).matmul(
                            PS[:, B_S[a], 0:nk], B["Qb"][r, qt * P:(qt + 1) * P], B["Kr"][r, 0:nk],
                            start=True, stop=True)))
                if before:
                    q_, m_wd = before
                    for kt in range(q_ + 1):
                        ins = T.on(m_wd, pt_free).transpose(
                            PS[:, B_PT, kt * P:(kt + 1) * P], B["Wd"][:, kt * P:(kt + 1) * P],
                            ident[:])
                    wd_free = T.mark(ins)
                yield
                if n < NT:
                    m_x = []
                    for a in range(2):
                        b = 2 * n + a
                        diag = PS[:, B_S[a], nk - P:nk]
                        m = V.mark(V.on(m_s[a]).tensor_tensor(diag, diag, causal[:], ALU.add))
                        m_x.append(V.mark(V.on(m).tensor_reduce(
                            nmax2[:, b:b + 1], PS[:, B_S[a], 0:nk], AXX, ALU.max, negate=True)))
                    b = 2 * n
                    m_x = V.mark(V.on(*m_x).tensor_tensor(nmax2[:, b:b + 2], nmax2[:, b:b + 2],
                                                          rqk_b[:, 0, qt, :], ALU.mult))
                if before:
                    m_pt = A.mark(A.on(wd_free, pts_free).activation(
                        tmp[:, 0, 0:(q_ + 1) * P], PS[:, B_PT, 0:(q_ + 1) * P], ACT.Copy))
                yield
                if n < NT:
                    m_p = []
                    for a in range(2):
                        b = 2 * n + a
                        m_p.append(A.mark(A.on(m_x, before and before[1]).activation(
                            P2[:, a, 0:nk], PS[:, B_S[a], 0:nk], ACT.Exp, bias=nmax2[:, b:b + 1],
                            scale=rqk_b[:, 0, qt, a:a + 1], accum_out=rsum2[:, b:b + 1])))
                    s_free = m_p
                if before:
                    for kt in range(q_ + 1):
                        ins = T.on(m_pt).matmul(
                            PS[:, B_PT, 0:P], tmp[:, 0, kt * P:(kt + 1) * P],
                            B["Vdt"][:, kt * P:(kt + 1) * P], start=(kt == 0), stop=(kt == q_))
                    pts_free = T.mark(ins)
                yield
                if n < NT:
                    b = 2 * n
                    m = V.mark(V.on(*m_p).reciprocal(rinv2[:, b:b + 2], rsum2[:, b:b + 2]))
                    m = V.mark(V.on(m).scalar_tensor_tensor(
                        out=neg_r[:, b:b + 1], in0=rinv2[:, b + 1:b + 2], scalar=neg_lam[:],
                        in1=rsum2[:, b:b + 1], op0=ALU.mult, op1=ALU.mult))
                    m_w = V.mark(V.on(m, wd_free).scalar_tensor_tensor(
                        out=B["Wd"][:, 0:nk], in0=P2[:, 1, 0:nk], scalar=neg_r[:, b:b + 1],
                        in1=P2[:, 0, 0:nk], op0=ALU.mult, op1=ALU.add))
                if before:
                    r_q = rinv2[:, 2 * (n - 1):2 * (n - 1) + 1]
                    pt_free = m_od = A.mark(A.on(pts_free).activation(
                        B["Od"][:, q_ * P:(q_ + 1) * P], PS[:, B_PT, 0:P], ACT.Copy, scale=r_q))
                before = (qt, m_w)
                yield
            st.diff_done, st.scores_read = m_s[1], s_free
            yield from out_norm(st, i, B["Od"], B["Wd"], 1, B_PT, m_od, SUB_EPS, subln[:, 0:1], ())

        class Rounds:

            def __init__(self):
                self.gens, self.owed = [], 0.0

            def __call__(self, steps):
                for g in list(self.gens):
                    try:
                        next(g)
                    except StopIteration:
                        self.gens.remove(g)
                self.owed += steps
                fill(int(self.owed))
                self.owed -= int(self.owed)

        def stages(i_a, i_b, h_mark):
            st = Head()
            st.convs, st.y_free, st.sq2, st.zs, st.sq_read = [], [None, None], [None, None], None, None
            st.h_ready = h_mark
            st.scanning, st.taps = i_b is not None, [iter(()), iter(())]
            rounds = st.rounds = Rounds()
            if i_a is not None:
                Fill.gens = [conv_unit(st, i_a, j) for j in range(3)] + [z_unit(st, 0)]
            if i_b is None:
                fill(2 * (KT + 1))
                chain = scalars()
                rounds.gens.insert(0, chain)
                while chain in rounds.gens:
                    rounds(PACE_SCALARS)
            else:
                chain = diff(st, i_b)
                rounds.gens = [scan(st, i_b), chain]
            if i_a is None:
                st.zs = A.mark(A.on(*st.start).activation(Zs[:], Zr[:], ACT.Silu))
                rounds.gens.append(split_outputs(st))
                Fill.gens = [projected(OUT_EARLY)]
                while rounds.gens:
                    rounds(PACE_END)
                fill_all()
                return
            rounds.gens = [norms(st), prep(st, i_a, i_b is not None)] + rounds.gens
            Fill.gens.append(z_unit(st, 1))
            while i_b is not None and chain in rounds.gens and st.diff_done is None:
                rounds(PACE_SCORES)
            Fill.gens += [qk_unit(st, "Kr", 1, C_KNORM), qk_unit(st, "Qb", 0, C_QNORM),
                          v_unit(st)]
            while Fill.gens:
                rounds(PACE_PREP if i_b is not None else PACE_FIRST)
            while rounds.gens:
                rounds(0)

        out_ready = {}
        stored = core.tally("stored", 16)

        def split_output(st, r):
            m = A.mark(A.on(*st.start).activation(Hh[:, r, :], O[:, r, :], ACT.Copy))
            out_ready[r] = V.mark(V.on(m, *st.start).tensor_tensor(
                Hl[:, r, :], O[:, r, :], Hh[:, r, :].bitcast(F32), ALU.subtract))

        def split_outputs(st):
            for r in range(2 * GH):
                if r % GH < GH - 1:
                    split_output(st, r)
                    yield

        def projected(blocks, final=False):
            for n, (k, r) in enumerate(blocks):
                unit_no, col = Dense.unit, n % KT
                b = Dense.group % 2
                if col == 0 and Dense.ahead < N_UNITS:
                    split_unit()
                begin, end = n == 0 or blocks[n - 1][0] != k, n + 1 == len(blocks) or blocks[n + 1][0] != k
                if begin:
                    T.on(bank_free[b].at(Dense.group // 2 + 1))
                while r not in out_ready:
                    yield
                T.on(split.at(unit_no + 1 + RING), out_ready[r])
                s, w = unit_no % RING, slice(col * P, (col + 1) * P)
                for m, (x, y) in enumerate(((Wh, Hh), (Wh, Hl), (Wl, Hh))):
                    ins = T.e.matmul(PS[:, b, :], x[:, s, w], y[:, r, :], start=begin and m == 0,
                                     stop=end and m == 2)
                if col == KT - 1:
                    done = used.inc(ins)
                    Dense.unit += 1
                elif end:
                    done = T.mark(ins)
                if end:
                    Dense.group += 1
                    m = bank_free[b].inc(V.on(done).tensor_tensor(X[:, k, :], X[:, k, :],
                                                                  PS[:, b, :], ALU.add))
                    if final:
                        stored.inc(A.on(m).dma_start(out[:, k, :], X[:, k, :]))
                yield

        stages(0, None, lambda r: (h_ready[r],))

        def next_head(i):
            stages(i + 1, i, None)
        dense_loop(GH - 1, BODY, BODY, (102, 43, 72, 17), next_head)
        stages(None, GH - 1, None)
        hb.close()

        last = Head()
        split_output(last, GH - 1)
        split_output(last, 2 * GH - 1)
        run(projected(OUT_LATE, final=True))
        A.on(stored.now())


def _units(np, w):
    k, n = w.shape
    return w.reshape(k // P, P, n // P, P).transpose(2, 1, 0, 3)


def _layout(np, inp):
    w1 = _units(np, inp["w_in"][0])
    order = []
    for h in range(PAIRS):
        order += [h, 4 + h, 8 + h, 12 + h, *range(16 + 4 * h, 20 + 4 * h)]
    p1 = w1[order]
    mix = np.concatenate([_units(np, inp["w_attn_out"][0]), _units(np, inp["w_pool_out"][0])], axis=2)
    wo = _units(np, inp["w_o"][0])
    up = _units(np, inp["w_up"][0])
    up = up.reshape(2, FT, P, KT, P).transpose(1, 0, 2, 3, 4).reshape(2 * FT, P, KT, P)
    down = _units(np, inp["w_down"][0])
    down = np.concatenate([down, np.zeros((KT, P, 24 - FT, P), np.float32)], axis=2)
    down = down.reshape(KT, P, 3, KT, P).transpose(0, 2, 1, 3, 4).reshape(24, P, KT, P)
    w2 = inp["w_in_2"][0]
    n = 4 * GH * P
    big = np.concatenate([w2[:, :n], w2[:, n + 2 * GH:]], axis=1)
    p2 = _units(np, big).reshape(8, GH, P, KT, P)[[0, 1, 2, 3, 7, 5, 4, 6]]
    p2 = p2.transpose(1, 0, 2, 3, 4).reshape(32, P, KT, P)
    wout = _units(np, inp["w_out_2"][0])
    wout = np.stack([wout[k, :, r] for k, r in OUT_EARLY + OUT_LATE]).reshape(KT, KT, P, P)
    wout = wout.transpose(0, 2, 1, 3)
    units = np.concatenate([p1, mix, wo, up, down, p2, wout], axis=0)
    units = np.ascontiguousarray(units).reshape(N_UNITS, P, D)
    w_ba = np.ascontiguousarray(w2[:, n:n + 2 * GH].reshape(KT, P, 2 * GH).transpose(1, 0, 2))

    def by_part(v):
        return v.reshape(-1, P).T

    conv = np.concatenate([inp["conv_w"][0], inp["conv_b"]], axis=0)
    conv = conv.reshape(4, 2, FT, P).transpose(3, 2, 1, 0).reshape(P, 4 * 2 * FT)
    conv2 = inp["conv_w_2"][0].reshape(4, 3, GH, P).transpose(3, 2, 1, 0).reshape(P, 48)
    cols = np.concatenate(
        [by_part(inp[k][0]) for k in ("norm_mix_pre", "norm_mix_post", "norm_ffn_pre",
                                      "norm_ffn_post", "w_norm_2", "b_gate", "pool_scale")]
        + [conv, conv2, by_part(inp["gdn_norm_w_2"][0])]
        + [np.concatenate([inp[k][0], inp[k][0]])[:, None] for k in ("q_norm_w_2", "k_norm_w_2")]
        + [by_part(inp["subln_w_2"][0])], axis=1)
    rows = np.concatenate([inp["a_log_2"][0], inp["dt_bias_2"][0], inp["lambda_q1_2"][0],
                           inp["lambda_k1_2"][0], inp["lambda_q2_2"][0], inp["lambda_k2_2"][0]])
    rows = np.broadcast_to(rows[None, :], (P, N_ROWS))
    rb = inp["rel_bias"][0]
    mid = (rb.shape[1] - 1) // 2
    dist = (S - P) + np.arange(P)[:, None] - np.arange(S)[None, :]
    rel = rb[:, np.clip(dist, -mid, mid) + mid].transpose(1, 0, 2)
    wgrp = inp["w_pool_group"][0].transpose(1, 0, 2)
    x = inp["x"][0].T.reshape(KT, P, S).transpose(1, 0, 2)

    t = np.arange(P)
    i, j = np.meshgrid(t, t, indexing="ij")
    same = (i // CH) == (j // CH)
    mats = [i == j, (i <= j) & same, same, (i // 64 == j // 64) & ((i % 64 + 32) % 64 == j % 64),
            np.where((i <= j) & same, 0.0, NEG), (i < j) & same]
    for lv in range(N_LEVELS):
        b = 1 << lv
        low = (i // (2 * b) == j // (2 * b)) & (i // b > j // b)
        mats += [low, low.T] if lv == 0 else [low.T]
    mats = np.stack([m.astype(np.float32) for m in mats], axis=1)
    inv = 10000.0 ** (-np.arange(0, HD, 2, dtype=np.float32) / np.float32(HD))
    ang = np.arange(S, dtype=np.float32)[:, None] * inv.astype(np.float32)[None, :]
    c, s = np.cos(ang).T, np.sin(ang).T
    causal = np.zeros((P, S), np.float32)
    causal[:, S - P:] = np.where(i >= j, 0.0, NEG)
    rope = np.stack([np.concatenate([c, c, c, c]), np.concatenate([-s, s, -s, s]), causal], axis=1)
    window = np.zeros((P, 4, 2 * P + LEAD))
    for g, w in enumerate(WINDOWS):
        count = np.minimum(t + 1, w)[None, :]
        near = (i <= j) & (j < i + w)
        window[:, g, :P] = near / w - (i == j)
        window[:, g, P:2 * P] = near / count - (i == j)
        window[:, g, 2 * P:] = ((j + P < i + w) / w)[:, :LEAD]
    return {"x": x, "w_units": units, "w_ba": w_ba, "cols": cols, "mats": mats, "rope": rope,
            "rows": rows, "rel": rel, "window": window, "wgrp": wgrp}


def kernel(**inputs):
    import numpy as _np
    import concourse.bacc as _bacc
    from concourse import mybir as _mybir
    from concourse.bass_utils import run_bass_kernel_spmd as _run

    nc = _bacc.Bacc("TRN2", target_bir_lowering=False, num_devices=1)
    arrays = _layout(_np, {k: _np.asarray(v) for k, v in inputs.items()})
    arrays = {"in_" + k: _np.ascontiguousarray(v, dtype=_np.float32) for k, v in arrays.items()}
    args = [nc.dram_tensor(k, v.shape, _mybir.dt.from_np(v.dtype), kind="ExternalInput").ap()
            for k, v in arrays.items()]
    out = nc.dram_tensor("out_0", (P, KT, S), _mybir.dt.float32, kind="ExternalOutput").ap()
    build(nc, *args, out)
    r = _run(nc, [arrays], core_ids=[0])
    got = r.results[0]["out_0"]
    return _np.ascontiguousarray(got.transpose(2, 1, 0)).reshape(1, S, D)
```
